# Optimizing a Trainium2 kernel written in Bass

```python
import math
import jax
import jax.numpy as jnp
from jax import lax
import numpy as np

D_MODEL = 1024
BATCH = 1
SEQ = 512
DEPTH = 1
DEC_BATCH = 8
DEC_SEQ = 4
PAST_LEN = 2048
PAGE_SIZE = 128

HEAD_DIM = 64
H_SB = 8
H_DIL = 8
D_SB = H_SB * HEAD_DIM
D_DIL = H_DIL * HEAD_DIM
DIL_CONFIGS = ((128, 1), (512, 4), (2048, 16))
DIL_SPAN = 128
WIN_MAX = 2048
Q_BLOCK = 128
ROPE_THETA = 10000.0
SB_BIAS_INIT = -6.0
PEER_HEADS = 8
PEER_NKEYS = 128
PEER_N = PEER_NKEYS * PEER_NKEYS
PEER_DKEY = 256
PEER_TOPK = 16
PEER_TOKEN_BLOCK = 256
DN_ALPHA = (2.0 * DEPTH) ** 0.25
DN_BETA = (8.0 * DEPTH) ** -0.25
LN_EPS = 1e-5

kernel_name = 'hybrid_stickbreak_dilated_peer_step'

def layer_norm(x, g, b):
    xf = x.astype(jnp.float32)
    mu = jnp.mean(xf, axis=-1, keepdims=True)
    var = jnp.mean(jnp.square(xf - mu), axis=-1, keepdims=True)
    y = (xf - mu) * lax.rsqrt(var + LN_EPS)
    return (y * g.astype(jnp.float32) + b.astype(jnp.float32)).astype(x.dtype)

def rope(x, pos):
    half = HEAD_DIM // 2
    inv = ROPE_THETA ** (-jnp.arange(half, dtype=jnp.float32) / half)
    ang = pos.astype(jnp.float32)[:, None] * inv[None, :]
    cos = jnp.cos(ang)[:, None, :]
    sin = jnp.sin(ang)[:, None, :]
    xf = x.astype(jnp.float32)
    x1, x2 = xf[..., :half], xf[..., half:]
    return jnp.concatenate([x1 * cos - x2 * sin, x2 * cos + x1 * sin], axis=-1).astype(x.dtype)

def split_projections(h, w_in):
    p = h @ w_in
    cuts = [D_SB, 2 * D_SB, 3 * D_SB, 3 * D_SB + D_DIL, 3 * D_SB + 2 * D_DIL]
    parts = jnp.split(p, cuts, axis=-1)
    lead = h.shape[:-1]
    heads = (H_SB, H_SB, H_SB, H_DIL, H_DIL, H_DIL)
    return [pp.reshape(lead + (nh, HEAD_DIM)) for pp, nh in zip(parts, heads)]

def stick_breaking_weights(z, mask):
    log_keep = jnp.where(mask, jax.nn.log_sigmoid(-z), 0.0)
    later = lax.cumsum(log_keep, axis=z.ndim - 1, reverse=True) - log_keep
    return jnp.where(mask, jnp.exp(jax.nn.log_sigmoid(z) + later), 0.0)

def sb_prompt(q, k, v, bias):
    B, S, H, Dh = q.shape
    nb = S // Q_BLOCK
    qb = q.reshape(B, nb, Q_BLOCK, H, Dh).transpose(1, 0, 2, 3, 4)
    kpos = jnp.arange(S)
    scale = HEAD_DIM ** -0.5
    b = bias.astype(jnp.float32)[:, None, None]

    def block(args):
        qi, bi = args
        z = jnp.einsum('bqhd,bkhd->bhqk', qi, k, preferred_element_type=jnp.float32) * scale + b
        qpos = bi * Q_BLOCK + jnp.arange(Q_BLOCK)
        mask = kpos[None, :] < qpos[:, None]
        w = stick_breaking_weights(z, mask)
        return jnp.einsum('bhqk,bkhd->bqhd', w.astype(v.dtype), v)

    o = lax.map(block, (qb, jnp.arange(nb)))
    return o.transpose(1, 0, 2, 3, 4).reshape(B, S, H, Dh)

def sb_sample(q, k_new, v_new, k_past, v_past, bias):
    P = k_past.shape[1]
    T = q.shape[1]
    scale = HEAD_DIM ** -0.5
    z_past = jnp.einsum('bthd,bkhd->bhtk', q, k_past, preferred_element_type=jnp.float32)
    z_new = jnp.einsum('bthd,bkhd->bhtk', q, k_new, preferred_element_type=jnp.float32)
    z = jnp.concatenate([z_past, z_new], axis=-1) * scale + bias.astype(jnp.float32)[:, None, None]
    mask = jnp.concatenate([jnp.ones((T, P), bool),
                            jnp.arange(T)[None, :] < jnp.arange(T)[:, None]], axis=-1)
    w = stick_breaking_weights(z, mask).astype(v_new.dtype)
    return (jnp.einsum('bhtk,bkhd->bthd', w[..., :P], v_past)
            + jnp.einsum('bhtk,bkhd->bthd', w[..., P:], v_new))

def dilated_band(q, k, v, dil):
    B, S, H, Dh = q.shape
    L = S // dil
    N = B * dil

    def to_sub(x):
        return x.reshape(B, L, dil, H, Dh).transpose(0, 2, 1, 3, 4).reshape(N, L, H, Dh)

    qs, ks, vs = to_sub(q), to_sub(k), to_sub(v)
    nb = -(-L // Q_BLOCK)
    Lp = nb * Q_BLOCK
    pad_tail = Lp - L
    qs = jnp.pad(qs, ((0, 0), (0, pad_tail), (0, 0), (0, 0)))
    ks = jnp.pad(ks, ((0, 0), (Q_BLOCK, pad_tail), (0, 0), (0, 0)))
    vs = jnp.pad(vs, ((0, 0), (Q_BLOCK, pad_tail), (0, 0), (0, 0)))
    qb = qs.reshape(N, nb, Q_BLOCK, H, Dh)
    kb = ks.reshape(N, nb + 1, Q_BLOCK, H, Dh)
    vb = vs.reshape(N, nb + 1, Q_BLOCK, H, Dh)
    kband = jnp.concatenate([kb[:, :-1], kb[:, 1:]], axis=2)
    vband = jnp.concatenate([vb[:, :-1], vb[:, 1:]], axis=2)
    z = jnp.einsum('nbqhd,nbkhd->nbhqk', qb, kband,
                   preferred_element_type=jnp.float32) * (HEAD_DIM ** -0.5)
    qi = jnp.arange(Q_BLOCK)[:, None]
    kj = jnp.arange(2 * Q_BLOCK)[None, :]
    dist = Q_BLOCK + qi - kj
    blk = jnp.arange(nb)[:, None, None]
    valid = (dist >= 0) & (dist <= DIL_SPAN) & ((blk > 0) | (kj >= Q_BLOCK))
    z = jnp.where(valid[None, :, None], z, -jnp.inf)
    lse = jax.nn.logsumexp(z, axis=-1)
    p = jnp.exp(z - lse[..., None]).astype(v.dtype)
    o = jnp.einsum('nbhqk,nbkhd->nbqhd', p, vband).reshape(N, Lp, H, Dh)[:, :L]
    lse = lse.transpose(0, 1, 3, 2).reshape(N, Lp, H)[:, :L]
    o = o.reshape(B, dil, L, H, Dh).transpose(0, 2, 1, 3, 4).reshape(B, S, H, Dh)
    lse = lse.reshape(B, dil, L, H).transpose(0, 2, 1, 3).reshape(B, S, H)
    return o, lse

def dilated_sample(q, kc, vc, n_buf):
    DB, T, H, Dh = q.shape
    steps = jnp.arange(DIL_SPAN + 1)
    outs, lses = [], []
    for _, dil in DIL_CONFIGS:
        idx = n_buf + jnp.arange(T)[:, None] - dil * steps[None, :]
        valid = idx >= 0
        flat = jnp.clip(idx, 0).reshape(-1)
        kg = jnp.take(kc, flat, axis=1).reshape(DB, T, DIL_SPAN + 1, H, Dh)
        vg = jnp.take(vc, flat, axis=1).reshape(DB, T, DIL_SPAN + 1, H, Dh)
        z = jnp.einsum('bthd,btjhd->bhtj', q, kg,
                       preferred_element_type=jnp.float32) * (HEAD_DIM ** -0.5)
        z = jnp.where(valid[None, None], z, -jnp.inf)
        lse = jax.nn.logsumexp(z, axis=-1)
        p = jnp.exp(z - lse[..., None]).astype(vc.dtype)
        outs.append(jnp.einsum('bhtj,btjhd->bthd', p, vg))
        lses.append(lse.transpose(0, 2, 1))
    return outs, lses

def merge_by_denominator(outs, lses):
    w = jax.nn.softmax(jnp.stack(lses, axis=0), axis=0)
    o = jnp.einsum('cbsh,cbshd->bshd', w, jnp.stack(outs, axis=0).astype(jnp.float32))
    return o.astype(outs[0].dtype)

def peer_ffn(x, wq, subkeys, u_tab, v_tab):
    n = x.shape[0]
    nb = -(-n // PEER_TOKEN_BLOCK)
    xb = jnp.pad(x, ((0, nb * PEER_TOKEN_BLOCK - n), (0, 0))).reshape(nb, PEER_TOKEN_BLOCK, D_MODEL)
    K = PEER_TOPK

    def block(xi):
        q = (xi @ wq).reshape(PEER_TOKEN_BLOCK, PEER_HEADS, 2, PEER_DKEY // 2)
        s = jnp.einsum('nhcd,ckd->nhck', q, subkeys, preferred_element_type=jnp.float32)
        sv, si = lax.top_k(s, K)
        cand = (sv[:, :, 0, :, None] + sv[:, :, 1, None, :]).reshape(PEER_TOKEN_BLOCK, PEER_HEADS, K * K)
        cid = (si[:, :, 0, :, None] * PEER_NKEYS + si[:, :, 1, None, :]).reshape(PEER_TOKEN_BLOCK, PEER_HEADS, K * K)
        top_s, pos = lax.top_k(cand, K)
        eid = jnp.take_along_axis(cid, pos, axis=-1)
        g = jax.nn.softmax(top_s, axis=-1)
        hpre = jnp.einsum('nd,nhkd->nhk', xi, u_tab[eid], preferred_element_type=jnp.float32)
        a = (jax.nn.gelu(hpre, approximate=False) * g).astype(xi.dtype)
        return jnp.einsum('nhk,nhkd->nd', a, v_tab[eid])

    return lax.map(block, xb).reshape(nb * PEER_TOKEN_BLOCK, D_MODEL)[:n]

def finish_layer(x, o_sb, o_dil, w_out, ln1_g, ln1_b, peer_wq, peer_subkeys, peer_u, peer_v, ln2_g, ln2_b):
    lead = x.shape[:-1]
    mixed = jnp.concatenate([o_sb.reshape(lead + (D_SB,)), o_dil.reshape(lead + (D_DIL,))], axis=-1) @ w_out
    h1 = layer_norm(DN_ALPHA * x + mixed, ln1_g, ln1_b)
    f = peer_ffn(h1.reshape(-1, D_MODEL), peer_wq, peer_subkeys, peer_u, peer_v).reshape(h1.shape)
    return layer_norm(DN_ALPHA * h1 + f, ln2_g, ln2_b)

def setup_inputs(seed: int = 0) -> dict:
    key = jax.random.key(seed)
    ks = jax.random.split(key, 20)
    n_pages = PAST_LEN // PAGE_SIZE
    n_used = DEC_BATCH * n_pages
    n_pool = n_used + n_used // 4
    page_table = jax.random.permutation(ks[0], n_pool)[:n_used].reshape(DEC_BATCH, n_pages).astype(jnp.int32)
    n_buf = min(WIN_MAX, PAST_LEN)
    d_in = 3 * D_SB + 3 * D_DIL
    col_scale = jnp.concatenate([jnp.ones((2 * D_SB,)), jnp.full((D_SB,), DN_BETA),
                                 jnp.ones((2 * D_DIL,)), jnp.full((D_DIL,), DN_BETA)])
    w_in = jax.random.normal(ks[1], (D_MODEL, d_in), jnp.float32) * (D_MODEL ** -0.5) * col_scale[None, :]
    w_out = jax.random.normal(ks[2], (D_SB + D_DIL, D_MODEL), jnp.float32) * ((D_SB + D_DIL) ** -0.5) * DN_BETA
    return {
        'x_prompt': jax.random.normal(ks[3], (BATCH, SEQ, D_MODEL), jnp.float32),
        'x_sample': jax.random.normal(ks[4], (DEC_BATCH, DEC_SEQ, D_MODEL), jnp.float32),
        'cache_k_sb': jax.random.normal(ks[5], (n_pool, PAGE_SIZE, H_SB, HEAD_DIM), jnp.float32),
        'cache_v_sb': jax.random.normal(ks[6], (n_pool, PAGE_SIZE, H_SB, HEAD_DIM), jnp.float32) * DN_BETA,
        'page_table': page_table,
        'state_k_win': jax.random.normal(ks[7], (DEC_BATCH, n_buf, H_DIL, HEAD_DIM), jnp.float32),
        'state_v_win': jax.random.normal(ks[8], (DEC_BATCH, n_buf, H_DIL, HEAD_DIM), jnp.float32) * DN_BETA,
        'w_in': w_in,
        'w_out': w_out,
        'sb_logit_bias': SB_BIAS_INIT + 0.1 * jax.random.normal(ks[17], (H_SB,), jnp.float32),
        'ln1_g': 1.0 + 0.02 * jax.random.normal(ks[9], (D_MODEL,), jnp.float32),
        'ln1_b': 0.02 * jax.random.normal(ks[10], (D_MODEL,), jnp.float32),
        'peer_wq': jax.random.normal(ks[11], (D_MODEL, PEER_HEADS * PEER_DKEY), jnp.float32) * (D_MODEL ** -0.5),
        'peer_subkeys': jax.random.normal(ks[12], (2, PEER_NKEYS, PEER_DKEY // 2), jnp.float32) * ((PEER_DKEY // 2) ** -0.5),
        'peer_u': jax.random.normal(ks[13], (PEER_N, D_MODEL), jnp.float32) * (D_MODEL ** -0.5),
        'peer_v': jax.random.normal(ks[14], (PEER_N, D_MODEL), jnp.float32) * DN_BETA,
        'ln2_g': 1.0 + 0.02 * jax.random.normal(ks[15], (D_MODEL,), jnp.float32),
        'ln2_b': 0.02 * jax.random.normal(ks[16], (D_MODEL,), jnp.float32),
    }

def reference(x_prompt, x_sample, cache_k_sb, cache_v_sb, page_table, state_k_win, state_v_win,
              w_in, w_out, sb_logit_bias, ln1_g, ln1_b, peer_wq, peer_subkeys, peer_u, peer_v, ln2_g, ln2_b):
    B, S, _ = x_prompt.shape
    DB, T, _ = x_sample.shape
    n_pages = page_table.shape[1]
    past_len = n_pages * PAGE_SIZE
    n_buf = state_k_win.shape[1]

    qa, ka, va, qd, kd, vd = split_projections(x_prompt, w_in)
    pos_p = jnp.arange(S)
    qd = rope(qd, pos_p)
    kd = rope(kd, pos_p)
    o_sb_p = sb_prompt(qa, ka, va, sb_logit_bias)
    outs_p, lses_p = [], []
    for _, dil in DIL_CONFIGS:
        o, l = dilated_band(qd, kd, vd, dil)
        outs_p.append(o)
        lses_p.append(l)
    o_dil_p = merge_by_denominator(outs_p, lses_p)
    y_prompt = finish_layer(x_prompt, o_sb_p, o_dil_p, w_out, ln1_g, ln1_b,
                            peer_wq, peer_subkeys, peer_u, peer_v, ln2_g, ln2_b)
    keep_p = min(WIN_MAX, S)

    qa_s, ka_s, va_s, qd_s, kd_s, vd_s = split_projections(x_sample, w_in)
    pos_s = past_len + jnp.arange(T)
    qd_s = rope(qd_s, pos_s)
    kd_s = rope(kd_s, pos_s)
    k_past = jnp.take(cache_k_sb, page_table, axis=0).reshape(DB, past_len, H_SB, HEAD_DIM)
    v_past = jnp.take(cache_v_sb, page_table, axis=0).reshape(DB, past_len, H_SB, HEAD_DIM)
    o_sb_s = sb_sample(qa_s, ka_s, va_s, k_past, v_past, sb_logit_bias)
    kc = jnp.concatenate([state_k_win, kd_s], axis=1)
    vc = jnp.concatenate([state_v_win, vd_s], axis=1)
    outs_s, lses_s = dilated_sample(qd_s, kc, vc, n_buf)
    o_dil_s = merge_by_denominator(outs_s, lses_s)
    y_sample = finish_layer(x_sample, o_sb_s, o_dil_s, w_out, ln1_g, ln1_b,
                            peer_wq, peer_subkeys, peer_u, peer_v, ln2_g, ln2_b)
    keep_s = min(WIN_MAX, n_buf + T)

    return (y_prompt, y_sample,
            ka.reshape(B, S // PAGE_SIZE, PAGE_SIZE, H_SB, HEAD_DIM),
            va.reshape(B, S // PAGE_SIZE, PAGE_SIZE, H_SB, HEAD_DIM),
            ka_s, va_s,
            kd[:, S - keep_p:], vd[:, S - keep_p:],
            kc[:, n_buf + T - keep_s:], vc[:, n_buf + T - keep_s:])


_drawn_inputs = setup_inputs


def setup_inputs(seed=0):
    import zlib

    import numpy as np

    out = dict(_drawn_inputs(seed))
    spreads = {}
    factors = {'sb_logit_bias': 8.0, 'ln2_g': 2.86, 'ln2_b': 2.857}
    for name, (base, spread) in spreads.items():
        noise = np.random.default_rng([zlib.crc32(name.encode()), seed]).standard_normal(out[name].shape)
        drawn = base * np.exp(spread * noise) if base else spread * noise
        out[name] = jnp.asarray(drawn.astype(out[name].dtype))
    for name, factor in factors.items():
        out[name] = (out[name] * factor).astype(out[name].dtype)
    return out
```

```python
from contextlib import ExitStack

import numpy as np

import concourse.bass as bass
from concourse import mybir

F32 = mybir.dt.float32
I32 = mybir.dt.int32
U32 = mybir.dt.uint32
ALU = mybir.AluOpType
ACT = mybir.ActivationFunctionType
AX_X = mybir.AxisListType.X

P = 128
D = 1024
KD = D // P
SEQ = 512
DB, DT = 8, 4
NS = DB * DT
N = SEQ + NS
NT = 5
NP = NT * P
H, HD = 8, 64
DH = H * HD
NPAIR = H // 2
PAGES = 16
N_POOL = 160
PAST = PAGES * P
WIN = 2048
SPAN = 128
DILS = (1, 4, 16)
TK = 16
NK = 128
PH = 8
HALF = N // 2
SCALE = HD ** -0.5
ALPHA = 2.0 ** 0.25
EPS = 1e-5
NEG = -1e30
LOWEST = -3.0e38
BANK = 512
CHUNK = 32
NCHUNK = N // CHUNK
GI = 4
NG = NK // GI
NEAR = 4
FAR = 3
NW = NEAR + FAR
K_SLOTS = 8


def constants():
    r = np.arange(P)
    ident = np.eye(P, dtype=np.float32)
    tri = (r[:, None] >= r[None, :]).astype(np.float32)
    ones = np.ones((P, P), np.float32)
    diag = np.where(r[None, :] > r[:, None], 0.0, NEG)
    iota = np.broadcast_to(r, (P, P))
    square = np.concatenate([ident, tri, ones, diag, iota], axis=1).astype(np.float32)

    def log_count(dist):
        count = ((dist >= 0) & (dist <= SPAN)).astype(np.int64)
        for dil in DILS[1:]:
            count = count + ((dist >= 0) & (dist % dil == 0) & (dist <= SPAN * dil))
        return np.where(count > 0, np.log(np.maximum(count, 1)) / SCALE, NEG)

    q = np.arange(SEQ)
    prompt = log_count(q[:, None] - q[None, :]).reshape(NT - 1, P, SEQ).transpose(1, 0, 2)
    near = WIN - NEAR * P + np.arange(NEAR * P)
    g = np.arange(FAR * P)
    far = 16 * (g // 4) + g % 4
    t = np.arange(DT)
    rows = WIN + np.tile(t, H)
    window = log_count(rows[:, None] - np.concatenate([near, far])[None, :])
    s = np.arange(NS)
    fresh = log_count(rows[:, None, None] - (WIN + s % DT)[None, None, :])
    own = (s // DT)[None, None, :] == np.arange(DB)[None, :, None]
    fresh = np.where(own, np.broadcast_to(fresh, (NS, DB, NS)), NEG)
    new = np.where((s[:, None] // DT == np.arange(DB)[None, :])[:, :, None]
                   & ((s % DT)[:, None, None] < np.tile(t, H)[None, None, :]), 0.0, NEG)
    pos = np.zeros((NT, P), np.float32)
    pos[:4] = np.arange(SEQ).reshape(4, P)
    pos[4, :NS] = PAST + s % DT
    inv = np.float32(10000.0) ** (-np.arange(HD // 2, dtype=np.float32) / np.float32(HD // 2))
    ang = (pos[:, :, None] * inv[None, None, :]).astype(np.float32).transpose(1, 0, 2)
    f = lambda a: np.ascontiguousarray(a.astype(np.float32))
    return {
        "square": f(square),
        "count_prompt": f(prompt.reshape(P, -1)),
        "count_window": f(window),
        "count_fresh": f(fresh.reshape(NS, -1)),
        "mask_new": f(new.reshape(NS, -1)),
        "cosine": f(np.cos(ang).reshape(P, -1)),
        "sine": f(np.sin(ang).reshape(P, -1)),
    }


class Steps:

    def __init__(self, eng, sem):
        self.eng, self.sem, self.base, self.n = eng, sem, 0, 0

    def do(self, ins):
        ins.then_inc(self.sem, 1)
        self.n += 1

    def wait(self, back=0):
        self.eng.wait_ge(self.sem, self.base + (self.n - back))

    def link(self, ins):
        self.do(ins)
        self.wait()

    def enter(self, i, per_turn):
        self.start, self.per_turn = self.n, per_turn
        self.base = i * per_turn

    def leave(self, turns):
        assert self.n - self.start == self.per_turn, (self.n - self.start, self.per_turn)
        self.base, self.n = 0, self.start + turns * self.per_turn


def build(nc, x_prompt, x_sample, cache_k_sb, cache_v_sb, page_table, state_k_win, state_v_win,
          w_in, w_out, sb_logit_bias, ln1_g, ln1_b, peer_wq, peer_subkeys, peer_u, peer_v, ln2_g, ln2_b,
          square, count_prompt, count_window, count_fresh, mask_new, cosine, sine,
          y_prompt, y_sample, k_sb_prompt, v_sb_prompt, k_sb_sample, v_sb_sample,
          k_win_prompt, v_win_prompt, k_win_sample, v_win_sample):
    with ExitStack() as ctx:
        arena = ctx.enter_context(nc.sbuf_tensor("arena", [P, 50176], F32))
        pages_sb = ctx.enter_context(nc.sbuf_tensor("pages_sb", [1, DB * PAGES], I32))
        psum = ctx.enter_context(nc.psum_tensor("psum", [P, 8 * BANK], F32))
        gates_dram = nc.dram_tensor("gates_dram", [NCHUNK, P, NK * CHUNK], F32).ap()

        made = {}

        def sem(name):
            if name not in made:
                made[name] = ctx.enter_context(nc.semaphore(name))
            return made[name]

        place = [0]

        def take(cols, at=None):
            if at is not None:
                place[0] = at
            o = place[0]
            place[0] = o + cols
            assert place[0] <= 50176, place[0]
            return arena[:, o:o + cols]

        def bank(b, n=1):
            return psum[:, b * BANK:(b + n) * BANK]

        x_nat = take(NT * D).rearrange("p (t d) -> p t d", t=NT)
        sq = take(5 * P)
        ident, tri, ones, diag, iota = (sq[:, i * P:(i + 1) * P] for i in range(5))
        small = take(384)
        o_t = take(KD * NP).rearrange("p (c n) -> p c n", c=KD)
        ERA = place[0]
        v_n = {k: take(NT * DH).rearrange("p (t d) -> p t d", t=NT) for k in ("sb", "dil")}
        q_s = {k: take(H * NS).rearrange("p (h s) -> p h s", h=H) for k in ("sb", "dil")}
        k_s = {k: take(NPAIR * NS).rearrange("p (c s) -> p c s", c=NPAIR) for k in ("sb", "dil")}
        q_wide = take(NPAIR * DB * NS).rearrange("p (c b n) -> p c b n", c=NPAIR, b=DB)
        SAMPLE = place[0]
        q_z = {k: take(H * N).rearrange("p (h n) -> p h n", h=H) for k in ("sb", "dil")}
        k_t = {k: take(NPAIR * N).rearrange("p (c n) -> p c n", c=NPAIR) for k in ("sb", "dil")}
        WORK = place[0]

        over = sem("stage_over")
        stage = {}

        def end_stage(eng):
            name = eng.engine
            stage[name] = stage.get(name, 0) + 1
            eng.drain().then_inc(over, 1)
            eng.wait_ge(over, 5 * stage[name])

        programs = {"sp": [], "pe": [], "act": [], "dve": [], "pool": []}

        def part(engine):
            return programs[engine].append
        steps = {}

        def own_steps(eng, name):
            if name not in steps:
                steps[name] = Steps(eng, sem(f"{name}_step"))
            return steps[name]

        x_t = take(KD * N, WORK).rearrange("p (k n) -> p k n", k=KD)
        w_g = [take(KD * DH).rearrange("p (k c) -> p k c", k=KD) for _ in range(2)]
        staged = [take(NT * DH).rearrange("p (t c) -> p t c", t=NT) for _ in range(2)]
        rope_a = take(NT * H * 32, ERA - KD * NP)
        rope_b = take(NT * H * 32)
        cos_sb, sin_sb = take(NT * 32), take(NT * 32)
        GROUPS = ("q_sb", "k_sb", "q_dil", "k_dil", "v_sb", "v_dil")
        COLUMN = {"q_sb": 0, "k_sb": 1, "v_sb": 2, "q_dil": 3, "k_dil": 4, "v_dil": 5}
        x_rows = x_prompt.rearrange("b (t p) d -> p (b t) d", p=P)
        xs_rows = x_sample.rearrange("b t d -> (b t) d")
        w_in_g = w_in.rearrange("(k p) (g c) -> g p k c", p=P, c=DH)

        def rows_of(t):
            return P if t < NT - 1 else NS

        def proj_out(c, t):
            kind = GROUPS[c].split("_")[1]
            to = v_n[kind] if GROUPS[c][0] == "v" else staged[c % 2]
            return to[0:rows_of(t), t, :]

        @part("sp")
        def _(sp):
            sp.dma_start(x_nat[:, 0:4, :], x_rows).then_inc(sem("x_prompt_in"), 16)
            sp.wait_ge(sem("tail_cleared"), 1)
            sp.dma_start(x_nat[0:NS, 4, :], xs_rows).then_inc(sem("x_sample_in"), 16)
            sp.dma_start(sq, square).then_inc(sem("square_in"), 16)
            sp.dma_start(cos_sb, cosine).then_inc(sem("angles_in"), 16)
            sp.dma_start(sin_sb, sine).then_inc(sem("angles_in"), 16)
            sp.dma_start(pages_sb[:, :], page_table.rearrange("b j -> (b j)").rearrange("(o n) -> o n", o=1))\
              .then_inc(sem("pages_in"), 16)
            for c in range(len(GROUPS)):
                if c >= 2:
                    sp.wait_ge(sem("proj_ready"), 5 * (c - 1))
                sp.dma_start(w_g[c % 2], w_in_g[COLUMN[GROUPS[c]]]).then_inc(sem(f"w_in_{c % 2}"), 16)
            for to, frm in ((k_win_sample, state_k_win), (v_win_sample, state_v_win)):
                sp.dma_start(to.rearrange("b w h d -> b (w h d)")[:, 0:(WIN - DT) * DH],
                             frm.rearrange("b w h d -> b (w h d)")[:, DT * DH:WIN * DH])\
                  .then_inc(sem("window_moved"), 16)

        @part("pool")
        def _(pool):
            def rows_out(tile, prompt, sample, name, ready, value):
                pool.wait_ge(sem(ready), value)
                pool.dma_start(prompt, tile[:, 0:4, :]).then_inc(sem(f"{name}_out"), 16)
                if name in ("k_sb", "v_sb"):
                    pool.dma_start(sample, tile[0:NS, 4, :]).then_inc(sem(f"{name}_out"), 16)
                else:
                    for b in range(DB):
                        pool.dma_start(sample[b], tile[b * DT:(b + 1) * DT, 4, :])\
                            .then_inc(sem(f"{name}_out"), 16)

            flat = "b (t p) h d -> p (b t) (h d)"
            pages = "b t p h d -> p (b t) (h d)"
            rows_out(staged[1], k_sb_prompt.rearrange(pages), k_sb_sample.rearrange("b t h d -> (b t) (h d)"),
                     "k_sb", "proj_copied", 5 * 2)
            rows_out(staged[1], k_win_prompt.rearrange(flat, p=P),
                     k_win_sample.rearrange("b w h d -> b w (h d)")[:, WIN - DT:WIN, :], "k_dil", "roped", 2)
            rows_out(v_n["sb"], v_sb_prompt.rearrange(pages), v_sb_sample.rearrange("b t h d -> (b t) (h d)"),
                     "v_sb", "proj_copied", 5 * 5)
            rows_out(v_n["dil"], v_win_prompt.rearrange(flat, p=P),
                     v_win_sample.rearrange("b w h d -> b w (h d)")[:, WIN - DT:WIN, :], "v_dil", "proj_copied", 5 * 6)
            for name in ("k_sb", "k_dil", "v_sb", "v_dil"):
                pool.wait_ge(sem(f"{name}_out"), 16 * (2 if name[2:] == "sb" else 1 + DB))

        @part("pe")
        def _(pe):
            pe.wait_ge(sem("square_in"), 16)
            for t in range(NT):
                pe.wait_ge(sem("x_prompt_in" if t < 4 else "x_sample_in"), 16)
                r = rows_of(t)
                for half in range(2):
                    u = 2 * t + half
                    if u >= 4:
                        pe.wait_ge(sem("x_t_copied"), u - 3)
                    for k in range(4):
                        last = pe.transpose(bank(u % 4)[:, k * P:k * P + r],
                                            x_nat[0:r, t, (4 * half + k) * P:(4 * half + k + 1) * P],
                                            ident[0:r, 0:r])
                    last.then_inc(sem("x_t_ready"), 1)
            pe.wait_ge(sem("x_t_copied"), 10)

            def turn(c):
                if c < 2:
                    pe.wait_ge(sem("proj_copied"), 5 * c + 5)
                else:
                    pe.wait_ge(sem("roped"), c - 1)
                for t in range(NT):
                    v = 5 * c + t
                    if v >= 4:
                        pe.wait_ge(sem("qk_copied_dve"), v - 3)
                        if (v - 4) // 5 % 2 == 0:
                            pe.wait_ge(sem("q_copied_act"), 5 * ((v - 4) // 10) + (v - 4) % 5 + 1)
                    r = rows_of(t)
                    for pair in range(NPAIR):
                        last = pe.transpose(bank(4 + v % 4)[:, pair * P:pair * P + r],
                                            staged[c % 2][0:r, t, pair * P:(pair + 1) * P], ident[0:r, 0:r])
                    last.then_inc(sem("qk_ready"), 1)

            for c in range(len(GROUPS)):
                pe.wait_ge(sem(f"w_in_{c % 2}"), 16 * (c // 2 + 1))
                for t in range(NT):
                    u = 5 * c + t
                    if u >= 4:
                        pe.wait_ge(sem("proj_copied"), u - 3)
                    r = rows_of(t)
                    for k in range(KD):
                        last = pe.matmul(bank(u % 4)[0:r, :], lhsT=x_t[:, k, t * P:t * P + r], rhs=w_g[c % 2][:, k, :],
                                         start=(k == 0), stop=(k == KD - 1))
                    last.then_inc(sem("proj_ready"), 1)
                if 1 <= c <= 4:
                    turn(c - 1)

        @part("act")
        def _(act):
            for t in range(NT):
                r = rows_of(t)
                for half in range(2):
                    u = 2 * t + half
                    act.wait_ge(sem("x_t_ready"), u + 1)
                    act.activation(x_t[:, 4 * half:4 * half + 4, t * P:t * P + r],
                                   bank(u % 4).rearrange("p (k n) -> p k n", k=4)[:, :, 0:r], ACT.Copy)\
                        .then_inc(sem("x_t_copied"), 1)
            act.wait_ge(sem("staged_cleared"), 4)

            def q_copy(c):
                kind = GROUPS[c].split("_")[1]
                for t in range(NT):
                    v = 5 * c + t
                    act.wait_ge(sem("qk_ready"), v + 1)
                    r = rows_of(t)
                    src = bank(4 + v % 4).rearrange("p (c n) -> p c n", c=NPAIR)[0:64, :, 0:r]
                    act.activation(q_z[kind].rearrange("p (c e) n -> p c e n", e=2)[0:64, :, 0, t * P:t * P + r],
                                   src, ACT.Copy).then_inc(sem("q_copied_act"), 1)

            for c in range(len(GROUPS)):
                for t in range(NT):
                    act.wait_ge(sem("proj_ready"), 5 * c + t + 1)
                    if c in (2, 3) and t == 0:
                        act.wait_ge(sem("qk_ready"), 5 * (c - 1))
                        if c == 3:
                            act.wait_ge(sem("k_sb_out"), 2 * 16)
                    act.activation(proj_out(c, t), bank((5 * c + t) % 4)[0:rows_of(t), :], ACT.Copy)\
                        .then_inc(sem("proj_copied"), 1)
                if c in (1, 3):
                    q_copy(c - 1)

        @part("dve")
        def _(dve):
            dve.memset(x_nat[:, 4, :], 0.0).then_inc(sem("tail_cleared"), 1)
            for i in range(2):
                dve.memset(staged[i][:, 4, :], 0.0).then_inc(sem("staged_cleared"), 1)
            for kind in ("sb", "dil"):
                dve.memset(v_n[kind][:, 4, :], 0.0).then_inc(sem("staged_cleared"), 1)
            for kind in ("sb", "dil"):
                halves = q_z[kind].rearrange("p (c e) n -> p c e n", e=2)
                dve.memset(halves[64:128, :, 0, :], 0.0).then_inc(sem("q_cleared"), 1)
                dve.memset(halves[0:64, :, 1, :], 0.0).then_inc(sem("q_cleared"), 1)

            def qk_copy(c):
                kind = GROUPS[c].split("_")[1]
                for t in range(NT):
                    v = 5 * c + t
                    dve.wait_ge(sem("qk_ready"), v + 1)
                    r = rows_of(t)
                    src = bank(4 + v % 4).rearrange("p (c n) -> p c n", c=NPAIR)[:, :, 0:r]
                    if GROUPS[c][0] == "k":
                        dve.tensor_copy(k_t[kind][:, :, t * P:t * P + r], src).then_inc(sem("qk_copied_dve"), 1)
                    else:
                        to = q_z[kind].rearrange("p (c e) n -> p c e n", e=2)
                        dve.tensor_copy(to[64:128, :, 1, t * P:t * P + r], src[64:128]).then_inc(sem("qk_copied_dve"), 1)

            st = own_steps(dve, "dve")

            def rope(c):
                dve.wait_ge(sem("proj_copied"), 5 * c + 5)
                x = staged[c % 2].rearrange("p t (h e d) -> p t h e d", e=2, d=32)
                x1, x2 = x[:, :, :, 0, :], x[:, :, :, 1, :]
                ta, tb = (a.rearrange("p (t h d) -> p t h d", t=NT, h=H) for a in (rope_a, rope_b))
                cos, sin = (a.rearrange("p (t o d) -> p t o d", t=NT, o=1).to_broadcast([P, NT, H, 32])
                            for a in (cos_sb, sin_sb))
                st.do(dve.tensor_tensor(ta, x1, cos, ALU.mult))
                st.link(dve.tensor_tensor(tb, x2, sin, ALU.mult))
                st.do(dve.tensor_tensor(rope_a, rope_a, rope_b, ALU.subtract))
                st.link(dve.tensor_tensor(x1, x1, sin, ALU.mult))
                st.link(dve.tensor_tensor(tb, x2, cos, ALU.mult))
                st.link(dve.tensor_tensor(x2, x1, tb, ALU.add))
                dve.tensor_copy(x1, ta).then_inc(sem("roped"), 1)

            dve.wait_ge(sem("angles_in"), 2 * 16)
            qk_copy(0)
            qk_copy(1)
            rope(2)
            qk_copy(2)
            rope(3)
            qk_copy(3)
            dve.wait_ge(sem("q_copied_act"), 10)
            dve.wait_ge(sem("qk_copied_dve"), 20)
            for kind in ("sb", "dil"):
                dve.tensor_copy(q_s[kind], q_z[kind][:, :, SEQ:N]).then_inc(sem("sample_apart"), 1)
                dve.tensor_copy(k_s[kind], k_t[kind][:, :, SEQ:N]).then_inc(sem("sample_apart"), 1)
            st.link(dve.memset(q_wide, 0.0))
            dve.wait_ge(sem("sample_apart"), 4)
            for pair in range(NPAIR):
                for e in range(2):
                    h = 2 * pair + e
                    dve.tensor_copy(q_wide[:, pair, :, h * DT:(h + 1) * DT],
                                    q_s["dil"][:, h, :].rearrange("p (b t) -> p b t", t=DT))
        for engine in programs:
            programs[engine].append(end_stage)

        KB = SEQ // P
        AT = (0, 512, 1024, 896)
        WIDE = 1280
        place[0] = WORK
        sb_z = [take(WIDE) for _ in range(2)]
        sb_e = [take(WIDE) for _ in range(2)]
        sb_p = [take(WIDE) for _ in range(2)]
        o_nat = take(4 * D).rearrange("p (t d) -> p t d", t=4)
        counts = take(4 * SEQ).rearrange("p (t k) -> p t k", t=4)
        bias = small[:, 0:8]
        bias_ht = small[:, 8:40].rearrange("p (h t) -> p h t", h=H)

        def region(kb):
            return slice(AT[kb], AT[kb] + SEQ - kb * P)

        @part("sp")
        def _(sp):
            sp.dma_start(bias, sb_logit_bias.rearrange("(o h) -> o h", o=1).to_broadcast([P, H]))\
              .then_inc(sem("bias_in"), 16)
            sp.dma_start(counts, count_prompt.rearrange("p (t k) -> p t k", t=4)).then_inc(sem("counts_in"), 16)

        @part("pe")
        def _(pe):
            def scores(h):
                if h >= 1:
                    pe.wait_ge(sem("sb_logits"), h)
                for kb in range(KB):
                    r = region(kb)
                    pe.matmul(psum[:, r], lhsT=k_t["sb"][:, h // 2, kb * P:(kb + 1) * P],
                              rhs=q_z["sb"][:, h, kb * P:SEQ], start=True, stop=False)
                    last = pe.matmul(psum[:, r.start:r.start + P], lhsT=ident, rhs=diag, start=False, stop=True)
                last.then_inc(sem("sb_scores"), 1)

            scores(0)
            for h in range(H):
                if h + 1 < H:
                    scores(h + 1)
                pe.wait_ge(sem("sb_softplus"), h + 1)
                if h >= 1:
                    pe.wait_ge(sem("sb_exponents"), h)
                sp_h = sb_p[h % 2]
                for kb in range(KB):
                    r = region(kb)
                    last = pe.matmul(bank(3, 3)[:, r], lhsT=tri, rhs=sp_h[:, r], start=True, stop=(kb == KB - 1))
                    for later in range(kb + 1, KB):
                        a = r.start + (later - kb) * P
                        last = pe.matmul(bank(3, 3)[:, a:r.stop], lhsT=ones, rhs=sp_h[:, region(later)],
                                         start=False, stop=(later == KB - 1))
                last.then_inc(sem("sb_sums"), 1)
                pe.wait_ge(sem("sb_weights"), h + 1)
                if h >= 2:
                    pe.wait_ge(sem("sb_out_copied"), h - 1)
                out = bank(6 + h % 2)
                for qb in range(KB):
                    for kb in range(qb + 1):
                        a = AT[kb] + (qb - kb) * P
                        last = pe.matmul(out[:, qb * HD:(qb + 1) * HD], lhsT=sb_z[h % 2][:, a:a + P],
                                         rhs=v_n["sb"][:, kb, h * HD:(h + 1) * HD], start=(kb == 0), stop=(kb == qb))
                last.then_inc(sem("sb_out"), 1)

        @part("act")
        def _(act):
            st = own_steps(act, "act")

            def log_part(h):
                e = sb_e[h % 2]
                act.wait_ge(sem("sb_logits"), h + 1)
                if h >= 2:
                    act.wait_ge(sem("sb_softplus"), h - 1)
                st.link(act.activation(e, sb_z[h % 2], ACT.Abs))
                st.link(act.activation(e, e, ACT.Exp, scale=-1.0))
                act.activation(e, e, ACT.Ln, bias=1.0).then_inc(sem("sb_log"), 1)

            log_part(0)
            for h in range(H):
                if h + 1 < H:
                    log_part(h + 1)
                act.wait_ge(sem("sb_exponents"), h + 1)
                act.activation(sb_z[h % 2], sb_z[h % 2], ACT.Exp).then_inc(sem("sb_weights"), 1)
                act.wait_ge(sem("sb_out"), h + 1)
                act.activation(o_nat[:, :, h * HD:(h + 1) * HD],
                               bank(6 + h % 2)[:, 0:KB * HD].rearrange("p (t d) -> p t d", t=KB), ACT.Copy)\
                    .then_inc(sem("sb_out_copied"), 1)

        @part("dve")
        def _(dve):
            dve.wait_ge(sem("bias_in"), 16)

            def logits(h):
                dve.wait_ge(sem("sb_scores"), h + 1)
                if h >= 2:
                    dve.wait_ge(sem("sb_out"), h - 1)
                dve.tensor_scalar(sb_z[h % 2], psum[:, 0:WIDE], SCALE, bias[:, h:h + 1], ALU.mult, ALU.add)\
                    .then_inc(sem("sb_logits"), 1)

            def softplus(h):
                dve.wait_ge(sem("sb_log"), h + 1)
                dve.wait_ge(sem("sb_logits"), h + 1)
                if h >= 2:
                    dve.wait_ge(sem("sb_sums"), h - 1)
                dve.scalar_tensor_tensor(sb_p[h % 2], sb_z[h % 2], 0.0, sb_e[h % 2], ALU.max, ALU.add)\
                    .then_inc(sem("sb_softplus"), 1)

            logits(0)
            softplus(0)
            for h in range(H):
                if h + 1 < H:
                    logits(h + 1)
                dve.wait_ge(sem("sb_sums"), h + 1)
                dve.tensor_tensor(sb_z[h % 2], sb_z[h % 2], bank(3, 3)[:, 0:WIDE], ALU.subtract)\
                    .then_inc(sem("sb_exponents"), 1)
                if h + 1 < H:
                    softplus(h + 1)

        for engine in programs:
            programs[engine].append(end_stage)

        PT_AT = (0, 1, 3, 6)
        dl_p = [take(WIDE, WORK)] + [take(WIDE)]
        dl_t = [take(WIDE) for _ in range(2)]
        dl_max, dl_neg, dl_sum, dl_inv = ([small[:, 64 + 16 * i + 4 * e:68 + 16 * i + 4 * e] for e in range(2)]
                                          for i in range(4))
        assert place[0] <= WORK + 6 * WIDE

        @part("pe")
        def _(pe):
            def scores(h):
                if h >= 1:
                    pe.wait_ge(sem("dl_logits"), 4 * h)
                for qb in range(KB):
                    last = pe.matmul(bank(qb)[:, 0:(qb + 1) * P], lhsT=q_z["dil"][:, h, qb * P:(qb + 1) * P],
                                     rhs=k_t["dil"][:, h // 2, 0:(qb + 1) * P], start=True, stop=True)
                last.then_inc(sem("dl_scores"), 1)

            scores(0)
            for h in range(H):
                if h + 1 < H:
                    scores(h + 1)
                pe.wait_ge(sem("dl_exp"), 4 * h + 4)
                if h >= 1:
                    pe.wait_ge(sem("dl_turned"), h)
                for j in range(10):
                    last = pe.transpose(bank(4, 3)[:, j * P:(j + 1) * P], dl_p[h % 2][:, j * P:(j + 1) * P], ident)
                last.then_inc(sem("dl_turn"), 1)
                pe.wait_ge(sem("dl_turned"), h + 1)
                if h >= 1:
                    pe.wait_ge(sem("dl_out_scaled"), h)
                for qb in range(KB):
                    for kb in range(qb + 1):
                        a = (PT_AT[qb] + kb) * P
                        c = qb * HD
                        last = pe.matmul(bank(7)[:, c:c + HD], lhsT=dl_t[h % 2][:, a:a + P],
                                         rhs=v_n["dil"][:, kb, h * HD:(h + 1) * HD], start=(kb == 0), stop=(kb == qb))
                last.then_inc(sem("dl_out"), 1)

        @part("act")
        def _(act):
            def exps(h):
                act.wait_ge(sem("dl_neg"), h + 1)
                for qb in range(KB):
                    a = PT_AT[qb] * P
                    x = dl_p[h % 2][:, a:a + (qb + 1) * P]
                    act.activation(x, x, ACT.Exp, bias=dl_neg[h % 2][:, qb:qb + 1],
                                   accum_out=dl_sum[h % 2][:, qb:qb + 1]).then_inc(sem("dl_exp"), 1)

            exps(0)
            for h in range(H):
                if h + 1 < H:
                    exps(h + 1)
                act.wait_ge(sem("dl_turn"), h + 1)
                if h >= 2:
                    act.wait_ge(sem("dl_out"), h - 1)
                act.activation(dl_t[h % 2], bank(4, 3)[:, 0:WIDE], ACT.Copy).then_inc(sem("dl_turned"), 1)

        @part("dve")
        def _(dve):
            dve.wait_ge(sem("counts_in"), 16)

            def logits(h):
                dve.wait_ge(sem("dl_scores"), h + 1)
                if h >= 2:
                    dve.wait_ge(sem("dl_turn"), h - 1)
                for qb in range(KB):
                    a, w = PT_AT[qb] * P, (qb + 1) * P
                    dve.tensor_tensor_reduce(out=dl_p[h % 2][:, a:a + w], in0=bank(qb)[:, 0:w], in1=counts[:, qb, 0:w],
                                             scale=SCALE, scalar=LOWEST, op0=ALU.add, op1=ALU.max,
                                             accum_out=dl_max[h % 2][:, qb:qb + 1]).then_inc(sem("dl_logits"), 1)
                dve.wait_ge(sem("dl_logits"), 4 * h + 4)
                dve.tensor_scalar(dl_neg[h % 2], dl_max[h % 2], -1.0, None, ALU.mult).then_inc(sem("dl_neg"), 1)

            logits(0)
            for h in range(H):
                if h + 1 < H:
                    logits(h + 1)
                dve.wait_ge(sem("dl_exp"), 4 * h + 4)
                dve.reciprocal(dl_inv[h % 2], dl_sum[h % 2]).then_inc(sem("dl_inverse"), 1)
                dve.wait_ge(sem("dl_inverse"), h + 1)
                dve.wait_ge(sem("dl_out"), h + 1)
                dve.tensor_tensor(o_nat[:, :, DH + h * HD:DH + (h + 1) * HD],
                                  bank(7)[:, 0:KB * HD].rearrange("p (t d) -> p t d", t=KB),
                                  dl_inv[h % 2].rearrange("p (t o) -> p t o", o=1).to_broadcast([P, KB, HD]), ALU.mult)\
                    .then_inc(sem("dl_out_scaled"), 1)

        @part("pe")
        def _(pe):
            pe.wait_ge(sem("dl_out_scaled"), H)
            for t in range(4):
                for half in range(2):
                    u = 2 * t + half
                    if u >= 4:
                        pe.wait_ge(sem("o_t_copied"), u - 3)
                    for c in range(4):
                        last = pe.transpose(bank(u % 4)[:, c * P:(c + 1) * P],
                                            o_nat[:, t, (4 * half + c) * P:(4 * half + c + 1) * P], ident)
                    last.then_inc(sem("o_t_ready"), 1)

        @part("act")
        def _(act):
            for u in range(8):
                t, half = u // 2, u % 2
                act.wait_ge(sem("o_t_ready"), u + 1)
                act.activation(o_t[:, 4 * half:4 * half + 4, t * P:(t + 1) * P],
                               bank(u % 4).rearrange("p (c n) -> p c n", c=4), ACT.Copy).then_inc(sem("o_t_copied"), 1)

        for engine in programs:
            programs[engine].append(end_stage)

        HT = H * DT
        SW = PAGES * HT
        place[0] = SAMPLE
        k_page = [take(DH) for _ in range(K_SLOTS)]
        v_page = [take(PAGES * DH).rearrange("p (j c) -> p j c", j=PAGES) for _ in range(2)]
        k_turned = [take(NPAIR * P).rearrange("p (c n) -> p c n", c=NPAIR) for _ in range(2)]
        ss_z, ss_e, ss_p, ss_c = (take(SW) for _ in range(4))
        new_z, new_e, new_p = (take(DB * HT) for _ in range(3))
        mask_sb = take(DB * HT)
        cache_k = cache_k_sb.rearrange("g p h d -> g p (h d)")
        cache_v = cache_v_sb.rearrange("g p h d -> g p (h d)")

        def by_b(a):
            return a.rearrange("p (b n) -> p b n", b=DB)

        @part("sp")
        def _(sp):
            sp.dma_start(mask_sb[0:NS, :], mask_new).then_inc(sem("mask_in"), 16)
            with sp.Fori(0, DB // 2) as i:
                for s in range(2):
                    for j in range(PAGES):
                        g = 2 * PAGES * i + PAGES * s + j
                        page = sp.value_load(pages_sb[0:1, bass.ds(g, 1)], min_val=0, max_val=N_POOL - 1)
                        sp.wait_ge(sem("page_turned"), g + 1)
                        sp.dma_start(k_page[j % K_SLOTS], cache_k[bass.ds(page, 1)].rearrange("o p c -> (o p) c"))\
                            .then_inc(sem(f"k_page_{j % K_SLOTS}"), 16)
                        if j == 0:
                            sp.wait_ge(sem("seq_out"), 2 * i + s + 1)
                        sp.dma_start(v_page[s][:, j, :], cache_v[bass.ds(page, 1)].rearrange("o p c -> (o p) c"))\
                            .then_inc(sem(f"v_pages_{s}"), 16)

        @part("pe")
        def _(pe):
            pe.drain().then_inc(sem("page_turned"), K_SLOTS)
            pe.drain().then_inc(sem("page_scored"), 2)
            pe.drain().then_inc(sem("seq_out"), 2)
            out = by_b(bank(5)[0:NS, 0:DB * HT])
            for pair in range(NPAIR):
                last = pe.matmul(out[:, :, pair * 8:(pair + 1) * 8].rearrange("p b (e t) -> p b e t", e=2),
                                 lhsT=k_s["sb"][:, pair, :],
                                 rhs=q_s["sb"][:, 2 * pair:2 * pair + 2, :].rearrange("p e (b t) -> p b e t", t=DT),
                                 start=True, stop=True)
            last.then_inc(sem("new_scores"), 1)
            pe.wait_ge(sem("new_softplus"), 1)
            pe.matmul(bank(6)[:, 0:DB * HT], lhsT=tri, rhs=new_p, start=True, stop=True).then_inc(sem("new_sums"), 1)

            def turn(b, j):
                pe.wait_ge(sem(f"k_page_{j % K_SLOTS}"), 32 * b + 16 * (j // K_SLOTS) + 16)
                pe.wait_ge(sem(f"page_copied_{j % 2}"), 8 * b + j // 2 + 1)
                for pair in range(NPAIR):
                    last = pe.transpose(bank(j % 2)[:, pair * P:(pair + 1) * P],
                                        k_page[j % K_SLOTS][:, pair * P:(pair + 1) * P], ident)
                last.then_inc(sem("page_turned"), 1)

            def score(b, j):
                pe.wait_ge(sem(f"page_copied_{j % 2}"), 8 * b + j // 2 + 2)
                for pair in range(NPAIR):
                    c = j * HT + pair * 8
                    last = pe.matmul(bank(2)[:, c:c + 8].rearrange("p (e t) -> p e t", e=2),
                                     lhsT=k_turned[j % 2][:, pair, :],
                                     rhs=q_s["sb"][:, 2 * pair:2 * pair + 2, bass.ds(b * DT, DT)], start=True, stop=True)
                last.then_inc(sem("page_scored"), 1)

            with pe.Fori(0, DB // 2) as i:
                for s in range(2):
                    b = 2 * i + s
                    for j in range(PAGES):
                        turn(b, j)
                        if j == 1:
                            pe.wait_ge(sem("seq_logits"), b + 1)
                        if j >= 1:
                            score(b, j - 1)
                    score(b, PAGES - 1)
                    pe.wait_ge(sem("seq_suffix"), b + 1)
                    pe.matmul(bank(3), lhsT=tri, rhs=ss_p, start=True, stop=False)
                    pe.matmul(bank(3)[:, 0:SW - HT], lhsT=ones, rhs=ss_c[:, HT:SW], start=False, stop=False)
                    pe.matmul(bank(3).rearrange("p (j n) -> p j n", j=PAGES), lhsT=ones,
                              rhs=by_b(new_p)[:, bass.ds(b, 1), :].to_broadcast([P, PAGES, HT]),
                              start=False, stop=True).then_inc(sem("seq_sums"), 1)
                    pe.wait_ge(sem("seq_weights"), b + 1)
                    pe.wait_ge(sem(f"v_pages_{s}"), 256 * i + 256)
                    for j in range(PAGES + 1):
                        for pair in range(NPAIR):
                            if j < PAGES:
                                v, w = v_page[s][:, j, :], ss_z[:, j * HT + pair * 8:j * HT + pair * 8 + 8]
                            else:
                                v = v_n["sb"][:, 4, :]
                                w = by_b(new_z)[:, bass.ds(b, 1), pair * 8:pair * 8 + 8].rearrange("p o n -> p (o n)")
                            last = pe.matmul(bank(4)[:, pair * 8:pair * 8 + 8], lhsT=v[:, pair * P:(pair + 1) * P], rhs=w,
                                             start=(j == 0 and pair == 0), stop=(j == PAGES), skip_group_check=True)
                    last.then_inc(sem("seq_out"), 1)

        @part("act")
        def _(act):
            st = own_steps(act, "act")
            act.wait_ge(sem("new_logits"), 1)
            st.link(act.activation(new_e[0:NS], new_z[0:NS], ACT.Abs))
            st.link(act.activation(new_e[0:NS], new_e[0:NS], ACT.Exp, scale=-1.0))
            act.activation(new_e[0:NS], new_e[0:NS], ACT.Ln, bias=1.0).then_inc(sem("new_log"), 1)
            act.wait_ge(sem("new_exponents"), 1)
            act.activation(new_z[0:NS], new_z[0:NS], ACT.Exp).then_inc(sem("new_weights"), 1)
            act.drain().then_inc(sem("page_copied_0"), 1)
            with act.Fori(0, DB // 2) as i:
                st.enter(i, 4)
                for s in range(2):
                    b = 2 * i + s
                    for j in range(0, PAGES, 2):
                        act.wait_ge(sem("page_turned"), PAGES * b + j + 1 + K_SLOTS)
                        act.wait_ge(sem("page_scored"), PAGES * b + j + 1)
                        act.activation(k_turned[0], bank(0).rearrange("p (c n) -> p c n", c=NPAIR), ACT.Copy)\
                            .then_inc(sem("page_copied_0"), 1)
                    act.wait_ge(sem("seq_logits"), b + 2)
                    st.link(act.activation(ss_e, ss_z, ACT.Abs))
                    st.link(act.activation(ss_e, ss_e, ACT.Exp, scale=-1.0))
                    act.activation(ss_e, ss_e, ACT.Ln, bias=1.0).then_inc(sem("seq_log"), 1)
                    act.wait_ge(sem("seq_exponents"), b + 1)
                    act.activation(ss_z, ss_z, ACT.Exp).then_inc(sem("seq_weights"), 1)
                st.leave(DB // 2)

        @part("dve")
        def _(dve):
            st = own_steps(dve, "dve")
            st.link(dve.tensor_copy(bias_ht, bias.rearrange("p (h o) -> p h o", o=1).to_broadcast([P, H, DT])))
            st.do(dve.memset(new_z, 0.0))
            st.do(dve.memset(new_p, 0.0))
            flat_bias = small[:, 8:40]
            dve.wait_ge(sem("mask_in"), 16)
            st.wait()
            st.link(dve.tensor_tensor(by_b(mask_sb)[0:NS], by_b(mask_sb)[0:NS],
                                      flat_bias[0:NS].rearrange("p (o n) -> p o n", o=1).to_broadcast([NS, DB, HT]), ALU.add))
            dve.wait_ge(sem("new_scores"), 1)
            dve.scalar_tensor_tensor(new_z[0:NS], bank(5)[0:NS, 0:DB * HT], SCALE, mask_sb[0:NS], ALU.mult, ALU.add)\
                .then_inc(sem("new_logits"), 1)
            dve.wait_ge(sem("new_log"), 1)
            dve.scalar_tensor_tensor(new_p[0:NS], new_z[0:NS], 0.0, new_e[0:NS], ALU.max, ALU.add)\
                .then_inc(sem("new_softplus"), 1)
            dve.wait_ge(sem("new_sums"), 1)
            dve.tensor_tensor(new_z[0:NS], new_z[0:NS], bank(6)[0:NS, 0:DB * HT], ALU.subtract)\
                .then_inc(sem("new_exponents"), 1)
            dve.drain().then_inc(sem("page_copied_1"), 1)
            dve.drain().then_inc(sem("seq_logits"), 1)
            with dve.Fori(0, DB // 2) as i:
                st.enter(i, 12)
                for s in range(2):
                    b = 2 * i + s
                    for j in range(1, PAGES, 2):
                        dve.wait_ge(sem("page_turned"), PAGES * b + j + 1 + K_SLOTS)
                        dve.wait_ge(sem("page_scored"), PAGES * b + j + 1)
                        dve.tensor_copy(k_turned[1], bank(1).rearrange("p (c n) -> p c n", c=NPAIR))\
                            .then_inc(sem("page_copied_1"), 1)
                    dve.wait_ge(sem("page_scored"), PAGES * b + PAGES + 2)
                    dve.wait_ge(sem("seq_out"), b + 2)
                    dve.scalar_tensor_tensor(ss_z.rearrange("p (j n) -> p j n", j=PAGES),
                                             bank(2).rearrange("p (j n) -> p j n", j=PAGES), SCALE,
                                             flat_bias.rearrange("p (o n) -> p o n", o=1).to_broadcast([P, PAGES, HT]),
                                             ALU.mult, ALU.add).then_inc(sem("seq_logits"), 1)
                    dve.wait_ge(sem("seq_log"), b + 1)
                    dve.wait_ge(sem("seq_logits"), b + 2)
                    st.link(dve.scalar_tensor_tensor(ss_p, ss_z, 0.0, ss_e, ALU.max, ALU.add))
                    st.do(dve.tensor_copy(ss_c[:, SW - HT:SW], ss_p[:, SW - HT:SW]))
                    st.link(dve.tensor_tensor(ss_c[:, 0:SW - HT], ss_p[:, 0:SW - HT], ss_p[:, HT:SW], ALU.add))
                    for step in (2, 4, 8):
                        w = SW - step * HT
                        ins = dve.tensor_tensor(ss_c[:, 0:w], ss_c[:, 0:w], ss_c[:, step * HT:SW], ALU.add)
                        if step < 8:
                            st.link(ins)
                        else:
                            ins.then_inc(sem("seq_suffix"), 1)
                    dve.wait_ge(sem("seq_sums"), b + 1)
                    st.link(dve.tensor_tensor(ss_c, ss_z, bank(3), ALU.subtract))
                    dve.tensor_copy(ss_z, ss_c).then_inc(sem("seq_exponents"), 1)
                    dve.wait_ge(sem("seq_out"), b + 3)
                    out = bank(4)[:, 0:HT].rearrange("p (c n) -> p c n", c=NPAIR)
                    for e in range(2):
                        r = slice(64 * e, 64 * e + 64)
                        dve.tensor_scalar(o_t[r, 0:4, bass.ds(b * DT + SEQ, DT)], out[r, :, e * DT:(e + 1) * DT],
                                          1.0, None, ALU.mult).then_inc(sem("seq_stored"), 1)
                st.leave(DB // 2)

        for engine in programs:
            programs[engine].append(end_stage)

        WK = NW * P
        place[0] = SAMPLE
        kw = [take(NW * DH).rearrange("p (m c) -> p m c", m=NW) for _ in range(2)]
        vw = [take(NW * DH).rearrange("p (m c) -> p m c", m=NW) for _ in range(2)]
        kw_t = take(NPAIR * WK).rearrange("p (c n) -> p c n", c=NPAIR)
        q_b = take(NPAIR * HT).rearrange("p (c n) -> p c n", c=NPAIR)
        dw_p = take(WK + NS)
        dw_t = take((NW + 1) * HT).rearrange("p (m n) -> p m n", m=NW + 1)
        window_sb = take(WK)
        fresh_sb = take(DB * NS)
        dw_max, dw_top, dw_sum, dw_inv = (small[0:HT, 128 + 4 * i:129 + 4 * i] for i in range(4))
        dw_max2 = small[0:HT, 129:130]
        near_rows = [a.rearrange("b (m p) h d -> b p m (h d)", p=P) for a in (state_k_win, state_v_win)]
        far_rows = [a.rearrange("b (m g s) h d -> b m g s (h d)", g=32, s=16) for a in (state_k_win, state_v_win)]

        @part("sp")
        def _(sp):
            sp.dma_start(window_sb[0:HT, :], count_window).then_inc(sem("window_in"), 16)
            sp.dma_start(fresh_sb[0:HT, :], count_fresh).then_inc(sem("window_in"), 16)
            with sp.Fori(0, DB // 2) as i:
                for s in range(2):
                    b = 2 * i + s
                    for x, to, name in ((0, kw, "k"), (1, vw, "v")):
                        sp.wait_ge(sem("kw_turned" if name == "k" else "dw_out"), b + 1)
                        sp.dma_start(to[s][:, 0:NEAR, :],
                                     near_rows[x][bass.ds(b, 1), :, WIN // P - NEAR:WIN // P, :]
                                     .rearrange("o p m c -> (o p) m c")).then_inc(sem(f"{name}_window_{s}"), 16)
                        for m in range(FAR):
                            sp.dma_start(to[s][:, NEAR + m, :],
                                         far_rows[x][bass.ds(b, 1), m, :, 0:DT, :].rearrange("o g s c -> (o g) s c"))\
                                .then_inc(sem(f"{name}_window_{s}"), 16)

        @part("pe")
        def _(pe):
            pe.drain().then_inc(sem("kw_turned"), 2)
            pe.drain().then_inc(sem("dw_out"), 2)
            pe.drain().then_inc(sem("dw_scores"), 1)
            with pe.Fori(0, DB // 2) as i:
                for s in range(2):
                    b = 2 * i + s
                    pe.wait_ge(sem(f"k_window_{s}"), 64 * i + 64)
                    for m in range(NW):
                        pe.wait_ge(sem(f"kw_copied_{m % 2}"), (4 - m % 2) * b + m // 2 + 1)
                        for pair in range(NPAIR):
                            last = pe.transpose(bank(m % 2)[:, pair * P:(pair + 1) * P],
                                                kw[s][:, m, pair * P:(pair + 1) * P], ident)
                        last.then_inc(sem("kw_turned" if m == NW - 1 else "kw_turn"), 1)
                    pe.wait_ge(sem("kw_copied_0"), 4 * b + 5)
                    pe.wait_ge(sem("kw_copied_1"), 3 * b + 4)
                    pe.wait_ge(sem("q_b_ready"), b + 1)
                    pe.wait_ge(sem("dw_logits"), 2 * b + 2)
                    for a, w in ((0, BANK), (BANK, WK - BANK), (WK, NS)):
                        for pair in range(NPAIR):
                            rhs = kw_t[:, pair, a:a + w] if a < WK else k_s["dil"][:, pair, :]
                            last = pe.matmul(bank(2, 2)[0:HT, a:a + w], lhsT=q_b[:, pair, :], rhs=rhs,
                                             start=(pair == 0), stop=(pair == NPAIR - 1))
                    last.then_inc(sem("dw_scores"), 1)
                    pe.wait_ge(sem("dw_scaled"), b + 1)
                    for m in range(NW + 1):
                        w = P if m < NW else NS
                        last = pe.transpose(bank(6, 2)[0:w, m * P:(m + 1) * P], dw_p[:, m * P:m * P + w], ident)
                    last.then_inc(sem("dw_turn"), 1)
                    pe.wait_ge(sem("dw_turned"), b + 1)
                    pe.wait_ge(sem(f"v_window_{s}"), 64 * i + 64)
                    pe.wait_ge(sem("dw_stored"), 2 * b + 1)
                    for m in range(NW + 1):
                        v = vw[s][:, m, :] if m < NW else v_n["dil"][:, 4, :]
                        for pair in range(NPAIR):
                            last = pe.matmul(bank(5)[:, pair * 8:pair * 8 + 8], lhsT=v[:, pair * P:(pair + 1) * P],
                                             rhs=dw_t[:, m, pair * 8:pair * 8 + 8],
                                             start=(m == 0 and pair == 0), stop=(m == NW), skip_group_check=True)
                    last.then_inc(sem("dw_out"), 1)

        @part("pool")
        def _(pool):
            with pool.Fori(0, DB) as b:
                pool.wait_ge(sem("dw_scores"), b + 1)
                pool.tensor_copy(q_b, q_wide[:, :, bass.ds(b, 1), :].rearrange("p c o n -> p (c o) n"))\
                    .then_inc(sem("q_b_ready"), 1)

        @part("act")
        def _(act):
            act.drain().then_inc(sem("kw_copied_0"), 1)
            with act.Fori(0, DB // 2) as i:
                for s in range(2):
                    b = 2 * i + s
                    act.wait_ge(sem("dw_scores"), b + 1)
                    for m in range(0, NW, 2):
                        if m < NW - 1:
                            act.wait_ge(sem("kw_turn"), (NW - 1) * b + m + 1)
                        else:
                            act.wait_ge(sem("kw_turned"), b + 3)
                        act.activation(kw_t[:, :, m * P:(m + 1) * P], bank(0).rearrange("p (c n) -> p c n", c=NPAIR),
                                       ACT.Copy).then_inc(sem("kw_copied_0"), 1)
                    act.wait_ge(sem("dw_top"), b + 1)
                    act.activation(dw_p[0:HT], dw_p[0:HT], ACT.Exp, bias=dw_top, accum_out=dw_sum)\
                        .then_inc(sem("dw_exp"), 1)

        @part("dve")
        def _(dve):
            st = own_steps(dve, "dve")
            st.do(dve.memset(dw_p, 0.0))
            st.link(dve.memset(dw_t, 0.0))
            turned = bank(6, 2).rearrange("p (m n) -> p m n", m=NW + 1)
            dve.drain().then_inc(sem("kw_copied_1"), 1)
            dve.drain().then_inc(sem("dw_logits"), 2)
            dve.drain().then_inc(sem("dw_stored"), 1)
            dve.wait_ge(sem("window_in"), 2 * 16)
            with dve.Fori(0, DB // 2) as i:
                st.enter(i, 6)
                for s in range(2):
                    b = 2 * i + s
                    for m in range(1, NW, 2):
                        dve.wait_ge(sem("kw_turn"), (NW - 1) * b + m + 1)
                        dve.tensor_copy(kw_t[:, :, m * P:(m + 1) * P], bank(1).rearrange("p (c n) -> p c n", c=NPAIR))\
                            .then_inc(sem("kw_copied_1"), 1)
                    dve.wait_ge(sem("dw_scores"), b + 2)
                    st.do(dve.tensor_tensor(dw_p[0:HT, WK:WK + NS], bank(2, 2)[0:HT, WK:WK + NS],
                                              fresh_sb[0:HT, bass.ds(b * NS, NS)], ALU.add))
                    dve.tensor_tensor_reduce(out=dw_p[0:HT, 0:WK], in0=bank(2, 2)[0:HT, 0:WK], in1=window_sb[0:HT],
                                             scale=SCALE, scalar=LOWEST, op0=ALU.add, op1=ALU.max, accum_out=dw_max)\
                        .then_inc(sem("dw_logits"), 1)
                    st.wait()
                    dve.tensor_scalar(dw_p[0:HT, WK:WK + NS], dw_p[0:HT, WK:WK + NS], SCALE, None, ALU.mult)\
                        .then_inc(sem("dw_logits"), 1)
                    dve.wait_ge(sem("dw_logits"), 2 * b + 4)
                    st.link(dve.tensor_reduce(dw_max2, dw_p[0:HT, WK:WK + NS], AX_X, ALU.max))
                    st.link(dve.tensor_tensor(dw_top, dw_max, dw_max2, ALU.max))
                    dve.tensor_scalar(dw_top, dw_top, -1.0, None, ALU.mult).then_inc(sem("dw_top"), 1)
                    dve.wait_ge(sem("dw_exp"), b + 1)
                    dve.reciprocal(dw_inv, dw_sum).then_inc(sem("dw_inverse"), 1)
                    dve.wait_ge(sem("dw_inverse"), b + 1)
                    dve.tensor_scalar(dw_p[0:HT], dw_p[0:HT], dw_inv, None, ALU.mult).then_inc(sem("dw_scaled"), 1)
                    dve.wait_ge(sem("dw_turn"), b + 1)
                    dve.tensor_copy(dw_t[:, 0:NW, :], turned[:, 0:NW, 0:HT])
                    dve.tensor_copy(dw_t[0:NS, NW, :], turned[0:NS, NW, 0:HT]).then_inc(sem("dw_turned"), 1)
                    dve.wait_ge(sem("dw_out"), b + 3)
                    out = bank(5)[:, 0:HT].rearrange("p (c n) -> p c n", c=NPAIR)
                    for e in range(2):
                        r = slice(64 * e, 64 * e + 64)
                        dve.tensor_scalar(o_t[r, 4:8, bass.ds(b * DT + SEQ, DT)], out[r, :, e * DT:(e + 1) * DT],
                                          1.0, None, ALU.mult).then_inc(sem("dw_stored"), 1)
                st.leave(DB // 2)
            dve.memset(o_t[:, :, N:NP], 0.0).then_inc(sem("pad_cleared"), 1)

        for engine in programs:
            programs[engine].append(end_stage)

        place[0] = ERA
        wo_sb = take(KD * D).rearrange("p (k n) -> p k n", k=KD)
        row_g, row_b = take(D), take(D)
        row_g2, row_b2 = take(D), take(D)
        h1_t = take(KD * NP).rearrange("p (k n) -> p k n", k=KD)
        PEER = place[0]
        stats = small[:, 64:76].rearrange("p (g s) -> p g s", g=2)
        mean_var, deviation, inverse = small[:, 80:82], small[:, 84:85], small[:, 88:89]
        eps = small[:, 92:93]

        def to_rows(a):
            return a.rearrange("(o d) -> o d", o=1).to_broadcast([P, D])

        def layer_norm(dve, st, x, g, b, name, r=P):
            for half in range(2):
                st.do(dve.bn_stats(stats[0:r, half, :], x[:, half * 512:(half + 1) * 512]))
            st.wait()
            dve.bn_aggr(mean_var[0:r], stats[0:r]).then_inc(sem(f"{name}_variance"), 1)

            def finish(count):
                dve.wait_ge(sem(f"{name}_deviation"), count)
                st.link(dve.reciprocal(inverse[0:r], deviation[0:r]))
                st.link(dve.tensor_scalar(x, x, mean_var[0:r, 0:1], inverse[0:r], ALU.subtract, ALU.mult))
                st.link(dve.tensor_tensor(x, x, g[0:r], ALU.mult))
                dve.tensor_tensor(x, x, b[0:r], ALU.add).then_inc(sem(f"{name}_done"), 1)

            return finish

        @part("sp")
        def _(sp):
            sp.dma_start(wo_sb, w_out.rearrange("(k p) n -> p k n", p=P)).then_inc(sem("w_out_in"), 16)
            for to, frm in ((row_g, ln1_g), (row_b, ln1_b), (row_g2, ln2_g), (row_b2, ln2_b)):
                sp.dma_start(to, to_rows(frm)).then_inc(sem("norms_in"), 16)

        @part("pe")
        def _(pe):
            pe.wait_ge(sem("w_out_in"), 16)

            def turn(t):
                pe.wait_ge(sem("ln1_done"), t + 1)
                for half in range(2):
                    u = 2 * t + half
                    if u >= 4:
                        pe.wait_ge(sem("h1_t_copied"), u - 3)
                    for k in range(4):
                        last = pe.transpose(bank(4 + u % 4)[:, k * P:(k + 1) * P],
                                            x_nat[:, t, (4 * half + k) * P:(4 * half + k + 1) * P], ident)
                    last.then_inc(sem("h1_t_ready"), 1)

            for t in range(NT):
                if t >= 2:
                    pe.wait_ge(sem("residual"), t - 1)
                for half in range(2):
                    for k in range(KD):
                        last = pe.matmul(bank(2 * (t % 2) + half), lhsT=o_t[:, k, t * P:(t + 1) * P],
                                         rhs=wo_sb[:, k, half * 512:(half + 1) * 512], start=(k == 0), stop=(k == KD - 1))
                last.then_inc(sem("mixed"), 1)
                if t >= 1:
                    turn(t - 1)
            turn(NT - 1)

        @part("act")
        def _(act):
            act.wait_ge(sem("eps_set"), 1)
            for t in range(NT):
                act.wait_ge(sem("ln1_variance"), t + 1)
                act.activation(deviation, mean_var[:, 1:2], ACT.Sqrt, bias=eps).then_inc(sem("ln1_deviation"), 1)
                for half in range(2):
                    u = 2 * t + half
                    act.wait_ge(sem("h1_t_ready"), u + 1)
                    act.activation(h1_t[:, 4 * half:4 * half + 4, t * P:(t + 1) * P],
                                   bank(4 + u % 4).rearrange("p (k n) -> p k n", k=4), ACT.Copy).then_inc(sem("h1_t_copied"), 1)

        @part("dve")
        def _(dve):
            st = own_steps(dve, "dve")
            dve.memset(eps, EPS).then_inc(sem("eps_set"), 1)
            dve.wait_ge(sem("norms_in"), 4 * 16)
            for t in range(NT):
                dve.wait_ge(sem("mixed"), t + 1)
                dve.scalar_tensor_tensor(x_nat[:, t, :], x_nat[:, t, :], ALPHA, bank(2 * (t % 2), 2), ALU.mult, ALU.add)\
                    .then_inc(sem("residual"), 1)
                dve.wait_ge(sem("residual"), t + 1)
                layer_norm(dve, st, x_nat[:, t, :], row_g, row_b, "ln1")(t + 1)

        for engine in programs:
            programs[engine].append(end_stage)

        NC = 2 * PH
        place[0] = PEER
        wq_sb = [take(KD * 512).rearrange("p (k c) -> p k c", k=KD) for _ in range(2)]
        s_all = take(NT * NC * NK).rearrange("p (t c n) -> p t c n", t=NT, c=NC)
        keys_n, keys_t = take(2 * P).rearrange("p (c d) -> p c d", c=2), take(2 * P).rearrange("p (c n) -> p c n", c=2)
        pq = [o_t.rearrange("p c n -> p (c n)")[:, e * NP:(e + 1) * NP] for e in range(2)]
        wq_g = peer_wq.rearrange("(k p) (g c) -> g p k c", p=P, c=512)

        @part("sp")
        def _(sp):
            sp.dma_start(keys_n, peer_subkeys.rearrange("c k d -> k c d")).then_inc(sem("subkeys_in"), 16)
            for g in range(4):
                if g >= 2:
                    sp.wait_ge(sem("pq_ready"), 8 * (g - 1))
                sp.dma_start(wq_sb[g % 2], wq_g[g]).then_inc(sem(f"wq_in_{g % 2}"), 16)

        @part("pe")
        def _(pe):
            pe.wait_ge(sem("subkeys_in"), 16)
            for c in range(2):
                last = pe.transpose(bank(4)[:, c * P:(c + 1) * P], keys_n[:, c, :], ident)
            last.then_inc(sem("subkeys_turn"), 1)
            pe.wait_ge(sem("subkeys_turned"), 1)

            def score(c):
                pe.wait_ge(sem("pq_copied"), 2 * c + 2)
                if c >= 2:
                    pe.wait_ge(sem("s_copied"), c - 1)
                for t in range(NT):
                    last = pe.matmul(bank(4 + 2 * (c % 2), 2)[:, t * P:(t + 1) * P], lhsT=pq[c % 2][:, t * P:(t + 1) * P],
                                     rhs=keys_t[:, c % 2, :], start=True, stop=True)
                last.then_inc(sem("s_ready"), 1)

            for c in range(NC):
                pe.wait_ge(sem(f"wq_in_{c // 4 % 2}"), 16 * (c // 8 + 1))
                for half in range(2):
                    u = 2 * c + half
                    if u >= 4:
                        pe.wait_ge(sem("pq_copied"), u - 3)
                    for k in range(KD):
                        last = pe.matmul(bank(u % 4)[:, 0:320], lhsT=wq_sb[c // 4 % 2][:, k, c % 4 * P:(c % 4 + 1) * P],
                                         rhs=h1_t[:, k, half * 320:(half + 1) * 320], start=(k == 0), stop=(k == KD - 1))
                    last.then_inc(sem("pq_ready"), 1)
                if c >= 1:
                    score(c - 1)
            score(NC - 1)

        @part("act")
        def _(act):
            for c in range(NC):
                for half in range(2):
                    u = 2 * c + half
                    act.wait_ge(sem("pq_ready"), u + 1)
                    if c >= 2:
                        act.wait_ge(sem("s_ready"), c - 1)
                    act.activation(pq[c % 2][:, half * 320:(half + 1) * 320], bank(u % 4)[:, 0:320], ACT.Copy)\
                        .then_inc(sem("pq_copied"), 1)

        @part("dve")
        def _(dve):
            dve.wait_ge(sem("subkeys_turn"), 1)
            dve.tensor_copy(keys_t, bank(4)[:, 0:2 * P].rearrange("p (c n) -> p c n", c=2)).then_inc(sem("subkeys_turned"), 1)
            for c in range(NC):
                dve.wait_ge(sem("s_ready"), c + 1)
                dve.tensor_copy(s_all[:, :, c, :], bank(4 + 2 * (c % 2), 2)[:, 0:NT * P].rearrange("p (t n) -> p t n", t=NT))\
                    .then_inc(sem("s_copied"), 1)

        for engine in programs:
            programs[engine].append(end_stage)

        place[0] = ERA
        s_rest = take(NC * NK).rearrange("p (c n) -> p c n", c=NC)
        top = take(NC * TK).rearrange("p (c k) -> p c k", c=NC)
        top_i = take(NC * TK).bitcast(U32).rearrange("p (c k) -> p c k", c=NC)
        top_f = take(NC * TK).rearrange("p (h e k) -> p h e k", h=PH, e=2)
        best = take(PH * TK).rearrange("p (h k) -> p h k", h=PH)
        best_i = take(PH * TK).bitcast(U32).rearrange("p (h k) -> p h k", h=PH)
        digit_u = [take(PH * TK).bitcast(U32) for _ in range(2)]
        digit_f = [take(PH * TK) for _ in range(2)]
        ijg = take(3 * P).rearrange("p (x n) -> p x n", x=3)
        best_sum, best_inv = take(PH), take(PH)
        gate_e = take(PH * TK)
        assert place[0] <= ERA + KD * D
        place[0] = PEER + 2 * KD * 512 + NT * NC * NK + 4 * P
        ijg_t = take(3 * NP).rearrange("p (x n) -> p x n", x=3)
        cand = take(PH * TK * TK, PEER).rearrange("p (h n) -> p h n", h=PH)
        cand_rest = take(PH * TK * TK).rearrange("p (h n) -> p h n", h=PH)
        equal = [take(PH * TK * TK) for _ in range(2)]
        assert place[0] <= PEER + 2 * KD * 512

        def top16(dve, st, values, rest, out, index, n):
            for c in range(n):
                st.do(dve.max(out[:, c, 0:8], values[:, c, :]))
            for c in range(n):
                st.wait(n - 1)
                st.do(dve.max_index(index[:, c, 0:8], out[:, c, 0:8], values[:, c, :]))
            for c in range(n):
                st.do(dve.match_replace(rest[:, c, :], out[:, c, 0:8], values[:, c, :], LOWEST))
            for c in range(n):
                st.wait(n - 1)
                st.do(dve.max(out[:, c, 8:16], rest[:, c, :]))
            for c in range(n):
                st.wait(n - 1)
                st.do(dve.max_index(index[:, c, 8:16], out[:, c, 8:16], rest[:, c, :]))
            st.wait()

        @part("act")
        def _(act):
            for t in range(NT):
                act.wait_ge(sem("best_less"), t + 1)
                act.activation(gate_e, gate_e, ACT.Exp).then_inc(sem("gate_exp"), 1)
                act.wait_ge(sem("ijg_turn"), t + 1)
                act.activation(ijg_t[:, :, t * P:(t + 1) * P], bank(0)[:, 0:3 * P].rearrange("p (x n) -> p x n", x=3), ACT.Copy)\
                    .then_inc(sem("ijg_turned"), 1)

        @part("pe")
        def _(pe):
            for t in range(NT):
                pe.wait_ge(sem("ijg_ready"), t + 1)
                if t >= 1:
                    pe.wait_ge(sem("ijg_turned"), t)
                for x in range(3):
                    last = pe.transpose(bank(0)[:, x * P:(x + 1) * P], ijg[:, x, :], ident)
                last.then_inc(sem("ijg_turn"), 1)

        @part("dve")
        def _(dve):
            st = own_steps(dve, "dve")
            grid = [PH, TK, TK]
            for t in range(NT):
                top16(dve, st, s_all[:, t], s_rest, top, top_i, NC)
                st.do(dve.tensor_copy(top_f.rearrange("p h e k -> p (h e k)"), top_i.rearrange("p c k -> p (c k)")))
                halves = top.rearrange("p (h e) k -> p h e k", e=2)
                st.link(dve.tensor_tensor(cand.rearrange("p h (a b) -> p h a b", a=TK),
                                          halves[:, :, 0, :].rearrange("p h (a o) -> p h a o", o=1).to_broadcast([P] + grid),
                                          halves[:, :, 1, :].rearrange("p h (o b) -> p h o b", o=1).to_broadcast([P] + grid),
                                          ALU.add))
                top16(dve, st, cand, cand_rest, best, best_i, PH)
                dve.tensor_tensor(gate_e.rearrange("p (h k) -> p h k", h=PH), best,
                                  best[:, :, 0:1].to_broadcast([P, PH, TK]), ALU.subtract).then_inc(sem("best_less"), 1)
                flat_i = best_i.rearrange("p h k -> p (h k)")
                st.do(dve.tensor_scalar(digit_u[0], flat_i, 4, None, ALU.logical_shift_right))
                st.link(dve.tensor_scalar(digit_u[1], flat_i, 15, None, ALU.bitwise_and))
                for e in range(2):
                    st.do(dve.tensor_copy(digit_f[e], digit_u[e]))
                st.wait()
                if t >= 1:
                    dve.wait_ge(sem("ijg_turned"), t)
                for e in range(2):
                    st.do(dve.tensor_tensor(equal[e].rearrange("p (n a) -> p n a", a=TK),
                                            digit_f[e].rearrange("p (n o) -> p n o", o=1).to_broadcast([P, PH * TK, TK]),
                                            iota[:, 0:TK].rearrange("p (o a) -> p o a", o=1).to_broadcast([P, PH * TK, TK]),
                                            ALU.is_equal))
                for e in range(2):
                    st.wait(1)
                    x = equal[e].rearrange("p (h k a) -> p h k a", h=PH, k=TK)
                    st.do(dve.tensor_tensor(x, x, top_f[:, :, e, :].rearrange("p h (o a) -> p h o a", o=1)
                                            .to_broadcast([P] + grid), ALU.mult))
                for e in range(2):
                    st.wait(1)
                    st.do(dve.tensor_reduce(ijg[:, e, :], equal[e].rearrange("p (n a) -> p n a", a=TK), AX_X, ALU.add))
                dve.wait_ge(sem("gate_exp"), t + 1)
                st.link(dve.tensor_reduce(best_sum, gate_e.rearrange("p (h k) -> p h k", h=PH), AX_X, ALU.add))
                st.link(dve.reciprocal(best_inv, best_sum))
                dve.tensor_tensor(ijg[:, 2, :].rearrange("p (h k) -> p h k", h=PH), gate_e.rearrange("p (h k) -> p h k", h=PH),
                                  best_inv.rearrange("p (h o) -> p h o", o=1).to_broadcast([P, PH, TK]), ALU.mult)\
                    .then_inc(sem("ijg_ready"), 1)

        for engine in programs:
            programs[engine].append(end_stage)

        HALF_C = CHUNK // 2
        place[0] = ERA
        table = [take(NK * CHUNK).rearrange("p (i n) -> p i n", i=NK) for _ in range(2)]
        assert place[0] <= ERA + KD * D + 2 * D
        place[0] = PEER
        hot_j = [take(HALF_C * NK).rearrange("p (n j) -> p n j", n=HALF_C) for _ in range(2)]
        hot_i = [take(HALF_C * NK).rearrange("p (n i) -> p n i", n=HALF_C) for _ in range(2)]

        def over_chunks(eng, body):
            with eng.Fori(0, NCHUNK // 2) as i:
                for s in range(2):
                    body(2 * i + s, s, i)
            body(NCHUNK - 1, 0, NCHUNK // 2)

        @part("sp")
        def _(sp):
            def store(c, s, i):
                sp.wait_ge(sem("table_copied"), 4 * c + 8)
                sp.dma_start(gates_dram[bass.ds(c, 1)].rearrange("o p n -> (o p) n"),
                             table[s].rearrange("p i n -> p (i n)")).then_inc(sem(f"table_out_{s}"), 16)

            over_chunks(sp, store)
            sp.wait_ge(sem("table_out_0"), 16 * (NCHUNK // 2 + 2))
            sp.wait_ge(sem("table_out_1"), 16 * (NCHUNK // 2 + 1))

        @part("dve")
        def _(dve):
            iota_b = iota.rearrange("p (o j) -> p o j", o=1).to_broadcast([P, HALF_C, NK])

            def hot(c, s, i):
                for half in range(2):
                    dve.wait_ge(sem("table_ready"), 4 * c + 2 * half + 4)
                    col = ijg_t[:, 1, bass.ds(c * CHUNK + half * HALF_C, HALF_C)]
                    dve.tensor_tensor(hot_j[half], iota_b,
                                      col.rearrange("p (n o) -> p n o", o=1).to_broadcast([P, HALF_C, NK]), ALU.is_equal)\
                        .then_inc(sem("hot_ready"), 1)
                    for n in range(HALF_C):
                        t = c * CHUNK + half * HALF_C + n
                        last = dve.tensor_scalar(hot_i[half][:, n, :], iota, ijg_t[:, 0, bass.ds(t, 1)],
                                                 ijg_t[:, 2, bass.ds(t, 1)], ALU.is_equal, ALU.mult)
                    last.then_inc(sem("hot_ready"), 1)

            over_chunks(dve, hot)

        @part("pe")
        def _(pe):
            pe.drain().then_inc(sem("table_ready"), 4)
            pe.wait_ge(sem("table_free"), 1)

            def spread(c, s, i):
                for half in range(2):
                    pe.wait_ge(sem("hot_ready"), 4 * c + 2 * half + 2)
                    for n in range(HALF_C):
                        if n % 8 == 0:
                            pe.wait_ge(sem("table_copied"), 4 * c + 2 * half + n // 8 + 1)
                        last = pe.matmul(bank(4 * half + n // 4)[:, n % 4 * NK:(n % 4 + 1) * NK],
                                         lhsT=hot_j[half][:, n, :], rhs=hot_i[half][:, n, :], start=True, stop=True)
                        if n % 8 == 7:
                            last.then_inc(sem("table_ready"), 1)

            over_chunks(pe, spread)

        @part("act")
        def _(act):
            act.drain().then_inc(sem("table_copied"), 4)
            act.drain().then_inc(sem("table_out_0"), 16)
            act.drain().then_inc(sem("table_out_1"), 16)
            act.drain().then_inc(sem("table_free"), 1)

            def copy(c, s, i):
                act.wait_ge(sem(f"table_out_{s}"), 16 * i + 16)
                for q in range(4):
                    act.wait_ge(sem("table_ready"), 4 * c + q + 5)
                    act.activation(table[s][:, :, 8 * q:8 * q + 8].rearrange("p i n -> p n i"),
                                   bank(2 * q, 2).rearrange("p (n i) -> p n i", n=8), ACT.Copy).then_inc(sem("table_copied"), 1)

            over_chunks(act, copy)

        for engine in programs:
            programs[engine].append(end_stage)

        f_t = take(KD * N, ERA).rearrange("p (c n) -> p c n", c=KD)
        place[0] = PEER
        u_sb = [take(D) for _ in range(GI)]
        v_sb = [take(D) for _ in range(GI)]
        u_t = [take(D).rearrange("p (k j) -> p k j", k=KD) for _ in range(2)]
        gelu = [take(N) for _ in range(2)]
        weight = [take(N) for _ in range(GI)]
        gates = take(NCHUNK * GI * CHUNK).rearrange("p (c i n) -> p c i n", c=NCHUNK, i=GI)
        gates_g = gates_dram.rearrange("c p (g n) -> p c g n", g=NG)

        @part("sp")
        def _(sp):
            with sp.Fori(0, NG) as g:
                for blk in range(GI):
                    sp.wait_ge(sem("u_turned"), GI * g + blk + 1)
                    sp.dma_start(u_sb[blk], peer_u[bass.ds((g * GI + blk) * P, P), :]).then_inc(sem(f"u_in_{blk}"), 16)
                sp.wait_ge(sem("weight_ready"), GI * g + GI)
                sp.dma_start(gates.rearrange("p c i n -> p c (i n)"),
                             gates_g[:, :, bass.ds(g, 1), :].rearrange("p c o n -> p (c o) n")).then_inc(sem("gates_in"), 16)
                sp.wait_ge(sem("y_ready"), 16 * g + 16)
                for blk in range(GI):
                    sp.dma_start(v_sb[blk], peer_v[bass.ds((g * GI + blk) * P, P), :]).then_inc(sem(f"v_in_{blk}"), 16)

        @part("pe")
        def _(pe):
            pe.drain().then_inc(sem("u_turned"), GI)
            pe.drain().then_inc(sem("h_ready"), 4)
            pe.drain().then_inc(sem("y_ready"), 16)

            def turn(g, blk):
                x = GI * g + blk
                pe.wait_ge(sem(f"u_in_{blk}"), 16 * g + 16)
                pe.wait_ge(sem("u_t_act"), x + 1)
                pe.wait_ge(sem("u_t_dve"), x + 1)
                for k in range(KD):
                    last = pe.transpose(bank(2 * (blk % 2), 2)[:, k * P:(k + 1) * P], u_sb[blk][:, k * P:(k + 1) * P], ident)
                last.then_inc(sem("u_turned"), 1)

            def hidden(g, blk):
                x = GI * g + blk
                pe.wait_ge(sem("u_t_act"), x + 3)
                pe.wait_ge(sem("u_t_dve"), x + 3)
                for half in range(2):
                    pe.wait_ge(sem("gelu_done"), 2 * x + half + 1)
                    for k in range(KD):
                        last = pe.matmul(bank(4 + half)[:, 0:HALF], lhsT=u_t[blk % 2][:, k, :],
                                         rhs=h1_t[:, k, half * HALF:(half + 1) * HALF], start=(k == 0), stop=(k == KD - 1))
                    last.then_inc(sem("h_ready"), 1)

            with pe.Fori(0, NG) as g:
                turn(g, 0)
                for blk in range(GI):
                    if blk + 1 < GI:
                        turn(g, blk + 1)
                    hidden(g, blk)
                for blk in range(GI):
                    pe.wait_ge(sem(f"v_in_{blk}"), 16 * g + 16)
                pe.wait_ge(sem("weight_ready"), GI * g + 2 * GI)
                for dc in range(KD):
                    for half in range(2):
                        pe.wait_ge(sem("y_added"), 16 * g + 2 * dc + half + 1)
                        for blk in range(GI):
                            last = pe.matmul(bank(6 + half)[:, 0:HALF], lhsT=v_sb[blk][:, dc * P:(dc + 1) * P],
                                             rhs=weight[blk][:, half * HALF:(half + 1) * HALF],
                                             start=(blk == 0), stop=(blk == GI - 1))
                        last.then_inc(sem("y_ready"), 1)

        @part("act")
        def _(act):
            act.drain().then_inc(sem("u_t_act"), 2)
            act.drain().then_inc(sem("gelu_done"), 2)

            def copy(g, blk):
                x = GI * g + blk
                act.wait_ge(sem("u_turned"), x + 1 + GI)
                act.wait_ge(sem("h_ready"), 2 * x + 2)
                act.activation(u_t[blk % 2][:, 0:4, :], bank(2 * (blk % 2)).rearrange("p (k j) -> p k j", k=4), ACT.Copy)\
                    .then_inc(sem("u_t_act"), 1)

            def activate(g, blk):
                x = GI * g + blk
                act.wait_ge(sem("weight_ready"), x + 3)
                for half in range(2):
                    act.wait_ge(sem("h_ready"), 2 * x + half + 5)
                    act.activation(gelu[blk % 2][:, half * HALF:(half + 1) * HALF], bank(4 + half)[:, 0:HALF], ACT.Gelu)\
                        .then_inc(sem("gelu_done"), 1)

            with act.Fori(0, NG) as g:
                copy(g, 0)
                for blk in range(GI):
                    if blk + 1 < GI:
                        copy(g, blk + 1)
                    activate(g, blk)

        @part("dve")
        def _(dve):
            dve.memset(f_t, 0.0).then_inc(sem("f_cleared"), 1)
            dve.wait_ge(sem("f_cleared"), 1)
            dve.drain().then_inc(sem("u_t_dve"), 2)
            dve.drain().then_inc(sem("weight_ready"), GI)
            dve.drain().then_inc(sem("y_added"), 2)

            def copy(g, blk):
                x = GI * g + blk
                dve.wait_ge(sem("u_turned"), x + 1 + GI)
                dve.wait_ge(sem("h_ready"), 2 * x + 2)
                dve.tensor_copy(u_t[blk % 2][:, 4:8, :], bank(2 * (blk % 2) + 1).rearrange("p (k j) -> p k j", k=4))\
                    .then_inc(sem("u_t_dve"), 1)

            with dve.Fori(0, NG) as g:
                copy(g, 0)
                for blk in range(GI):
                    if blk + 1 < GI:
                        copy(g, blk + 1)
                    if blk == 0:
                        dve.wait_ge(sem("gates_in"), 16 * g + 16)
                    dve.wait_ge(sem("gelu_done"), 2 * (GI * g + blk) + 4)
                    dve.tensor_tensor(weight[blk].rearrange("p (c n) -> p c n", c=NCHUNK),
                                      gelu[blk % 2].rearrange("p (c n) -> p c n", c=NCHUNK), gates[:, :, blk, :], ALU.mult)\
                        .then_inc(sem("weight_ready"), 1)
                for dc in range(KD):
                    for half in range(2):
                        k = 2 * dc + half
                        to = f_t[:, dc, half * HALF:(half + 1) * HALF]
                        dve.wait_ge(sem("y_ready"), 16 * g + k + 17)
                        if k < 2:
                            dve.wait_ge(sem("y_added"), 16 * g + k + 2)
                        dve.tensor_tensor(to, to, bank(6 + half)[:, 0:HALF], ALU.add).then_inc(sem("y_added"), 1)

        for engine in programs:
            programs[engine].append(end_stage)

        y_rows = y_prompt.rearrange("b (t p) d -> t (b p) d", p=P)

        @part("pe")
        def _(pe):
            for t in range(NT):
                r = rows_of(t)
                if t >= 2:
                    pe.wait_ge(sem("residual2"), t - 1)
                for k in range(KD):
                    last = pe.transpose(bank(2 * (t % 2), 2)[0:r, k * P:(k + 1) * P], f_t[:, k, t * P:t * P + r], ident)
                last.then_inc(sem("f_turned"), 1)

        @part("act")
        def _(act):
            for t in range(NT):
                r = rows_of(t)
                act.wait_ge(sem("ln2_variance"), t + 1)
                act.activation(deviation[0:r], mean_var[0:r, 1:2], ACT.Sqrt, bias=eps[0:r]).then_inc(sem("ln2_deviation"), 1)

        @part("dve")
        def _(dve):
            st = own_steps(dve, "dve")
            for t in range(NT):
                r = rows_of(t)
                dve.wait_ge(sem("f_turned"), t + 1)
                dve.scalar_tensor_tensor(x_nat[0:r, t, :], x_nat[0:r, t, :], ALPHA, bank(2 * (t % 2), 2)[0:r],
                                         ALU.mult, ALU.add).then_inc(sem("residual2"), 1)
                dve.wait_ge(sem("residual2"), t + 1)
                layer_norm(dve, st, x_nat[0:r, t, :], row_g2, row_b2, "ln2", r)(t + 1)

        @part("sp")
        def _(sp):
            for t in range(NT):
                sp.wait_ge(sem("ln2_done"), t + 1)
                to = y_rows[t] if t < 4 else y_sample.rearrange("b t d -> (b t) d")
                sp.dma_start(to, x_nat[0:rows_of(t), t, :]).then_inc(sem("y_out"), 16)
            sp.wait_ge(sem("y_out"), NT * 16)

        @part("sp")
        def _(sp):
            sp.wait_ge(sem("pages_in"), 16)
            sp.wait_ge(sem("window_moved"), 2 * 16)

        block = ctx.enter_context(nc.Block())

        def run(parts, eng):
            for p in parts:
                p(eng)

        @block.sync
        def _(eng):
            run(programs["sp"], eng)

        @block.tensor
        def _(eng):
            run(programs["pe"], eng)

        @block.scalar
        def _(eng):
            run(programs["act"], eng)

        @block.vector
        def _(eng):
            run(programs["dve"], eng)

        @block.gpsimd
        def _(eng):
            run(programs["pool"], eng)


_INS = ["x_prompt", "x_sample", "cache_k_sb", "cache_v_sb", "page_table", "state_k_win", "state_v_win",
        "w_in", "w_out", "sb_logit_bias", "ln1_g", "ln1_b", "peer_wq", "peer_subkeys", "peer_u", "peer_v",
        "ln2_g", "ln2_b"]
_OUTS = [(1, SEQ, D), (DB, DT, D), (1, SEQ // P, P, H, HD), (1, SEQ // P, P, H, HD), (DB, DT, H, HD),
         (DB, DT, H, HD), (1, SEQ, H, HD), (1, SEQ, H, HD), (DB, WIN, H, HD), (DB, WIN, H, HD)]


def kernel(**inputs):
    import numpy as _np
    import concourse.bacc as _bacc
    from concourse.bass_utils import run_bass_kernel_spmd as _run

    nc = _bacc.Bacc("TRN2", target_bir_lowering=False, num_devices=1)
    given = {name: _np.ascontiguousarray(inputs[name]) for name in _INS}
    given.update(constants())
    arrays, args = {}, []
    for name, a in given.items():
        arrays[f"in_{name}_dram"] = a
        args.append(nc.dram_tensor(f"in_{name}_dram", a.shape, mybir.dt.from_np(a.dtype), kind="ExternalInput").ap())
    for i, shape in enumerate(_OUTS):
        args.append(nc.dram_tensor(f"out_{i}_dram", shape, F32, kind="ExternalOutput").ap())
    build(nc, *args)
    r = _run(nc, [arrays], core_ids=[0])
    return tuple(r.results[0][f"out_{i}_dram"] for i in range(len(_OUTS)))
```

```python
from contextlib import ExitStack

import numpy as np

import concourse.bass as bass
from concourse import mybir

F32 = mybir.dt.float32
F32R = mybir.dt.float32r
I32 = mybir.dt.int32
U32 = mybir.dt.uint32
ALU = mybir.AluOpType
ACT = mybir.ActivationFunctionType
AX_X = mybir.AxisListType.X

P = 128
D = 1024
KD = D // P
SEQ = 512
DB, DT = 8, 4
NS = DB * DT
N = SEQ + NS
NT = 5
NP = NT * P
H, HD = 8, 64
DH = H * HD
NPAIR = H // 2
PAGES = 16
N_POOL = 160
PAST = PAGES * P
WIN = 2048
SPAN = 128
DILS = (1, 4, 16)
TK = 16
NK = 128
PH = 8
HALF = N // 2
SCALE = HD ** -0.5
ALPHA = 2.0 ** 0.25
EPS = 1e-5
NEG = -1e30
LOWEST = -3.0e38
BANK = 512
CHUNK = 32
NCHUNK = N // CHUNK
GI = 2
NG = NK // GI
NEAR = 4
FAR = 3
NW = NEAR + FAR
K_SLOTS = 8
ALL_COLUMNS = 50176
KEPT = 2 * NT * D + 5 * P + 384
ATTENTION = 2 * NT * DH + 2 * (H + NPAIR) * NS + NPAIR * DB * NS
SAMPLE_R = 5 * 2 * DH + 2 * (PAGES + 1) * H * DT
H1_R = 2 * KD * NP
PARTS = ((0, 0), (0, 1), (1, 0))
EXPERT_R = 2 * (GI * D + 2 * GI * D + 2 * GI * N)
WQ_R = 2 * 2 * KD * 2 * P


def constants():
    r = np.arange(P)
    ident = np.eye(P, dtype=np.float32)
    tri = (r[:, None] >= r[None, :]).astype(np.float32)
    ones = np.ones((P, P), np.float32)
    diag = np.where(r[None, :] > r[:, None], 0.0, NEG)
    iota = np.broadcast_to(r, (P, P))
    square = np.concatenate([ident, tri, ones, diag, iota], axis=1).astype(np.float32)

    def log_count(dist):
        count = ((dist >= 0) & (dist <= SPAN)).astype(np.int64)
        for dil in DILS[1:]:
            count = count + ((dist >= 0) & (dist % dil == 0) & (dist <= SPAN * dil))
        return np.where(count > 0, np.log(np.maximum(count, 1)) / SCALE, NEG)

    q = np.arange(SEQ)
    prompt = log_count(q[:, None] - q[None, :]).reshape(NT - 1, P, SEQ).transpose(1, 0, 2)
    near = WIN - NEAR * P + np.arange(NEAR * P)
    g = np.arange(FAR * P)
    far = 16 * (g // 4) + g % 4
    t = np.arange(DT)
    rows = WIN + np.tile(t, H)
    window = log_count(rows[:, None] - np.concatenate([near, far])[None, :])
    s = np.arange(NS)
    fresh = log_count(rows[:, None, None] - (WIN + s % DT)[None, None, :])
    own = (s // DT)[None, None, :] == np.arange(DB)[None, :, None]
    fresh = np.where(own, np.broadcast_to(fresh, (NS, DB, NS)), NEG)
    new = np.where((s[:, None] // DT == np.arange(DB)[None, :])[:, :, None]
                   & ((s % DT)[:, None, None] < np.tile(t, H)[None, None, :]), 0.0, NEG)
    pos = np.zeros((NT, P), np.float32)
    pos[:4] = np.arange(SEQ).reshape(4, P)
    pos[4, :NS] = PAST + s % DT
    inv = np.float32(10000.0) ** (-np.arange(HD // 2, dtype=np.float32) / np.float32(HD // 2))
    ang = (pos[:, :, None] * inv[None, None, :]).astype(np.float32).transpose(1, 0, 2)
    f = lambda a: np.ascontiguousarray(a.astype(np.float32))
    return {
        "square": f(square),
        "count_prompt": f(prompt.reshape(P, -1)),
        "count_window": f(window),
        "count_fresh": f(fresh.reshape(NS, -1)),
        "mask_new": f(new.reshape(NS, -1)),
        "cosine": f(np.cos(ang).reshape(P, -1)),
        "sine": f(np.sin(ang).reshape(P, -1)),
    }


class Steps:

    def __init__(self, eng, sem):
        self.eng, self.sem, self.base, self.n = eng, sem, 0, 0

    def do(self, ins):
        ins.then_inc(self.sem, 1)
        self.n += 1

    def wait(self, back=0):
        self.eng.wait_ge(self.sem, self.base + (self.n - back))

    def link(self, ins):
        self.do(ins)
        self.wait()

    def enter(self, i, per_turn):
        self.start, self.per_turn = self.n, per_turn
        self.base = i * per_turn

    def leave(self, turns):
        assert self.n - self.start == self.per_turn, (self.n - self.start, self.per_turn)
        self.base, self.n = 0, self.start + turns * self.per_turn


def build(nc, x_prompt, x_sample, cache_k_sb, cache_v_sb, page_table, state_k_win, state_v_win,
          w_in, w_out, sb_logit_bias, ln1_g, ln1_b, peer_wq, peer_subkeys, peer_u, peer_v, ln2_g, ln2_b,
          square, count_prompt, count_window, count_fresh, mask_new, cosine, sine,
          y_prompt, y_sample, k_sb_prompt, v_sb_prompt, k_sb_sample, v_sb_sample,
          k_win_prompt, v_win_prompt, k_win_sample, v_win_sample):
    with ExitStack() as ctx:
        kept = ctx.enter_context(nc.sbuf_tensor("kept", [P, KEPT], F32))
        pages_sb = ctx.enter_context(nc.sbuf_tensor("pages_sb", [1, DB * PAGES], I32))
        psum = ctx.enter_context(nc.psum_tensor("psum", [P, 8 * BANK], F32))
        gates_dram = nc.dram_tensor("gates_dram", [NCHUNK, P, NK * CHUNK], F32).ap()

        made = {}

        def sem(name):
            if name not in made:
                made[name] = ctx.enter_context(nc.semaphore(name))
            return made[name]

        place, era, era_tensor = [0], ExitStack(), [None]

        def take_in(stack, name, cols):
            era_tensor[0] = stack.enter_context(nc.sbuf_tensor(name, [P, cols], F32)), cols, place[0]

        def open_era(name, cols):
            era.close()
            place[0] = KEPT
            take_in(era, name, cols)

        def take(cols, at=None):
            if at is not None:
                place[0] = at
            o = place[0]
            place[0] = o + cols
            if place[0] <= KEPT:
                return kept[:, o:o + cols]
            tensor, size, base = era_tensor[0]
            assert o >= base and place[0] <= base + size, (o, place[0], base, size)
            return tensor[:, o - base:o - base + cols]

        def bank(b, n=1):
            return psum[:, b * BANK:(b + n) * BANK]

        x_nat = take(NT * D).rearrange("p (t d) -> p t d", t=NT)
        sq = take(5 * P)
        ident, tri, ones, diag, iota = (sq[:, i * P:(i + 1) * P] for i in range(5))
        small = take(384)
        o_t = take(KD * NP).rearrange("p (c n) -> p c n", c=KD)
        ERA = place[0]
        assert ERA == KEPT
        open_era("attention", ATTENTION)
        v_n = {k: take(NT * DH).rearrange("p (t d) -> p t d", t=NT) for k in ("sb", "dil")}
        q_s = {k: take(H * NS).rearrange("p (h s) -> p h s", h=H) for k in ("sb", "dil")}
        k_s = {k: take(NPAIR * NS).rearrange("p (c s) -> p c s", c=NPAIR) for k in ("sb", "dil")}
        q_wide = take(NPAIR * DB * NS).rearrange("p (c b n) -> p c b n", c=NPAIR, b=DB)
        SAMPLE = place[0]
        assert SAMPLE == KEPT + ATTENTION
        work_era = ExitStack()
        take_in(work_era, "prompt", ALL_COLUMNS - SAMPLE)
        q_z = {k: take(H * N).rearrange("p (h n) -> p h n", h=H) for k in ("sb", "dil")}
        k_t = {k: take(NPAIR * N).rearrange("p (c n) -> p c n", c=NPAIR) for k in ("sb", "dil")}
        WORK = place[0]

        over = sem("stage_over")
        stage = {}

        def end_stage(eng):
            name = eng.engine
            stage[name] = stage.get(name, 0) + 1
            eng.drain().then_inc(over, 1)
            eng.wait_ge(over, 5 * stage[name])

        programs = {"sp": [], "pe": [], "act": [], "dve": [], "pool": []}

        def part(engine):
            return programs[engine].append
        steps = {}

        def own_steps(eng, name):
            if name not in steps:
                steps[name] = Steps(eng, sem(f"{name}_step"))
            return steps[name]

        x_t = take(KD * N, WORK).rearrange("p (k n) -> p k n", k=KD)
        w_g = [take(KD * DH).rearrange("p (k c) -> p k c", k=KD) for _ in range(2)]
        staged = [take(NT * DH).rearrange("p (t c) -> p t c", t=NT) for _ in range(2)]
        rope_a = take(NT * H * 32, ERA - KD * NP)
        rope_b = take(NT * H * 32)
        cos_sb, sin_sb = take(NT * 32), take(NT * 32)
        GROUPS = ("q_sb", "k_sb", "q_dil", "k_dil", "v_sb", "v_dil")
        COLUMN = {"q_sb": 0, "k_sb": 1, "v_sb": 2, "q_dil": 3, "k_dil": 4, "v_dil": 5}
        x_rows = x_prompt.rearrange("b (t p) d -> p (b t) d", p=P)
        xs_rows = x_sample.rearrange("b t d -> (b t) d")
        w_in_g = w_in.rearrange("(k p) (g c) -> g p k c", p=P, c=DH)

        def rows_of(t):
            return P if t < NT - 1 else NS

        def proj_out(c, t):
            kind = GROUPS[c].split("_")[1]
            to = v_n[kind] if GROUPS[c][0] == "v" else staged[c % 2]
            return to[0:rows_of(t), t, :]

        @part("sp")
        def _(sp):
            sp.dma_start(x_nat[:, 0:4, :], x_rows).then_inc(sem("x_prompt_in"), 16)
            sp.wait_ge(sem("tail_cleared"), 1)
            sp.dma_start(x_nat[0:NS, 4, :], xs_rows).then_inc(sem("x_sample_in"), 16)
            sp.dma_start(sq, square).then_inc(sem("square_in"), 16)
            sp.dma_start(cos_sb, cosine).then_inc(sem("angles_in"), 16)
            sp.dma_start(sin_sb, sine).then_inc(sem("angles_in"), 16)
            sp.dma_start(pages_sb[:, :], page_table.rearrange("b j -> (b j)").rearrange("(o n) -> o n", o=1))\
              .then_inc(sem("pages_in"), 16)
            for c in range(len(GROUPS)):
                if c >= 2:
                    sp.wait_ge(sem("proj_ready"), 5 * (c - 1))
                sp.dma_start(w_g[c % 2], w_in_g[COLUMN[GROUPS[c]]]).then_inc(sem(f"w_in_{c % 2}"), 16)

        @part("pool")
        def _(pool):
            def rows_out(tile, prompt, sample, name, ready, value):
                pool.wait_ge(sem(ready), value)
                pool.dma_start(prompt, tile[:, 0:4, :]).then_inc(sem(f"{name}_out"), 16)
                if name in ("k_sb", "v_sb"):
                    pool.dma_start(sample, tile[0:NS, 4, :]).then_inc(sem(f"{name}_out"), 16)
                else:
                    for b in range(DB):
                        pool.dma_start(sample[b], tile[b * DT:(b + 1) * DT, 4, :])\
                            .then_inc(sem(f"{name}_out"), 16)

            flat = "b (t p) h d -> p (b t) (h d)"
            pages = "b t p h d -> p (b t) (h d)"
            rows_out(staged[1], k_sb_prompt.rearrange(pages), k_sb_sample.rearrange("b t h d -> (b t) (h d)"),
                     "k_sb", "proj_copied", 5 * 2)
            rows_out(staged[1], k_win_prompt.rearrange(flat, p=P),
                     k_win_sample.rearrange("b w h d -> b w (h d)")[:, WIN - DT:WIN, :], "k_dil", "roped", 2)
            rows_out(v_n["sb"], v_sb_prompt.rearrange(pages), v_sb_sample.rearrange("b t h d -> (b t) (h d)"),
                     "v_sb", "proj_copied", 5 * 5)
            rows_out(v_n["dil"], v_win_prompt.rearrange(flat, p=P),
                     v_win_sample.rearrange("b w h d -> b w (h d)")[:, WIN - DT:WIN, :], "v_dil", "proj_copied", 5 * 6)
            pool.wait_ge(sem("k_sb_out"), 2 * 16)
            pool.wait_ge(sem("k_dil_out"), (1 + DB) * 16)

        @part("pe")
        def _(pe):
            pe.wait_ge(sem("square_in"), 16)
            for t in range(NT):
                pe.wait_ge(sem("x_prompt_in" if t < 4 else "x_sample_in"), 16)
                r = rows_of(t)
                for half in range(2):
                    u = 2 * t + half
                    if u >= 4:
                        pe.wait_ge(sem("x_t_copied"), u - 3)
                    for k in range(4):
                        last = pe.transpose(bank(u % 4)[:, k * P:k * P + r],
                                            x_nat[0:r, t, (4 * half + k) * P:(4 * half + k + 1) * P],
                                            ident[0:r, 0:r])
                    last.then_inc(sem("x_t_ready"), 1)
            pe.wait_ge(sem("x_t_copied"), 10)

            def turn(c):
                if c < 2:
                    pe.wait_ge(sem("proj_copied"), 5 * c + 5)
                else:
                    pe.wait_ge(sem("roped"), c - 1)
                for t in range(NT):
                    v = 5 * c + t
                    if v >= 4:
                        pe.wait_ge(sem("qk_copied_dve"), v - 3)
                        if (v - 4) // 5 % 2 == 0:
                            pe.wait_ge(sem("q_copied_act"), 5 * ((v - 4) // 10) + (v - 4) % 5 + 1)
                    r = rows_of(t)
                    for pair in range(NPAIR):
                        last = pe.transpose(bank(4 + v % 4)[:, pair * P:pair * P + r],
                                            staged[c % 2][0:r, t, pair * P:(pair + 1) * P], ident[0:r, 0:r])
                    last.then_inc(sem("qk_ready"), 1)

            for c in range(len(GROUPS)):
                pe.wait_ge(sem(f"w_in_{c % 2}"), 16 * (c // 2 + 1))
                for t in range(NT):
                    u = 5 * c + t
                    if u >= 4:
                        pe.wait_ge(sem("proj_copied"), u - 3)
                    r = rows_of(t)
                    for k in range(KD):
                        last = pe.matmul(bank(u % 4)[0:r, :], lhsT=x_t[:, k, t * P:t * P + r], rhs=w_g[c % 2][:, k, :],
                                         start=(k == 0), stop=(k == KD - 1))
                    last.then_inc(sem("proj_ready"), 1)
                if 1 <= c <= 4:
                    turn(c - 1)

        @part("act")
        def _(act):
            for t in range(NT):
                r = rows_of(t)
                for half in range(2):
                    u = 2 * t + half
                    act.wait_ge(sem("x_t_ready"), u + 1)
                    act.activation(x_t[:, 4 * half:4 * half + 4, t * P:t * P + r],
                                   bank(u % 4).rearrange("p (k n) -> p k n", k=4)[:, :, 0:r], ACT.Copy)\
                        .then_inc(sem("x_t_copied"), 1)
            act.wait_ge(sem("staged_cleared"), 8)

            def q_copy(c):
                kind = GROUPS[c].split("_")[1]
                for t in range(NT):
                    v = 5 * c + t
                    act.wait_ge(sem("qk_ready"), v + 1)
                    r = rows_of(t)
                    src = bank(4 + v % 4).rearrange("p (c n) -> p c n", c=NPAIR)[0:64, :, 0:r]
                    act.activation(q_z[kind].rearrange("p (c e) n -> p c e n", e=2)[0:64, :, 0, t * P:t * P + r],
                                   src, ACT.Copy).then_inc(sem("q_copied_act"), 1)

            for c in range(len(GROUPS)):
                for t in range(NT):
                    act.wait_ge(sem("proj_ready"), 5 * c + t + 1)
                    if c in (2, 3) and t == 0:
                        act.wait_ge(sem("qk_ready"), 5 * (c - 1))
                        if c == 3:
                            act.wait_ge(sem("k_sb_out"), 2 * 16)
                    act.activation(proj_out(c, t), bank((5 * c + t) % 4)[0:rows_of(t), :], ACT.Copy)\
                        .then_inc(sem("proj_copied"), 1)
                if c in (1, 3):
                    q_copy(c - 1)

        @part("dve")
        def _(dve):
            dve.memset(x_nat[:, 4, :], 0.0).then_inc(sem("tail_cleared"), 1)
            for i in range(2):
                dve.memset(staged[i][:, 4, :], 0.0).then_inc(sem("staged_cleared"), 1)
            for kind in ("sb", "dil"):
                dve.memset(v_n[kind][:, 4, :], 0.0).then_inc(sem("staged_cleared"), 1)
            for kind in ("sb", "dil"):
                halves = q_z[kind].rearrange("p (c e) n -> p c e n", e=2)
                dve.memset(halves[64:128, :, 0, :], 0.0).then_inc(sem("staged_cleared"), 1)
                dve.memset(halves[0:64, :, 1, :], 0.0).then_inc(sem("staged_cleared"), 1)

            def qk_copy(c):
                kind = GROUPS[c].split("_")[1]
                for t in range(NT):
                    v = 5 * c + t
                    dve.wait_ge(sem("qk_ready"), v + 1)
                    r = rows_of(t)
                    src = bank(4 + v % 4).rearrange("p (c n) -> p c n", c=NPAIR)[:, :, 0:r]
                    if GROUPS[c][0] == "k":
                        dve.tensor_copy(k_t[kind][:, :, t * P:t * P + r], src).then_inc(sem("qk_copied_dve"), 1)
                    else:
                        to = q_z[kind].rearrange("p (c e) n -> p c e n", e=2)
                        dve.tensor_copy(to[64:128, :, 1, t * P:t * P + r], src[64:128]).then_inc(sem("qk_copied_dve"), 1)

            st = own_steps(dve, "dve")

            def rope(c):
                dve.wait_ge(sem("proj_copied"), 5 * c + 5)
                x = staged[c % 2].rearrange("p t (h e d) -> p t h e d", e=2, d=32)
                x1, x2 = x[:, :, :, 0, :], x[:, :, :, 1, :]
                ta, tb = (a.rearrange("p (t h d) -> p t h d", t=NT, h=H) for a in (rope_a, rope_b))
                cos, sin = (a.rearrange("p (t o d) -> p t o d", t=NT, o=1).to_broadcast([P, NT, H, 32])
                            for a in (cos_sb, sin_sb))
                st.do(dve.tensor_tensor(ta, x1, cos, ALU.mult))
                st.link(dve.tensor_tensor(tb, x2, sin, ALU.mult))
                st.do(dve.tensor_tensor(rope_a, rope_a, rope_b, ALU.subtract))
                st.link(dve.tensor_tensor(x1, x1, sin, ALU.mult))
                st.link(dve.tensor_tensor(tb, x2, cos, ALU.mult))
                st.link(dve.tensor_tensor(x2, x1, tb, ALU.add))
                dve.tensor_copy(x1, ta).then_inc(sem("roped"), 1)

            dve.wait_ge(sem("angles_in"), 2 * 16)
            qk_copy(0)
            qk_copy(1)
            rope(2)
            qk_copy(2)
            rope(3)
            qk_copy(3)
            dve.wait_ge(sem("q_copied_act"), 10)
            dve.wait_ge(sem("qk_copied_dve"), 20)
            for kind in ("sb", "dil"):
                dve.tensor_copy(q_s[kind], q_z[kind][:, :, SEQ:N]).then_inc(sem("sample_apart"), 1)
                dve.tensor_copy(k_s[kind], k_t[kind][:, :, SEQ:N]).then_inc(sem("sample_apart"), 1)
            st.link(dve.memset(q_wide, 0.0))
            dve.wait_ge(sem("sample_apart"), 4)
            for pair in range(NPAIR):
                for e in range(2):
                    h = 2 * pair + e
                    dve.tensor_copy(q_wide[:, pair, :, h * DT:(h + 1) * DT],
                                    q_s["dil"][:, h, :].rearrange("p (b t) -> p b t", t=DT))
        for engine in programs:
            programs[engine].append(end_stage)

        KB = SEQ // P
        AT = (0, 512, 1024, 896)
        WIDE = 1280
        place[0] = WORK
        sb_z = [take(WIDE) for _ in range(2)]
        sb_e = [take(WIDE) for _ in range(2)]
        sb_p = [take(WIDE) for _ in range(2)]
        o_nat = take(4 * D).rearrange("p (t d) -> p t d", t=4)
        counts = take(4 * SEQ).rearrange("p (t k) -> p t k", t=4)
        bias = small[:, 0:8]
        bias_ht = small[:, 8:40].rearrange("p (h t) -> p h t", h=H)

        def region(kb):
            return slice(AT[kb], AT[kb] + SEQ - kb * P)

        @part("sp")
        def _(sp):
            sp.dma_start(bias, sb_logit_bias.rearrange("(o h) -> o h", o=1).to_broadcast([P, H]))\
              .then_inc(sem("counts_in"), 16)
            sp.dma_start(counts, count_prompt.rearrange("p (t k) -> p t k", t=4)).then_inc(sem("counts_in"), 16)

        @part("pool")
        def _(pool):
            pool.wait_ge(sem("v_sb_out"), 2 * 16)
            pool.wait_ge(sem("v_dil_out"), (1 + DB) * 16)

        @part("pe")
        def _(pe):
            def scores(h):
                if h >= 1:
                    pe.wait_ge(sem("sb_logits"), h)
                for kb in range(KB):
                    r = region(kb)
                    pe.matmul(psum[:, r], lhsT=k_t["sb"][:, h // 2, kb * P:(kb + 1) * P],
                              rhs=q_z["sb"][:, h, kb * P:SEQ], start=True, stop=False)
                    last = pe.matmul(psum[:, r.start:r.start + P], lhsT=ident, rhs=diag, start=False, stop=True)
                last.then_inc(sem("sb_scores"), 1)

            scores(0)
            for h in range(H):
                if h + 1 < H:
                    scores(h + 1)
                pe.wait_ge(sem("sb_softplus"), h + 1)
                if h >= 1:
                    pe.wait_ge(sem("sb_exponents"), h)
                sp_h = sb_p[h % 2]
                for kb in range(KB):
                    r = region(kb)
                    last = pe.matmul(bank(3, 3)[:, r], lhsT=tri, rhs=sp_h[:, r], start=True, stop=(kb == KB - 1))
                    for later in range(kb + 1, KB):
                        a = r.start + (later - kb) * P
                        last = pe.matmul(bank(3, 3)[:, a:r.stop], lhsT=ones, rhs=sp_h[:, region(later)],
                                         start=False, stop=(later == KB - 1))
                last.then_inc(sem("sb_sums"), 1)
                pe.wait_ge(sem("sb_weights"), h + 1)
                if h >= 2:
                    pe.wait_ge(sem("sb_out_copied"), h - 1)
                out = bank(6 + h % 2)
                for qb in range(KB):
                    for kb in range(qb + 1):
                        a = AT[kb] + (qb - kb) * P
                        last = pe.matmul(out[:, qb * HD:(qb + 1) * HD], lhsT=sb_z[h % 2][:, a:a + P],
                                         rhs=v_n["sb"][:, kb, h * HD:(h + 1) * HD], start=(kb == 0), stop=(kb == qb))
                last.then_inc(sem("sb_out"), 1)

        @part("act")
        def _(act):
            st = own_steps(act, "act")

            def log_part(h):
                e = sb_e[h % 2]
                act.wait_ge(sem("sb_logits"), h + 1)
                if h >= 2:
                    act.wait_ge(sem("sb_softplus"), h - 1)
                st.link(act.activation(e, sb_z[h % 2], ACT.Abs))
                st.link(act.activation(e, e, ACT.Exp, scale=-1.0))
                act.activation(e, e, ACT.Ln, bias=1.0).then_inc(sem("sb_log"), 1)

            log_part(0)
            for h in range(H):
                if h + 1 < H:
                    log_part(h + 1)
                act.wait_ge(sem("sb_exponents"), h + 1)
                act.activation(sb_z[h % 2], sb_z[h % 2], ACT.Exp).then_inc(sem("sb_weights"), 1)
                act.wait_ge(sem("sb_out"), h + 1)
                act.activation(o_nat[:, :, h * HD:(h + 1) * HD],
                               bank(6 + h % 2)[:, 0:KB * HD].rearrange("p (t d) -> p t d", t=KB), ACT.Copy)\
                    .then_inc(sem("sb_out_copied"), 1)

        @part("dve")
        def _(dve):
            dve.wait_ge(sem("counts_in"), 2 * 16)

            def logits(h):
                dve.wait_ge(sem("sb_scores"), h + 1)
                if h >= 2:
                    dve.wait_ge(sem("sb_out"), h - 1)
                dve.tensor_scalar(sb_z[h % 2], psum[:, 0:WIDE], SCALE, bias[:, h:h + 1], ALU.mult, ALU.add)\
                    .then_inc(sem("sb_logits"), 1)

            def softplus(h):
                dve.wait_ge(sem("sb_log"), h + 1)
                dve.wait_ge(sem("sb_logits"), h + 1)
                if h >= 2:
                    dve.wait_ge(sem("sb_sums"), h - 1)
                dve.scalar_tensor_tensor(sb_p[h % 2], sb_z[h % 2], 0.0, sb_e[h % 2], ALU.max, ALU.add)\
                    .then_inc(sem("sb_softplus"), 1)

            logits(0)
            softplus(0)
            for h in range(H):
                if h + 1 < H:
                    logits(h + 1)
                dve.wait_ge(sem("sb_sums"), h + 1)
                dve.tensor_tensor(sb_z[h % 2], sb_z[h % 2], bank(3, 3)[:, 0:WIDE], ALU.subtract)\
                    .then_inc(sem("sb_exponents"), 1)
                if h + 1 < H:
                    softplus(h + 1)

        for engine in programs:
            programs[engine].append(end_stage)

        PT_AT = (0, 1, 3, 6)
        dl_p = [take(WIDE, WORK)] + [take(WIDE)]
        dl_t = [take(WIDE) for _ in range(2)]
        dl_max, dl_neg, dl_sum, dl_inv = ([small[:, 64 + 16 * i + 4 * e:68 + 16 * i + 4 * e] for e in range(2)]
                                          for i in range(4))
        assert place[0] <= WORK + 6 * WIDE

        @part("pe")
        def _(pe):
            def scores(h):
                if h >= 1:
                    pe.wait_ge(sem("dl_logits"), 4 * h)
                for qb in range(KB):
                    last = pe.matmul(bank(qb)[:, 0:(qb + 1) * P], lhsT=q_z["dil"][:, h, qb * P:(qb + 1) * P],
                                     rhs=k_t["dil"][:, h // 2, 0:(qb + 1) * P], start=True, stop=True)
                last.then_inc(sem("dl_scores"), 1)

            scores(0)
            for h in range(H):
                if h + 1 < H:
                    scores(h + 1)
                pe.wait_ge(sem("dl_exp"), 4 * h + 4)
                if h >= 1:
                    pe.wait_ge(sem("dl_turned"), h)
                for j in range(10):
                    last = pe.transpose(bank(4, 3)[:, j * P:(j + 1) * P], dl_p[h % 2][:, j * P:(j + 1) * P], ident)
                last.then_inc(sem("dl_turn"), 1)
                pe.wait_ge(sem("dl_turned"), h + 1)
                if h >= 1:
                    pe.wait_ge(sem("dl_out_scaled"), h)
                for qb in range(KB):
                    for kb in range(qb + 1):
                        a = (PT_AT[qb] + kb) * P
                        c = qb * HD
                        last = pe.matmul(bank(7)[:, c:c + HD], lhsT=dl_t[h % 2][:, a:a + P],
                                         rhs=v_n["dil"][:, kb, h * HD:(h + 1) * HD], start=(kb == 0), stop=(kb == qb))
                last.then_inc(sem("dl_out"), 1)

        @part("act")
        def _(act):
            def exps(h):
                act.wait_ge(sem("dl_neg"), h + 1)
                for qb in range(KB):
                    a = PT_AT[qb] * P
                    x = dl_p[h % 2][:, a:a + (qb + 1) * P]
                    act.activation(x, x, ACT.Exp, bias=dl_neg[h % 2][:, qb:qb + 1],
                                   accum_out=dl_sum[h % 2][:, qb:qb + 1]).then_inc(sem("dl_exp"), 1)

            exps(0)
            for h in range(H):
                if h + 1 < H:
                    exps(h + 1)
                act.wait_ge(sem("dl_turn"), h + 1)
                if h >= 2:
                    act.wait_ge(sem("dl_out"), h - 1)
                act.activation(dl_t[h % 2], bank(4, 3)[:, 0:WIDE], ACT.Copy).then_inc(sem("dl_turned"), 1)

        @part("dve")
        def _(dve):
            dve.wait_ge(sem("counts_in"), 2 * 16)

            def logits(h):
                dve.wait_ge(sem("dl_scores"), h + 1)
                if h >= 2:
                    dve.wait_ge(sem("dl_turn"), h - 1)
                for qb in range(KB):
                    a, w = PT_AT[qb] * P, (qb + 1) * P
                    dve.tensor_tensor_reduce(out=dl_p[h % 2][:, a:a + w], in0=bank(qb)[:, 0:w], in1=counts[:, qb, 0:w],
                                             scale=SCALE, scalar=LOWEST, op0=ALU.add, op1=ALU.max,
                                             accum_out=dl_max[h % 2][:, qb:qb + 1]).then_inc(sem("dl_logits"), 1)
                dve.wait_ge(sem("dl_logits"), 4 * h + 4)
                dve.tensor_scalar(dl_neg[h % 2], dl_max[h % 2], -1.0, None, ALU.mult).then_inc(sem("dl_neg"), 1)

            logits(0)
            for h in range(H):
                if h + 1 < H:
                    logits(h + 1)
                dve.wait_ge(sem("dl_exp"), 4 * h + 4)
                dve.reciprocal(dl_inv[h % 2], dl_sum[h % 2]).then_inc(sem("dl_inverse"), 1)
                dve.wait_ge(sem("dl_inverse"), h + 1)
                dve.wait_ge(sem("dl_out"), h + 1)
                dve.tensor_tensor(o_nat[:, :, DH + h * HD:DH + (h + 1) * HD],
                                  bank(7)[:, 0:KB * HD].rearrange("p (t d) -> p t d", t=KB),
                                  dl_inv[h % 2].rearrange("p (t o) -> p t o", o=1).to_broadcast([P, KB, HD]), ALU.mult)\
                    .then_inc(sem("dl_out_scaled"), 1)

        @part("pe")
        def _(pe):
            pe.wait_ge(sem("dl_out_scaled"), H)
            for t in range(4):
                for half in range(2):
                    u = 2 * t + half
                    if u >= 4:
                        pe.wait_ge(sem("o_t_copied"), u - 3)
                    for c in range(4):
                        last = pe.transpose(bank(u % 4)[:, c * P:(c + 1) * P],
                                            o_nat[:, t, (4 * half + c) * P:(4 * half + c + 1) * P], ident)
                    last.then_inc(sem("o_t_ready"), 1)

        @part("act")
        def _(act):
            for u in range(8):
                t, half = u // 2, u % 2
                act.wait_ge(sem("o_t_ready"), u + 1)
                act.activation(o_t[:, 4 * half:4 * half + 4, t * P:(t + 1) * P],
                               bank(u % 4).rearrange("p (c n) -> p c n", c=4), ACT.Copy).then_inc(sem("o_t_copied"), 1)

        for engine in programs:
            programs[engine].append(end_stage)

        HT = H * DT
        SW = PAGES * HT
        SUMS_AT, EXP_AT, PV_AT = 5, 6, 8
        V_SLOTS, V_PARTS = 4, 4
        work_era.close()
        take_in(work_era, "sample", ALL_COLUMNS - SAMPLE - SAMPLE_R)
        parts_tensor = work_era.enter_context(nc.sbuf_tensor("sample_parts", [P, SAMPLE_R], F32R))
        at_r = [0]

        def take_s(cols):
            at_r[0] += cols
            return parts_tensor[:, at_r[0] - cols:at_r[0]]

        k_page = [take(DH) for _ in range(K_SLOTS)]
        v_page = [take(DH) for _ in range(V_SLOTS)]
        ss_e, ss_p, ss_c = (take(SW) for _ in range(3))
        ss_z = take(SW + HT)
        new_z, new_e, new_p = (take(DB * HT) for _ in range(3))
        mask_sb = take(DB * HT)
        k_turned = [take(DH).rearrange("p (c n) -> p c n", c=NPAIR) for _ in range(2)]
        pv_rows = take(DH)
        PV_N = 2 * HT + 8
        pv_cols = take(NPAIR * PV_N)
        v_parts = [take_s(2 * DH).rearrange("p (x c) -> p x c", x=2) for _ in range(V_PARTS)]
        v_new_r = take_s(2 * DH).rearrange("p (x c) -> p x c", x=2)
        w_r = take_s(2 * (SW + HT)).rearrange("p (j x n) -> p j x n", j=PAGES + 1, x=2)
        z_pages = ss_z.rearrange("p (j n) -> p j n", j=PAGES + 1)
        cache_k = cache_k_sb.rearrange("g p h d -> g p (h d)")
        cache_v = cache_v_sb.rearrange("g p h d -> g p (h d)")

        def by_b(a):
            return a.rearrange("p (b n) -> p b n", b=DB)

        def over_sequences(eng, turn, st=None, per_turn=0):
            turn(0, True, False)
            with eng.Fori(0, DB - 1) as i:
                if st:
                    st.enter(i, per_turn)
                turn(i + 1, True, True)
                if st:
                    st.leave(DB - 1)
            turn(DB, False, True)

        def values_at(step):
            return range(2 * (step - PV_AT), 2 * (step - PV_AT) + 2) if PV_AT <= step < PAGES else ()

        @part("sp")
        def _(sp):
            sp.dma_start(mask_sb[0:NS, :], mask_new).then_inc(sem("mask_in"), 16)

            def load(b, j, cache, to, free, name):
                g = PAGES * b + j
                page = sp.value_load(pages_sb[0:1, bass.ds(g, 1)], min_val=0, max_val=N_POOL - 1)
                sp.wait_ge(sem(free), g + 1)
                sp.dma_start(to[j % len(to)], cache[bass.ds(page, 1)].rearrange("o p c -> (o p) c"))\
                    .then_inc(sem(f"{name}_{j % len(to)}"), 16)

            def keys(b, j):
                load(b, j, cache_k, k_page, "page_turned", "k_page")

            def values(b, j):
                load(b, j, cache_v, v_page, "page_v_low", "v_page")

            def turn(b, pages, before):
                for s in range(PAGES):
                    if s < PAGES - K_SLOTS and pages:
                        keys(b, K_SLOTS + s)
                    if s >= PAGES - K_SLOTS and pages and not (isinstance(b, int) and b == DB - 1):
                        keys(b + 1, s - (PAGES - K_SLOTS))
                    if before:
                        for j in range(V_SLOTS) if s == 0 else values_at(s + 1):
                            v = j if s == 0 else j + V_SLOTS
                            if v < PAGES:
                                values(b - 1, v)

            for j in range(K_SLOTS):
                keys(0, j)
            turn(0, True, False)
            with sp.Fori(0, DB - 2) as i:
                turn(i + 1, True, True)
            turn(DB - 1, True, True)
            turn(DB, False, True)

        @part("pe")
        def _(pe):
            pe.drain().then_inc(sem("page_turned"), K_SLOTS)
            pe.drain().then_inc(sem("page_scored"), 2)
            pe.drain().then_inc(sem("values_used"), V_PARTS)
            pe.drain().then_inc(sem("seq_out"), 1)
            out = by_b(bank(6)[0:NS, 0:DB * HT])
            for pair in range(NPAIR):
                last = pe.matmul(out[:, :, pair * 8:(pair + 1) * 8].rearrange("p b (e t) -> p b e t", e=2),
                                 lhsT=k_s["sb"][:, pair, :],
                                 rhs=q_s["sb"][:, 2 * pair:2 * pair + 2, :].rearrange("p e (b t) -> p b e t", t=DT),
                                 start=True, stop=True)
            last.then_inc(sem("new_scores"), 1)
            pe.wait_ge(sem("new_softplus"), 1)
            pe.matmul(bank(7)[:, 0:DB * HT], lhsT=tri, rhs=new_p, start=True, stop=True).then_inc(sem("new_sums"), 1)

            def turn_page(b, j):
                pe.wait_ge(sem(f"k_page_{j % K_SLOTS}"), 32 * b + 16 * (j // K_SLOTS) + 16)
                pe.wait_ge(sem("page_copied"), PAGES * b + j + 1)
                for pair in range(NPAIR):
                    last = pe.transpose(bank(j % 2)[:, pair * P:(pair + 1) * P],
                                        k_page[j % K_SLOTS][:, pair * P:(pair + 1) * P], ident)
                last.then_inc(sem("page_turned"), 1)

            def score(b, j):
                if j == 0:
                    pe.wait_ge(sem("seq_logits"), 2 * b + 1)
                pe.wait_ge(sem("page_copied"), PAGES * b + j + 3)
                for pair in range(NPAIR):
                    c = j * HT + pair * 8
                    last = pe.matmul(bank(2)[:, c:c + 8].rearrange("p (e t) -> p e t", e=2), lhsT=k_turned[j % 2][:, pair, :],
                                     rhs=q_s["sb"][:, 2 * pair:2 * pair + 2, bass.ds(b * DT, DT)], start=True, stop=True)
                last.then_inc(sem("page_scored"), 1)

            def sums(b):
                pe.wait_ge(sem("seq_suffix"), b + 1)
                pe.matmul(bank(4), lhsT=tri, rhs=ss_p, start=True, stop=False)
                pe.matmul(bank(4)[:, 0:SW - HT], lhsT=ones, rhs=ss_c[:, HT:SW], start=False, stop=False)
                pe.matmul(bank(4).rearrange("p (j n) -> p j n", j=PAGES), lhsT=ones,
                          rhs=by_b(new_p)[:, bass.ds(b, 1), :].to_broadcast([P, PAGES, HT]),
                          start=False, stop=True).then_inc(sem("seq_sums"), 1)

            def weigh(b, j):
                if j == 0:
                    pe.wait_ge(sem("weights_low"), b + 1)
                    pe.wait_ge(sem("seq_rows"), b + 1)
                if j < PAGES:
                    pe.wait_ge(sem("page_v_low"), PAGES * b + j + V_SLOTS + 1)
                else:
                    pe.wait_ge(sem("new_v_low"), 1)
                v = v_parts[j % V_PARTS] if j < PAGES else v_new_r
                for x in range(2):
                    last = pe.matmul(bank(5)[0:2 * HT, :], lhsT=w_r[:, j].rearrange("p x n -> p (x n)"), rhs=v[:, x, :],
                                     start=(j == 0 and x == 0), stop=(j == PAGES and x == 1))
                last.then_inc(sem("values_used" if j < PAGES else "seq_out"), 1)

            def turn_out(b):
                pe.wait_ge(sem("seq_rows"), b + 2)
                pe.wait_ge(sem("seq_stored"), 2 * b + 1)
                for pair in range(NPAIR):
                    last = pe.transpose(bank(6)[:, pair * P:(pair + 1) * P], pv_rows[:, pair * P:(pair + 1) * P], ident)
                last.then_inc(sem("seq_turned"), 1)

            def turn(b, pages, before):
                for s in range(PAGES):
                    if pages:
                        turn_page(b, s)
                        if s >= 1:
                            score(b, s - 1)
                    if before:
                        if s == SUMS_AT:
                            sums(b - 1)
                        for j in values_at(s):
                            weigh(b - 1, j)
                if before:
                    weigh(b - 1, PAGES)
                if pages:
                    score(b, PAGES - 1)
                if before:
                    turn_out(b - 1)

            over_sequences(pe, turn)

        @part("act")
        def _(act):
            st = own_steps(act, "act")
            act.drain().then_inc(sem("page_copied"), 2)
            act.activation(v_new_r[:, 0, :], v_n["sb"][:, 4, :], ACT.Copy).then_inc(sem("new_v_high"), 1)
            act.wait_ge(sem("new_logits"), 1)
            st.link(act.activation(new_e[0:NS], new_z[0:NS], ACT.Abs))
            st.link(act.activation(new_e[0:NS], new_e[0:NS], ACT.Exp, scale=-1.0))
            act.activation(new_e[0:NS], new_e[0:NS], ACT.Ln, bias=1.0).then_inc(sem("new_log"), 1)
            act.wait_ge(sem("new_exponents"), 1)
            act.activation(new_z[0:NS], new_z[0:NS], ACT.Exp).then_inc(sem("new_weights"), 1)

            def turn(b, pages, before):
                for s in range(PAGES):
                    if pages:
                        act.wait_ge(sem("page_scored"), PAGES * b + s + 1)
                        act.wait_ge(sem("page_turned"), PAGES * b + s + 1 + K_SLOTS)
                        act.activation(k_turned[s % 2], bank(s % 2).rearrange("p (c n) -> p c n", c=NPAIR), ACT.Copy)\
                            .then_inc(sem("page_copied"), 1)
                    if not before:
                        continue
                    if s == 0:
                        act.wait_ge(sem("seq_logits"), 2 * b + 1)
                        st.do(act.activation(ss_e, ss_z[:, 0:SW], ACT.Abs))
                    if s == 1:
                        st.wait()
                        st.do(act.activation(ss_e, ss_e, ACT.Exp, scale=-1.0))
                    if s == 2:
                        st.wait()
                        act.activation(ss_e, ss_e, ACT.Ln, bias=1.0).then_inc(sem("seq_log"), 1)
                    if s == EXP_AT:
                        act.wait_ge(sem("seq_exponents"), b)
                        st.do(act.activation(ss_z[:, 0:SW], ss_z[:, 0:SW], ACT.Exp))
                        act.wait_ge(sem("seq_out"), b)
                        st.wait()
                        act.activation(w_r[:, :, 0, :], z_pages, ACT.Copy)\
                            .then_inc(sem("weights_high"), 1)
                    for j in values_at(s + 1):
                        act.wait_ge(sem("values_used"), PAGES * (b - 1) + j + 1)
                        act.wait_ge(sem(f"v_page_{j % V_SLOTS}"), 16 * PAGES // V_SLOTS * (b - 1) + 16 * (j // V_SLOTS) + 16)
                        act.activation(v_parts[j % V_PARTS][:, 0], v_page[j % V_SLOTS], ACT.Copy).then_inc(sem("page_v_high"), 1)

            over_sequences(act, turn, st, 3)

        @part("dve")
        def _(dve):
            st = own_steps(dve, "dve")
            st.link(dve.tensor_copy(bias_ht, bias.rearrange("p (h o) -> p h o", o=1).to_broadcast([P, H, DT])))
            st.do(dve.memset(new_z, 0.0))
            st.do(dve.memset(new_p, 0.0))
            flat_bias = small[:, 8:40]
            dve.wait_ge(sem("mask_in"), 16)
            st.wait()
            st.link(dve.tensor_tensor(by_b(mask_sb)[0:NS], by_b(mask_sb)[0:NS],
                                      flat_bias[0:NS].rearrange("p (o n) -> p o n", o=1).to_broadcast([NS, DB, HT]), ALU.add))
            st.do(dve.memset(pv_rows, 0.0))
            dve.wait_ge(sem("new_v_high"), 1)
            dve.tensor_tensor(v_new_r[:, 1, :], v_n["sb"][:, 4, :], v_new_r[:, 0, :], ALU.subtract).then_inc(sem("new_v_low"), 1)
            dve.wait_ge(sem("new_scores"), 1)
            dve.scalar_tensor_tensor(new_z[0:NS], bank(6)[0:NS, 0:DB * HT], SCALE, mask_sb[0:NS], ALU.mult, ALU.add)\
                .then_inc(sem("new_logits"), 1)
            dve.wait_ge(sem("new_log"), 1)
            dve.scalar_tensor_tensor(new_p[0:NS], new_z[0:NS], 0.0, new_e[0:NS], ALU.max, ALU.add)\
                .then_inc(sem("new_softplus"), 1)
            dve.wait_ge(sem("new_sums"), 1)
            dve.tensor_tensor(new_z[0:NS], new_z[0:NS], bank(7)[0:NS, 0:DB * HT], ALU.subtract)\
                .then_inc(sem("new_exponents"), 1)
            dve.wait_ge(sem("new_weights"), 1)
            dve.drain().then_inc(sem("page_v_low"), V_SLOTS)
            dve.drain().then_inc(sem("seq_logits"), 1)
            dve.drain().then_inc(sem("seq_rows"), 1)
            dve.drain().then_inc(sem("seq_stored"), 1)

            def logits(b):
                dve.wait_ge(sem("page_scored"), PAGES * b + PAGES + 2)
                dve.scalar_tensor_tensor(ss_z[:, 0:SW].rearrange("p (j n) -> p j n", j=PAGES),
                                         bank(2).rearrange("p (j n) -> p j n", j=PAGES), SCALE,
                                         flat_bias.rearrange("p (o n) -> p o n", o=1).to_broadcast([P, PAGES, HT]),
                                         ALU.mult, ALU.add).then_inc(sem("seq_logits"), 1)
                dve.tensor_scalar(ss_z[:, SW:SW + HT], by_b(new_z)[:, bass.ds(b, 1), :].rearrange("p o n -> p (o n)"),
                                  1.0, None, ALU.mult).then_inc(sem("seq_logits"), 1)

            def turn(b, pages, before):
                for s in range(PAGES):
                    if not before:
                        continue
                    if s == 3:
                        dve.wait_ge(sem("seq_log"), b)
                        dve.wait_ge(sem("seq_logits"), 2 * b + 1)
                        st.link(dve.scalar_tensor_tensor(ss_p, ss_z[:, 0:SW], 0.0, ss_e, ALU.max, ALU.add))
                        st.do(dve.tensor_copy(ss_c[:, SW - HT:SW], ss_p[:, SW - HT:SW]))
                        st.link(dve.tensor_tensor(ss_c[:, 0:SW - HT], ss_p[:, 0:SW - HT], ss_p[:, HT:SW], ALU.add))
                        for step in (2, 4, 8):
                            w = SW - step * HT
                            ins = dve.tensor_tensor(ss_c[:, 0:w], ss_c[:, 0:w], ss_c[:, step * HT:SW], ALU.add)
                            if step < 8:
                                st.link(ins)
                            else:
                                ins.then_inc(sem("seq_suffix"), 1)
                    if s == SUMS_AT:
                        dve.wait_ge(sem("seq_sums"), b)
                        dve.tensor_tensor(ss_z[:, 0:SW], ss_z[:, 0:SW], bank(4), ALU.subtract).then_inc(sem("seq_exponents"), 1)
                    if s == EXP_AT:
                        dve.wait_ge(sem("weights_high"), b)
                        dve.tensor_tensor(w_r[:, :, 1, :], z_pages, w_r[:, :, 0, :], ALU.subtract)\
                            .then_inc(sem("weights_low"), 1)
                    for j in values_at(s + 1):
                        dve.wait_ge(sem("page_v_high"), PAGES * (b - 1) + j + 1)
                        dve.tensor_tensor(v_parts[j % V_PARTS][:, 1], v_page[j % V_SLOTS], v_parts[j % V_PARTS][:, 0], ALU.subtract)\
                            .then_inc(sem("page_v_low"), 1)
                if before:
                    dve.wait_ge(sem("seq_out"), b + 1)
                    dve.tensor_copy(pv_rows[0:2 * HT], bank(5)[0:2 * HT, :]).then_inc(sem("seq_rows"), 1)
                if pages:
                    logits(b)
                if before:
                    dve.wait_ge(sem("seq_turned"), b)
                    cols = pv_cols.rearrange("p (c n) -> p c n", c=NPAIR)
                    st.link(dve.tensor_copy(pv_cols[:, 0:NPAIR * 2 * HT].rearrange("p (c n) -> p c n", c=NPAIR),
                                            bank(6).rearrange("p (c n) -> p c n", c=NPAIR)[:, :, 0:2 * HT]))
                    for e in range(2):
                        r = slice(64 * e, 64 * e + 64)
                        dve.tensor_tensor(o_t[r, 0:4, bass.ds((b - 1) * DT + SEQ, DT)], cols[r, :, e * DT:(e + 1) * DT],
                                          cols[r, :, HT + e * DT:HT + (e + 1) * DT], ALU.add).then_inc(sem("seq_stored"), 1)

            over_sequences(dve, turn, st, 6)

        for engine in programs:
            programs[engine].append(end_stage)

        KEYS_IN, VALUES_IN = 16 * DB * PAGES // K_SLOTS, 16 * DB * PAGES // V_SLOTS
        WK = NW * P
        work_era.close()
        take_in(work_era, "windows", ALL_COLUMNS - SAMPLE)
        kw = [take(NW * DH).rearrange("p (m c) -> p m c", m=NW) for _ in range(2)]
        vw = [take(NW * DH).rearrange("p (m c) -> p m c", m=NW) for _ in range(2)]
        kw_t = take(NPAIR * WK).rearrange("p (c n) -> p c n", c=NPAIR)
        q_b = take(NPAIR * HT).rearrange("p (c n) -> p c n", c=NPAIR)
        dw_p = take(WK + NS)
        dw_t = take((NW + 1) * HT).rearrange("p (m n) -> p m n", m=NW + 1)
        window_sb = take(WK)
        fresh_sb = take(DB * NS)
        dw_max, dw_top, dw_sum, dw_inv = (small[0:HT, 128 + 4 * i:129 + 4 * i] for i in range(4))
        dw_max2 = small[0:HT, 129:130]

        def over_windows(eng, turn, st=None, per_turn=0):
            turn(0, 0, 0, False)
            with eng.Fori(0, DB // 2 - 1) as i:
                if st:
                    st.enter(i, per_turn)
                turn(2 * i + 1, 1, i, True)
                turn(2 * i + 2, 0, i + 1, True)
                if st:
                    st.leave(DB // 2 - 1)
            turn(DB - 1, 1, DB // 2 - 1, True)

        near_rows = [a.rearrange("b (m p) h d -> b p m (h d)", p=P) for a in (state_k_win, state_v_win)]
        far_rows = [a.rearrange("b (m g s) h d -> b m g s (h d)", g=32, s=16) for a in (state_k_win, state_v_win)]

        @part("sp")
        def _(sp):
            sp.dma_start(window_sb[0:HT, :], count_window).then_inc(sem("window_in"), 16)
            sp.dma_start(fresh_sb[0:HT, :], count_fresh).then_inc(sem("window_in"), 16)
            with sp.Fori(0, DB // 2) as i:
                for s in range(2):
                    b = 2 * i + s
                    for x, to, name in ((0, kw, "k"), (1, vw, "v")):
                        sp.wait_ge(sem("kw_turned" if name == "k" else "dw_out"), b + 1)
                        sp.dma_start(to[s][:, 0:NEAR, :],
                                     near_rows[x][bass.ds(b, 1), :, WIN // P - NEAR:WIN // P, :]
                                     .rearrange("o p m c -> (o p) m c")).then_inc(sem(f"{name}_page_{s}"), 16)
                        for m in range(FAR):
                            sp.dma_start(to[s][:, NEAR + m, :],
                                         far_rows[x][bass.ds(b, 1), m, :, 0:DT, :].rearrange("o g s c -> (o g) s c"))\
                                .then_inc(sem(f"{name}_page_{s}"), 16)

        @part("pe")
        def _(pe):
            pe.drain().then_inc(sem("kw_turned"), 2)
            pe.drain().then_inc(sem("dw_out"), 2)
            pe.drain().then_inc(sem("dw_scores"), 1)

            def turn_keys(b, s, i):
                pe.wait_ge(sem(f"k_page_{s}"), KEYS_IN + 64 * i + 64)
                for m in range(NW):
                    pe.wait_ge(sem(f"kw_copied_{m % 2}"), (4 - m % 2) * b + m // 2 + 1)
                    for pair in range(NPAIR):
                        last = pe.transpose(bank(m % 2)[:, pair * P:(pair + 1) * P],
                                            kw[s][:, m, pair * P:(pair + 1) * P], ident)
                    last.then_inc(sem("kw_turned" if m == NW - 1 else "kw_turn"), 1)

            def scores(b):
                pe.wait_ge(sem("kw_copied_0"), 4 * b + 5)
                pe.wait_ge(sem("kw_copied_1"), 3 * b + 4)
                pe.wait_ge(sem("q_b_ready"), b + 1)
                pe.wait_ge(sem("dw_logits"), 2 * b + 2)
                for a, w in ((0, BANK), (BANK, WK - BANK), (WK, NS)):
                    for pair in range(NPAIR):
                        rhs = kw_t[:, pair, a:a + w] if a < WK else k_s["dil"][:, pair, :]
                        last = pe.matmul(bank(2, 2)[0:HT, a:a + w], lhsT=q_b[:, pair, :], rhs=rhs,
                                         start=(pair == 0), stop=(pair == NPAIR - 1))
                last.then_inc(sem("dw_scores"), 1)

            def weigh(b, s, i):
                pe.wait_ge(sem("dw_scaled"), b + 1)
                for m in range(NW + 1):
                    w = P if m < NW else NS
                    last = pe.transpose(bank(6, 2)[0:w, m * P:(m + 1) * P], dw_p[:, m * P:m * P + w], ident)
                last.then_inc(sem("dw_turn"), 1)
                pe.wait_ge(sem("dw_turned"), b + 1)
                pe.wait_ge(sem(f"v_page_{s}"), VALUES_IN + 64 * i + 64)
                pe.wait_ge(sem("dw_stored"), 2 * b + 1)
                for m in range(NW + 1):
                    v = vw[s][:, m, :] if m < NW else v_n["dil"][:, 4, :]
                    for pair in range(NPAIR):
                        last = pe.matmul(bank(5)[:, pair * 8:pair * 8 + 8], lhsT=v[:, pair * P:(pair + 1) * P],
                                         rhs=dw_t[:, m, pair * 8:pair * 8 + 8],
                                         start=(m == 0 and pair == 0), stop=(m == NW), skip_group_check=True)
                last.then_inc(sem("dw_out"), 1)

            def turn(b, s, i, before):
                turn_keys(b, s, i)
                scores(b)
                if before:
                    weigh(b - 1, 1 - s, i if s == 1 else i - 1)

            over_windows(pe, turn)
            weigh(DB - 1, 1, DB // 2 - 1)

        @part("pool")
        def _(pool):
            with pool.Fori(0, DB) as b:
                pool.wait_ge(sem("dw_scores"), b + 1)
                pool.tensor_copy(q_b, q_wide[:, :, bass.ds(b, 1), :].rearrange("p c o n -> p (c o) n"))\
                    .then_inc(sem("q_b_ready"), 1)

        @part("act")
        def _(act):
            act.drain().then_inc(sem("kw_copied_0"), 1)

            def turn(b, s, i, before):
                act.wait_ge(sem("dw_scores"), b + 1)
                for m in range(0, NW, 2):
                    if m < NW - 1:
                        act.wait_ge(sem("kw_turn"), (NW - 1) * b + m + 1)
                    else:
                        act.wait_ge(sem("kw_turned"), b + 3)
                    act.activation(kw_t[:, :, m * P:(m + 1) * P], bank(0).rearrange("p (c n) -> p c n", c=NPAIR),
                                   ACT.Copy).then_inc(sem("kw_copied_0"), 1)
                act.wait_ge(sem("dw_top"), b + 1)
                act.activation(dw_p[0:HT], dw_p[0:HT], ACT.Exp, bias=dw_top, accum_out=dw_sum)\
                    .then_inc(sem("dw_exp"), 1)

            over_windows(act, turn)

        @part("dve")
        def _(dve):
            st = own_steps(dve, "dve")
            st.do(dve.memset(dw_p, 0.0))
            st.link(dve.memset(dw_t, 0.0))
            turned = bank(6, 2).rearrange("p (m n) -> p m n", m=NW + 1)
            dve.drain().then_inc(sem("kw_copied_1"), 1)
            dve.drain().then_inc(sem("dw_logits"), 2)
            dve.drain().then_inc(sem("dw_stored"), 1)
            dve.wait_ge(sem("window_in"), 2 * 16)

            def normalise(b):
                dve.wait_ge(sem("dw_exp"), b + 1)
                dve.reciprocal(dw_inv, dw_sum).then_inc(sem("dw_inverse"), 1)
                dve.wait_ge(sem("dw_inverse"), b + 1)
                dve.tensor_scalar(dw_p[0:HT], dw_p[0:HT], dw_inv, None, ALU.mult).then_inc(sem("dw_scaled"), 1)

            def copy_turned(b):
                dve.wait_ge(sem("dw_turn"), b + 1)
                dve.tensor_copy(dw_t[:, 0:NW, :], turned[:, 0:NW, 0:HT])
                dve.tensor_copy(dw_t[0:NS, NW, :], turned[0:NS, NW, 0:HT]).then_inc(sem("dw_turned"), 1)

            def logits(b):
                dve.wait_ge(sem("dw_scores"), b + 2)
                st.do(dve.tensor_tensor(dw_p[0:HT, WK:WK + NS], bank(2, 2)[0:HT, WK:WK + NS],
                                        fresh_sb[0:HT, bass.ds(b * NS, NS)], ALU.add))
                dve.tensor_tensor_reduce(out=dw_p[0:HT, 0:WK], in0=bank(2, 2)[0:HT, 0:WK], in1=window_sb[0:HT],
                                         scale=SCALE, scalar=LOWEST, op0=ALU.add, op1=ALU.max, accum_out=dw_max)\
                    .then_inc(sem("dw_logits"), 1)
                st.wait()
                dve.tensor_scalar(dw_p[0:HT, WK:WK + NS], dw_p[0:HT, WK:WK + NS], SCALE, None, ALU.mult)\
                    .then_inc(sem("dw_logits"), 1)
                dve.wait_ge(sem("dw_logits"), 2 * b + 4)
                st.link(dve.tensor_reduce(dw_max2, dw_p[0:HT, WK:WK + NS], AX_X, ALU.max))
                st.link(dve.tensor_tensor(dw_top, dw_max, dw_max2, ALU.max))
                dve.tensor_scalar(dw_top, dw_top, -1.0, None, ALU.mult).then_inc(sem("dw_top"), 1)

            def store(b):
                dve.wait_ge(sem("dw_out"), b + 3)
                out = bank(5)[:, 0:HT].rearrange("p (c n) -> p c n", c=NPAIR)
                for e in range(2):
                    r = slice(64 * e, 64 * e + 64)
                    dve.tensor_scalar(o_t[r, 4:8, bass.ds(b * DT + SEQ, DT)], out[r, :, e * DT:(e + 1) * DT],
                                      1.0, None, ALU.mult).then_inc(sem("dw_stored"), 1)

            def turn(b, s, i, before):
                for m in range(1, NW, 2):
                    dve.wait_ge(sem("kw_turn"), (NW - 1) * b + m + 1)
                    dve.tensor_copy(kw_t[:, :, m * P:(m + 1) * P], bank(1).rearrange("p (c n) -> p c n", c=NPAIR))\
                        .then_inc(sem("kw_copied_1"), 1)
                if before:
                    normalise(b - 1)
                    copy_turned(b - 1)
                logits(b)
                if before:
                    store(b - 1)

            over_windows(dve, turn, st, 6)
            normalise(DB - 1)
            copy_turned(DB - 1)
            store(DB - 1)
            dve.memset(o_t[:, :, N:NP], 0.0).then_inc(sem("pad_cleared"), 1)

        for engine in programs:
            programs[engine].append(end_stage)

        work_era.close()
        era.close()
        h1_r = ctx.enter_context(nc.sbuf_tensor("h1_parts", [P, H1_R], F32R))[:, :]\
            .rearrange("p (s k n) -> p s k n", s=2, k=KD)
        open_era("peer", ALL_COLUMNS - KEPT - H1_R - WQ_R)
        wo_sb = take(KD * D).rearrange("p (k n) -> p k n", k=KD)
        row_g, row_b = take(D), take(D)
        stats = small[:, 64:76].rearrange("p (g s) -> p g s", g=2)
        mean_var, deviation, inverse = small[:, 80:82], small[:, 84:85], small[:, 88:89]
        eps = small[:, 92:93]

        def to_rows(a):
            return a.rearrange("(o d) -> o d", o=1).to_broadcast([P, D])

        def layer_norm(dve, st, x, g, b, count, r=P):
            for half in range(2):
                st.do(dve.bn_stats(stats[0:r, half, :], x[:, half * 512:(half + 1) * 512]))
            st.wait()
            dve.bn_aggr(mean_var[0:r], stats[0:r]).then_inc(sem("variance"), 1)
            dve.wait_ge(sem("deviation"), count)
            st.link(dve.reciprocal(inverse[0:r], deviation[0:r]))
            st.link(dve.tensor_scalar(x, x, mean_var[0:r, 0:1], inverse[0:r], ALU.subtract, ALU.mult))
            st.link(dve.tensor_tensor(x, x, g[0:r], ALU.mult))
            dve.tensor_tensor(x, x, b[0:r], ALU.add).then_inc(sem("normed"), 1)

        @part("sp")
        def _(sp):
            sp.dma_start(wo_sb, w_out.rearrange("(k p) n -> p k n", p=P)).then_inc(sem("w_out_in"), 16)
            for to, frm in ((row_g, ln1_g), (row_b, ln1_b)):
                sp.dma_start(to, to_rows(frm)).then_inc(sem("norms_in"), 16)

        @part("pe")
        def _(pe):
            pe.wait_ge(sem("w_out_in"), 16)

            def turn(t):
                pe.wait_ge(sem("normed"), t + 1)
                for half in range(2):
                    u = 2 * t + half
                    if u >= 4:
                        pe.wait_ge(sem("h1_low"), u - 3)
                    for k in range(4):
                        last = pe.transpose(bank(4 + u % 4)[:, k * P:(k + 1) * P],
                                            x_nat[:, t, (4 * half + k) * P:(4 * half + k + 1) * P], ident)
                    last.then_inc(sem("h1_t_ready"), 1)

            for t in range(NT):
                if t >= 2:
                    pe.wait_ge(sem("residual"), t - 1)
                for half in range(2):
                    for k in range(KD):
                        last = pe.matmul(bank(2 * (t % 2) + half), lhsT=o_t[:, k, t * P:(t + 1) * P],
                                         rhs=wo_sb[:, k, half * 512:(half + 1) * 512], start=(k == 0), stop=(k == KD - 1))
                last.then_inc(sem("mixed"), 1)
                if t >= 1:
                    turn(t - 1)
            turn(NT - 1)

        @part("act")
        def _(act):
            act.wait_ge(sem("eps_set"), 1)
            for t in range(NT):
                act.wait_ge(sem("variance"), t + 1)
                act.activation(deviation, mean_var[:, 1:2], ACT.Sqrt, bias=eps).then_inc(sem("deviation"), 1)
                for half in range(2):
                    u = 2 * t + half
                    act.wait_ge(sem("h1_t_ready"), u + 1)
                    act.activation(h1_r[:, 0, 4 * half:4 * half + 4, t * P:(t + 1) * P],
                                   bank(4 + u % 4).rearrange("p (k n) -> p k n", k=4), ACT.Copy).then_inc(sem("h1_high"), 1)

        @part("dve")
        def _(dve):
            st = own_steps(dve, "dve")
            dve.memset(eps, EPS).then_inc(sem("eps_set"), 1)
            dve.wait_ge(sem("norms_in"), 2 * 16)

            def low(t):
                for half in range(2):
                    u = 2 * t + half
                    dve.wait_ge(sem("h1_high"), u + 1)
                    ks = slice(4 * half, 4 * half + 4)
                    dve.tensor_tensor(h1_r[:, 1, ks, t * P:(t + 1) * P], bank(4 + u % 4).rearrange("p (k n) -> p k n", k=4),
                                      h1_r[:, 0, ks, t * P:(t + 1) * P], ALU.subtract).then_inc(sem("h1_low"), 1)

            for t in range(NT):
                dve.wait_ge(sem("mixed"), t + 1)
                dve.scalar_tensor_tensor(x_nat[:, t, :], x_nat[:, t, :], ALPHA, bank(2 * (t % 2), 2), ALU.mult, ALU.add)\
                    .then_inc(sem("residual"), 1)
                dve.wait_ge(sem("residual"), t + 1)
                layer_norm(dve, st, x_nat[:, t, :], row_g, row_b, t + 1)
                if t >= 1:
                    low(t - 1)
            low(NT - 1)

        for engine in programs:
            programs[engine].append(end_stage)

        NC = 2 * PH
        NWQ = NC // 2
        place[0] = KEPT
        wq_sb = [take(KD * 2 * P).rearrange("p (k c) -> p k c", k=KD) for _ in range(2)]
        keys_n, keys_t = take(2 * P).rearrange("p (c d) -> p c d", c=2), take(2 * P).rearrange("p (c n) -> p c n", c=2)
        assert place[0] <= KEPT + 4 * PH * TK * TK
        s_copy = [take(NT * NK, KEPT + 4 * PH * TK * TK + e * NT * NK).rearrange("p (t n) -> p t n", t=NT) for e in range(2)]
        s_rest = take(NT * NK).rearrange("p (t n) -> p t n", t=NT)
        top = take(NT * NC * TK).rearrange("p (t c k) -> p t c k", t=NT, c=NC)
        top_i = take(NT * NC * TK).bitcast(U32).rearrange("p (t c k) -> p t c k", t=NT, c=NC)
        top_f = take(NT * NC * TK).rearrange("p (t h e k) -> p t h e k", t=NT, h=PH, e=2)
        IJG_T = max(place[0], KEPT + 4 * NK * CHUNK)
        wq_tensor = era.enter_context(nc.sbuf_tensor("wq_parts", [P, WQ_R], F32R))
        wq_r = [wq_tensor[:, e * (WQ_R // 2):(e + 1) * (WQ_R // 2)].rearrange("p (s k c) -> p s k c", s=2, k=KD)
                for e in range(2)]
        pq = [o_t.rearrange("p c n -> p (c n)")[:, e * NP:(e + 1) * NP] for e in range(2)]
        wq_g = peer_wq.rearrange("(k p) (g c) -> g p k c", p=P, c=2 * P)

        def top16(dve, st, values, rest, out, index, n, chunk=None):
            for c in range(n):
                st.do(dve.max(out[:, c, 0:8], values[:, c, :]))
            for c in range(n):
                st.wait(n - 1)
                st.do(dve.max_index(index[:, c, 0:8], out[:, c, 0:8], values[:, c, :]))
            for c in range(n):
                st.do(dve.match_replace(rest[:, c, :], out[:, c, 0:8], values[:, c, :], LOWEST))
            for c in range(n):
                st.wait(n - 1)
                st.do(dve.max(out[:, c, 8:16], rest[:, c, :]))
            for c in range(n):
                st.wait(n - 1)
                ins = dve.max_index(index[:, c, 8:16], out[:, c, 8:16], rest[:, c, :])
                if c == n - 1 and chunk is not None:
                    ins.then_inc(sem("top_found"), 1)
                else:
                    st.do(ins)
            if chunk is not None:
                dve.wait_ge(sem("top_found"), chunk + 1)
            else:
                st.wait()

        @part("sp")
        def _(sp):
            sp.dma_start(keys_n, peer_subkeys.rearrange("c k d -> k c d")).then_inc(sem("subkeys_in"), 16)
            for g in range(NWQ):
                if g >= 2:
                    sp.wait_ge(sem("wq_low"), g - 1)
                sp.dma_start(wq_sb[g % 2], wq_g[g]).then_inc(sem(f"w_in_{g % 2}"), 16)

        @part("pe")
        def _(pe):
            pe.wait_ge(sem("subkeys_in"), 16)
            for c in range(2):
                last = pe.transpose(bank(4)[:, c * P:(c + 1) * P], keys_n[:, c, :], ident)
            last.then_inc(sem("subkeys_turn"), 1)
            pe.wait_ge(sem("subkeys_turned"), 1)

            def score(c):
                pe.wait_ge(sem("pq_copied"), 2 * c + 2)
                if c >= 2:
                    pe.wait_ge(sem("s_copied"), c - 1)
                for t in range(NT):
                    last = pe.matmul(bank(4 + 2 * (c % 2), 2)[:, t * P:(t + 1) * P], lhsT=pq[c % 2][:, t * P:(t + 1) * P],
                                     rhs=keys_t[:, c % 2, :], start=True, stop=True)
                last.then_inc(sem("s_ready"), 1)

            for c in range(NC):
                pe.wait_ge(sem("wq_high"), c // 2 + 1)
                pe.wait_ge(sem("wq_low"), c // 2 + 1)
                w = wq_r[c // 2 % 2]
                for half in range(2):
                    u = 2 * c + half
                    if u >= 4:
                        pe.wait_ge(sem("pq_copied"), u - 3)
                    n = 0
                    for x, y in PARTS[::-1]:
                        for k in range(KD):
                            n += 1
                            last = pe.matmul(bank(u % 4)[:, 0:320], lhsT=w[:, x, k, c % 2 * P:(c % 2 + 1) * P],
                                             rhs=h1_r[:, y, k, half * 320:(half + 1) * 320],
                                             start=(n == 1), stop=(n == 3 * KD))
                    last.then_inc(sem("pq_ready"), 1)
                if c >= 1:
                    score(c - 1)
            score(NC - 1)

        @part("act")
        def _(act):
            def high(g):
                act.wait_ge(sem(f"w_in_{g % 2}"), 16 * (len(GROUPS) // 2 + g // 2 + 1))
                if g >= 2:
                    act.wait_ge(sem("pq_ready"), 4 * (g - 1))
                act.activation(wq_r[g % 2][:, 0], wq_sb[g % 2], ACT.Copy).then_inc(sem("wq_high"), 1)

            def scores_out(c):
                act.wait_ge(sem("s_ready"), c + 1)
                if c >= 2:
                    act.wait_ge(sem("top_found"), c - 1)
                act.activation(s_copy[c % 2], bank(4 + 2 * (c % 2), 2)[:, 0:NT * P].rearrange("p (t n) -> p t n", t=NT), ACT.Copy)\
                    .then_inc(sem("s_copied"), 1)

            high(0)
            high(1)
            for c in range(NC):
                for half in range(2):
                    u = 2 * c + half
                    act.wait_ge(sem("pq_ready"), u + 1)
                    if c >= 2:
                        act.wait_ge(sem("s_ready"), c - 1)
                    act.activation(pq[c % 2][:, half * 320:(half + 1) * 320], bank(u % 4)[:, 0:320], ACT.Copy)\
                        .then_inc(sem("pq_copied"), 1)
                if c % 2 == 1 and c // 2 + 2 < NWQ:
                    high(c // 2 + 2)
                if c >= 1:
                    scores_out(c - 1)
            scores_out(NC - 1)

        @part("dve")
        def _(dve):
            dve.wait_ge(sem("subkeys_turn"), 1)
            dve.tensor_copy(keys_t, bank(4)[:, 0:2 * P].rearrange("p (c n) -> p c n", c=2)).then_inc(sem("subkeys_turned"), 1)

            def low(g):
                dve.wait_ge(sem("wq_high"), g + 1)
                dve.tensor_tensor(wq_r[g % 2][:, 1], wq_sb[g % 2], wq_r[g % 2][:, 0], ALU.subtract).then_inc(sem("wq_low"), 1)

            st = own_steps(dve, "dve")
            low(0)
            low(1)
            for c in range(NC):
                if c % 2 == 1 and c // 2 + 2 < NWQ:
                    low(c // 2 + 2)
                dve.wait_ge(sem("s_copied"), c + 1)
                top16(dve, st, s_copy[c % 2], s_rest, top[:, :, c, :], top_i[:, :, c, :], NT, c)
            dve.tensor_copy(top_f.rearrange("p t h e k -> p (t h e k)"), top_i.rearrange("p t c k -> p (t c k)"))

        for engine in programs:
            programs[engine].append(end_stage)

        place[0] = KEPT - KD * NP
        best = take(PH * TK).rearrange("p (h k) -> p h k", h=PH)
        best_i = take(PH * TK).bitcast(U32).rearrange("p (h k) -> p h k", h=PH)
        digit_u = [take(PH * TK).bitcast(U32) for _ in range(2)]
        digit_f = [take(PH * TK) for _ in range(2)]
        ijg = take(3 * P).rearrange("p (x n) -> p x n", x=3)
        best_sum, best_inv = take(PH), take(PH)
        gate_e = take(PH * TK)
        assert place[0] <= KEPT
        cand = take(PH * TK * TK, KEPT).rearrange("p (h n) -> p h n", h=PH)
        cand_rest = take(PH * TK * TK).rearrange("p (h n) -> p h n", h=PH)
        equal = [take(PH * TK * TK) for _ in range(2)]
        ijg_t = take(3 * NP, IJG_T).rearrange("p (x n) -> p x n", x=3)

        @part("act")
        def _(act):
            for t in range(NT):
                act.wait_ge(sem("best_less"), t + 1)
                act.activation(gate_e, gate_e, ACT.Exp).then_inc(sem("gate_exp"), 1)
                act.wait_ge(sem("ijg_turn"), t + 1)
                act.activation(ijg_t[:, :, t * P:(t + 1) * P], bank(0)[:, 0:3 * P].rearrange("p (x n) -> p x n", x=3), ACT.Copy)\
                    .then_inc(sem("ijg_turned"), 1)

        @part("pe")
        def _(pe):
            for t in range(NT):
                pe.wait_ge(sem("ijg_ready"), t + 1)
                if t >= 1:
                    pe.wait_ge(sem("ijg_turned"), t)
                for x in range(3):
                    last = pe.transpose(bank(0)[:, x * P:(x + 1) * P], ijg[:, x, :], ident)
                last.then_inc(sem("ijg_turn"), 1)

        @part("dve")
        def _(dve):
            st = own_steps(dve, "dve")
            grid = [PH, TK, TK]
            for t in range(NT):
                halves = top[:, t].rearrange("p (h e) k -> p h e k", e=2)
                st.link(dve.tensor_tensor(cand.rearrange("p h (a b) -> p h a b", a=TK),
                                          halves[:, :, 0, :].rearrange("p h (a o) -> p h a o", o=1).to_broadcast([P] + grid),
                                          halves[:, :, 1, :].rearrange("p h (o b) -> p h o b", o=1).to_broadcast([P] + grid),
                                          ALU.add))
                top16(dve, st, cand, cand_rest, best, best_i, PH)
                dve.tensor_tensor(gate_e.rearrange("p (h k) -> p h k", h=PH), best,
                                  best[:, :, 0:1].to_broadcast([P, PH, TK]), ALU.subtract).then_inc(sem("best_less"), 1)
                flat_i = best_i.rearrange("p h k -> p (h k)")
                st.do(dve.tensor_scalar(digit_u[0], flat_i, 4, None, ALU.logical_shift_right))
                st.link(dve.tensor_scalar(digit_u[1], flat_i, 15, None, ALU.bitwise_and))
                for e in range(2):
                    st.do(dve.tensor_copy(digit_f[e], digit_u[e]))
                st.wait()
                if t >= 1:
                    dve.wait_ge(sem("ijg_turned"), t)
                for e in range(2):
                    st.do(dve.tensor_tensor(equal[e].rearrange("p (n a) -> p n a", a=TK),
                                            digit_f[e].rearrange("p (n o) -> p n o", o=1).to_broadcast([P, PH * TK, TK]),
                                            iota[:, 0:TK].rearrange("p (o a) -> p o a", o=1).to_broadcast([P, PH * TK, TK]),
                                            ALU.is_equal))
                for e in range(2):
                    st.wait(1)
                    x = equal[e].rearrange("p (h k a) -> p h k a", h=PH, k=TK)
                    st.do(dve.tensor_tensor(x, x, top_f[:, t, :, e, :].rearrange("p h (o a) -> p h o a", o=1)
                                            .to_broadcast([P] + grid), ALU.mult))
                for e in range(2):
                    st.wait(1)
                    st.do(dve.tensor_reduce(ijg[:, e, :], equal[e].rearrange("p (n a) -> p n a", a=TK), AX_X, ALU.add))
                dve.wait_ge(sem("gate_exp"), t + 1)
                st.link(dve.tensor_reduce(best_sum, gate_e.rearrange("p (h k) -> p h k", h=PH), AX_X, ALU.add))
                st.link(dve.reciprocal(best_inv, best_sum))
                dve.tensor_tensor(ijg[:, 2, :].rearrange("p (h k) -> p h k", h=PH), gate_e.rearrange("p (h k) -> p h k", h=PH),
                                  best_inv.rearrange("p (h o) -> p h o", o=1).to_broadcast([P, PH, TK]), ALU.mult)\
                    .then_inc(sem("ijg_ready"), 1)

        for engine in programs:
            programs[engine].append(end_stage)

        HALF_C = CHUNK // 2
        table = [take(NK * CHUNK, KEPT).rearrange("p (i n) -> p i n", i=NK)] + \
            [take(NK * CHUNK).rearrange("p (i n) -> p i n", i=NK)]
        hot_j = [take(HALF_C * NK).rearrange("p (n j) -> p n j", n=HALF_C) for _ in range(2)]
        hot_i = [take(HALF_C * NK).rearrange("p (n i) -> p n i", n=HALF_C) for _ in range(2)]
        assert place[0] <= IJG_T

        def over_chunks(eng, body):
            with eng.Fori(0, NCHUNK // 2) as i:
                for s in range(2):
                    body(2 * i + s, s, i)
            body(NCHUNK - 1, 0, NCHUNK // 2)

        @part("sp")
        def _(sp):
            def store(c, s, i):
                sp.wait_ge(sem("table_copied"), 4 * c + 8)
                sp.dma_start(gates_dram[bass.ds(c, 1)].rearrange("o p n -> (o p) n"),
                             table[s].rearrange("p i n -> p (i n)")).then_inc(sem(f"table_out_{s}"), 16)

            over_chunks(sp, store)
            sp.wait_ge(sem("table_out_0"), 16 * (NCHUNK // 2 + 2))
            sp.wait_ge(sem("table_out_1"), 16 * (NCHUNK // 2 + 1))

        def columns(x, c, half):
            cols = ijg_t[:, x, bass.ds(c * CHUNK + half * HALF_C, HALF_C)]
            return cols.rearrange("p (n o) -> p n o", o=1).to_broadcast([P, HALF_C, NK])

        @part("pool")
        def _(pool):
            def scale(c, s, i):
                for half in range(2):
                    pool.wait_ge(sem("hot_i_ready"), 2 * c + half + 1)
                    pool.wait_ge(sem("ijg_turned"), NT)
                    pool.tensor_tensor(hot_i[half], hot_i[half], columns(2, c, half), ALU.mult).then_inc(sem("hot_scaled"), 1)

            over_chunks(pool, scale)

        @part("dve")
        def _(dve):
            iota_b = iota.rearrange("p (o j) -> p o j", o=1).to_broadcast([P, HALF_C, NK])

            def hot(c, s, i):
                for half in range(2):
                    dve.wait_ge(sem("table_ready"), 4 * c + 2 * half + 2)
                    dve.tensor_tensor(hot_i[half], iota_b, columns(0, c, half), ALU.is_equal).then_inc(sem("hot_i_ready"), 1)
                    dve.tensor_tensor(hot_j[half], iota_b, columns(1, c, half), ALU.is_equal).then_inc(sem("hot_j_ready"), 1)

            over_chunks(dve, hot)

        @part("pe")
        def _(pe):
            pe.drain().then_inc(sem("table_ready"), 4)
            pe.wait_ge(sem("table_free"), 1)

            def spread(c, s, i):
                for half in range(2):
                    pe.wait_ge(sem("hot_j_ready"), 2 * c + half + 1)
                    pe.wait_ge(sem("hot_scaled"), 2 * c + half + 1)
                    for n in range(HALF_C):
                        if n % 8 == 0:
                            pe.wait_ge(sem("table_copied"), 4 * c + 2 * half + n // 8 + 1)
                        last = pe.matmul(bank(4 * half + n // 4)[:, n % 4 * NK:(n % 4 + 1) * NK],
                                         lhsT=hot_j[half][:, n, :], rhs=hot_i[half][:, n, :], start=True, stop=True)
                        if n % 8 == 7:
                            last.then_inc(sem("table_ready"), 1)

            over_chunks(pe, spread)

        @part("act")
        def _(act):
            act.drain().then_inc(sem("table_copied"), 4)
            act.drain().then_inc(sem("table_out_0"), 16)
            act.drain().then_inc(sem("table_out_1"), 16)
            act.drain().then_inc(sem("table_free"), 1)

            def copy(c, s, i):
                act.wait_ge(sem(f"table_out_{s}"), 16 * i + 16)
                for q in range(4):
                    act.wait_ge(sem("table_ready"), 4 * c + q + 5)
                    act.activation(table[s][:, :, 8 * q:8 * q + 8].rearrange("p i n -> p n i"),
                                   bank(2 * q, 2).rearrange("p (n i) -> p n i", n=8), ACT.Copy).then_inc(sem("table_copied"), 1)

            over_chunks(act, copy)

        for engine in programs:
            programs[engine].append(end_stage)

        era.close()
        f_t = kept[:, KEPT - KD * NP:KEPT - KD * NP + KD * N].rearrange("p (c n) -> p c n", c=KD)
        open_era("experts", ALL_COLUMNS - KEPT - H1_R - EXPERT_R)
        expert_r = era.enter_context(nc.sbuf_tensor("expert_parts", [P, EXPERT_R], F32R))
        ctx.callback(era.close)
        place_r = [0]

        def take_r(cols):
            place_r[0] += cols
            return expert_r[:, place_r[0] - cols:place_r[0]]

        u_sb = [take(D) for _ in range(GI)]
        v_sb = [take(D) for _ in range(GI)]
        gelu = [take(N) for _ in range(GI)]
        gates = take(NCHUNK * 2 * GI * CHUNK).rearrange("p (c i n) -> p c i n", c=NCHUNK, i=2 * GI)
        row_g2, row_b2 = take(D), take(D)
        u_t = [take_r(2 * D).rearrange("p (s k j) -> p s k j", s=2, k=KD) for _ in range(GI)]
        v_r = [[take_r(2 * D).rearrange("p (s d) -> p s d", s=2) for _ in range(GI)] for _ in range(2)]
        weight = [[take_r(2 * N).rearrange("p (s n) -> p s n", s=2) for _ in range(GI)] for _ in range(2)]
        gates_g = gates_dram.rearrange("c p (g n) -> p c g n", g=NG // 2)

        def over_groups(eng, body):
            body(0, 0, 0)
            with eng.Fori(0, NG // 2 - 1) as i:
                body(2 * i + 1, 1, i)
                body(2 * i + 2, 0, i + 1)
            body(NG - 1, 1, NG // 2 - 1)

        @part("sp")
        def _(sp):
            for to, frm in ((row_g2, ln2_g), (row_b2, ln2_b)):
                sp.dma_start(to, to_rows(frm)).then_inc(sem("norms_in"), 16)

            def load(g):
                for blk in range(GI):
                    x = GI * g + blk
                    sp.wait_ge(sem("u_turned"), x + 1)
                    sp.dma_start(u_sb[blk], peer_u[bass.ds(x * P, P), :]).then_inc(sem(f"u_in_{blk}"), 16)
                    sp.wait_ge(sem("v_low"), x + 1)
                    sp.dma_start(v_sb[blk], peer_v[bass.ds(x * P, P), :]).then_inc(sem(f"v_in_{blk}"), 16)

            with sp.Fori(0, NG // 2) as pair:
                load(2 * pair)
                sp.wait_ge(sem("gated"), 2 * GI * pair + 1)
                sp.dma_start(gates.rearrange("p c i n -> p c (i n)"),
                             gates_g[:, :, bass.ds(pair, 1), :].rearrange("p c o n -> p (c o) n")).then_inc(sem("gates_in"), 16)
                load(2 * pair + 1)

        @part("pool")
        def _(pool):
            for b in range(DB):
                pool.wait_ge(sem("y_ready"), 16 * (7 * b + 3))
                for to, frm in ((k_win_sample, state_k_win), (v_win_sample, state_v_win)):
                    pool.dma_start(to[b].rearrange("w h d -> (w h d)")[0:(WIN - DT) * DH],
                                   frm[b].rearrange("w h d -> (w h d)")[DT * DH:WIN * DH]).then_inc(sem("window_moved"), 16)

        @part("pe")
        def _(pe):
            pe.drain().then_inc(sem("u_turned"), 2)
            pe.drain().then_inc(sem("h_ready"), 4)
            pe.drain().then_inc(sem("y_ready"), 32)

            def turn(g, s, blk):
                x = GI * g + blk
                pe.wait_ge(sem(f"u_in_{blk}"), 16 * g + 16)
                pe.wait_ge(sem("u_low"), 2 * x + 4)
                for k in range(KD):
                    last = pe.transpose(bank(0, 2)[:, k * P:(k + 1) * P], u_sb[blk][:, k * P:(k + 1) * P], ident)
                last.then_inc(sem("u_turned"), 1)

            def hidden(g, s, blk):
                x = GI * g + blk
                pe.wait_ge(sem("u_low"), 2 * x + 6)
                for half in range(2):
                    pe.wait_ge(sem("gelu_done"), 2 * x + half + 1)
                    n = 0
                    for k in range(KD):
                        for a, b in PARTS:
                            n += 1
                            last = pe.matmul(bank(2 + half)[:, 0:HALF], lhsT=u_t[blk][:, a, k, :],
                                             rhs=h1_r[:, b, k, half * HALF:(half + 1) * HALF],
                                             start=(n == 1), stop=(n == 3 * KD))
                    last.then_inc(sem("h_ready"), 1)

            def add_up(g, s, dcs):
                pe.wait_ge(sem("v_low"), GI * g + GI + 2)
                pe.wait_ge(sem("weight_low"), GI * g + GI + 2)
                for dc in dcs:
                    for half in range(2):
                        pe.wait_ge(sem("y_added"), 16 * g + 2 * dc + half + 1)
                        n = 0
                        for blk in range(GI):
                            for a, b in PARTS:
                                n += 1
                                last = pe.matmul(bank(4 + (2 * dc + half) % 4)[:, 0:HALF], lhsT=v_r[s][blk][:, a, dc * P:(dc + 1) * P],
                                                 rhs=weight[s][blk][:, b, half * HALF:(half + 1) * HALF],
                                                 start=(n == 1), stop=(n == 3 * GI))
                        last.then_inc(sem("y_ready"), 1)

            turn(0, 0, 0)

            def group(g, s, pair):
                first, final = s == 0 and isinstance(g, int), s == 1 and isinstance(g, int)
                turn(g, s, 1)
                hidden(g, s, 0)
                if not first:
                    add_up(g - 1, 1 - s, range(0, KD // 2))
                if not final:
                    turn(g + 1, 1 - s, 0)
                hidden(g, s, 1)
                if not first:
                    add_up(g - 1, 1 - s, range(KD // 2, KD))

            over_groups(pe, group)
            add_up(NG - 1, 1, range(KD))

        @part("act")
        def _(act):
            act.drain().then_inc(sem("gelu_done"), 2)

            def u_high(g, s, blk):
                x = GI * g + blk
                act.wait_ge(sem("h_ready"), 2 * x + 2)
                for half in range(2):
                    act.wait_ge(sem("u_turned"), x + 3)
                    act.activation(u_t[blk][:, 0, 4 * half:4 * half + 4, :],
                                   bank(half).rearrange("p (k j) -> p k j", k=4), ACT.Copy)\
                        .then_inc(sem("u_high"), 1)

            def v_high(g, s, blk):
                act.wait_ge(sem("y_ready"), 16 * g + 16)
                act.wait_ge(sem(f"v_in_{blk}"), 16 * g + 16)
                act.activation(v_r[s][blk][:, 0, :], v_sb[blk], ACT.Copy).then_inc(sem("v_high"), 1)

            def activate(g, s, blk):
                x = GI * g + blk
                act.wait_ge(sem("weight_low"), x + 1)
                for half in range(2):
                    act.wait_ge(sem("h_ready"), 2 * x + half + 5)
                    act.activation(gelu[blk][:, half * HALF:(half + 1) * HALF], bank(2 + half)[:, 0:HALF], ACT.Gelu)\
                        .then_inc(sem("gelu_done"), 1)

            def weight_high(g, s, blk):
                act.wait_ge(sem("gated"), GI * g + blk + 2)
                act.activation(weight[s][blk][:, 0, :], gelu[blk], ACT.Copy).then_inc(sem("weight_high"), 1)

            u_high(0, 0, 0)

            def group(g, s, pair):
                final = s == 1 and isinstance(g, int)
                for blk in range(GI):
                    if blk == 0:
                        u_high(g, s, 1)
                    elif not final:
                        u_high(g + 1, 1 - s, 0)
                    v_high(g, s, blk)
                    activate(g, s, blk)
                    weight_high(g, s, blk)

            over_groups(act, group)

        @part("dve")
        def _(dve):
            dve.memset(f_t, 0.0).then_inc(sem("f_cleared"), 1)
            dve.wait_ge(sem("f_cleared"), 1)
            dve.drain().then_inc(sem("u_low"), 4)
            dve.drain().then_inc(sem("v_low"), 2)
            dve.drain().then_inc(sem("weight_low"), 2)
            dve.drain().then_inc(sem("gated"), 1)
            dve.drain().then_inc(sem("y_added"), 4)

            def u_low(g, s, blk):
                x = GI * g + blk
                for half in range(2):
                    dve.wait_ge(sem("u_high"), 2 * x + half + 1)
                    ks = slice(4 * half, 4 * half + 4)
                    dve.tensor_tensor(u_t[blk][:, 1, ks, :], bank(half).rearrange("p (k j) -> p k j", k=4),
                                      u_t[blk][:, 0, ks, :], ALU.subtract).then_inc(sem("u_low"), 1)

            def v_low(g, s, blk):
                dve.wait_ge(sem("v_high"), GI * g + blk + 1)
                dve.tensor_tensor(v_r[s][blk][:, 1, :], v_sb[blk], v_r[s][blk][:, 0, :], ALU.subtract).then_inc(sem("v_low"), 1)

            def gate(g, s, pair, blk):
                if blk == 0:
                    dve.wait_ge(sem("gates_in"), 16 * pair + 16)
                dve.wait_ge(sem("gelu_done"), 2 * (GI * g + blk) + 4)
                out = gelu[blk].rearrange("p (c n) -> p c n", c=NCHUNK)
                dve.tensor_tensor(out, out, gates[:, :, GI * s + blk, :], ALU.mult).then_inc(sem("gated"), 1)

            def weight_low(g, s, blk):
                dve.wait_ge(sem("weight_high"), GI * g + blk + 1)
                dve.tensor_tensor(weight[s][blk][:, 1, :], gelu[blk], weight[s][blk][:, 0, :], ALU.subtract)\
                    .then_inc(sem("weight_low"), 1)

            def add(g, ks):
                for k in ks:
                    to = f_t[:, k // 2, k % 2 * HALF:(k % 2 + 1) * HALF]
                    dve.wait_ge(sem("y_ready"), 16 * g + k + 33)
                    if k < 4:
                        dve.wait_ge(sem("y_added"), 16 * g + k + 2)
                    dve.tensor_tensor(to, to, bank(4 + k % 4)[:, 0:HALF], ALU.add).then_inc(sem("y_added"), 1)

            u_low(0, 0, 0)

            def group(g, s, pair):
                first, final = s == 0 and isinstance(g, int), s == 1 and isinstance(g, int)
                for blk in range(GI):
                    if blk == 0:
                        u_low(g, s, 1)
                    elif not final:
                        u_low(g + 1, 1 - s, 0)
                    v_low(g, s, blk)
                    gate(g, s, pair, blk)
                    if not first:
                        add(g - 1, range(KD * blk, KD * (blk + 1)))
                    weight_low(g, s, blk)

            over_groups(dve, group)
            add(NG - 1, range(2 * KD))

        for engine in programs:
            programs[engine].append(end_stage)

        y_rows = y_prompt.rearrange("b (t p) d -> t (b p) d", p=P)

        @part("pe")
        def _(pe):
            for t in range(NT):
                r = rows_of(t)
                if t >= 2:
                    pe.wait_ge(sem("residual"), NT + t - 1)
                for k in range(KD):
                    last = pe.transpose(bank(2 * (t % 2), 2)[0:r, k * P:(k + 1) * P], f_t[:, k, t * P:t * P + r], ident)
                last.then_inc(sem("f_turned"), 1)

        @part("act")
        def _(act):
            for t in range(NT):
                r = rows_of(t)
                act.wait_ge(sem("variance"), NT + t + 1)
                act.activation(deviation[0:r], mean_var[0:r, 1:2], ACT.Sqrt, bias=eps[0:r]).then_inc(sem("deviation"), 1)

        @part("dve")
        def _(dve):
            st = own_steps(dve, "dve")
            dve.wait_ge(sem("norms_in"), 4 * 16)
            for t in range(NT):
                r = rows_of(t)
                dve.wait_ge(sem("f_turned"), t + 1)
                dve.scalar_tensor_tensor(x_nat[0:r, t, :], x_nat[0:r, t, :], ALPHA, bank(2 * (t % 2), 2)[0:r],
                                         ALU.mult, ALU.add).then_inc(sem("residual"), 1)
                dve.wait_ge(sem("residual"), NT + t + 1)
                layer_norm(dve, st, x_nat[0:r, t, :], row_g2, row_b2, NT + t + 1, r)

        @part("sp")
        def _(sp):
            for t in range(NT):
                sp.wait_ge(sem("normed"), NT + t + 1)
                to = y_rows[t] if t < 4 else y_sample.rearrange("b t d -> (b t) d")
                sp.dma_start(to, x_nat[0:rows_of(t), t, :]).then_inc(sem("y_out"), 16)
            sp.wait_ge(sem("y_out"), NT * 16)


        @part("sp")
        def _(sp):
            sp.wait_ge(sem("pages_in"), 16)
            sp.wait_ge(sem("window_moved"), 2 * DB * 16)
        block = ctx.enter_context(nc.Block())

        def run(parts, eng):
            for p in parts:
                p(eng)

        @block.sync
        def _(eng):
            run(programs["sp"], eng)

        @block.tensor
        def _(eng):
            run(programs["pe"], eng)

        @block.scalar
        def _(eng):
            run(programs["act"], eng)

        @block.vector
        def _(eng):
            run(programs["dve"], eng)

        @block.gpsimd
        def _(eng):
            run(programs["pool"], eng)


_INS = ["x_prompt", "x_sample", "cache_k_sb", "cache_v_sb", "page_table", "state_k_win", "state_v_win",
        "w_in", "w_out", "sb_logit_bias", "ln1_g", "ln1_b", "peer_wq", "peer_subkeys", "peer_u", "peer_v",
        "ln2_g", "ln2_b"]
_OUTS = [(1, SEQ, D), (DB, DT, D), (1, SEQ // P, P, H, HD), (1, SEQ // P, P, H, HD), (DB, DT, H, HD),
         (DB, DT, H, HD), (1, SEQ, H, HD), (1, SEQ, H, HD), (DB, WIN, H, HD), (DB, WIN, H, HD)]


def kernel(**inputs):
    import numpy as _np
    import concourse.bacc as _bacc
    from concourse.bass_utils import run_bass_kernel_spmd as _run

    nc = _bacc.Bacc("TRN2", target_bir_lowering=False, num_devices=1)
    given = {name: _np.ascontiguousarray(inputs[name]) for name in _INS}
    given.update(constants())
    arrays, args = {}, []
    for name, a in given.items():
        arrays[f"in_{name}_dram"] = a
        args.append(nc.dram_tensor(f"in_{name}_dram", a.shape, mybir.dt.from_np(a.dtype), kind="ExternalInput").ap())
    for i, shape in enumerate(_OUTS):
        args.append(nc.dram_tensor(f"out_{i}_dram", shape, F32, kind="ExternalOutput").ap())
    build(nc, *args)
    r = _run(nc, [arrays], core_ids=[0])
    return tuple(r.results[0][f"out_{i}_dram"] for i in range(len(_OUTS)))
```

```python
from contextlib import ExitStack

import numpy as np

import concourse.bass as bass
from concourse import mybir

F32 = mybir.dt.float32
F32R = mybir.dt.float32r
I32 = mybir.dt.int32
U32 = mybir.dt.uint32
ALU = mybir.AluOpType
ACT = mybir.ActivationFunctionType
AX_X = mybir.AxisListType.X

P = 128
D = 1024
KD = D // P
SEQ = 512
DB, DT = 8, 4
NS = DB * DT
N = SEQ + NS
NT = 5
NP = NT * P
H, HD = 8, 64
DH = H * HD
NPAIR = H // 2
PAGES = 16
N_POOL = 160
PAST = PAGES * P
WIN = 2048
SPAN = 128
DILS = (1, 4, 16)
TK = 16
NK = 128
PH = 8
HALF = N // 2
SCALE = HD ** -0.5
ALPHA = 2.0 ** 0.25
EPS = 1e-5
NEG = -1e30
LOWEST = -3.0e38
BANK = 512
CHUNK = 32
NCHUNK = N // CHUNK
GI = 2
NG = NK // GI
NEAR = 4
FAR = 3
NW = NEAR + FAR
K_SLOTS = 8
ALL_COLUMNS = 50176
KEPT = 2 * NT * D + 5 * P + 384
PROJ_R = 2 * KD * (N + DH)
ATTENTION = 2 * NT * DH + 2 * (H + NPAIR) * NS + NPAIR * DB * NS
SAMPLE_R = 5 * 2 * DH + 2 * (PAGES + 1) * H * DT
H1_R = 2 * KD * NP
PARTS = ((0, 0), (0, 1), (1, 0))
PEER = 3 * PH * TK * TK + 3 * NT * NK + 3 * NT * 2 * PH * TK
EXPERT_R = 2 * (GI * D + 2 * GI * D + 2 * GI * N)
WQ_R = 2 * 2 * KD * 2 * P


def constants():
    r = np.arange(P)
    ident = np.eye(P, dtype=np.float32)
    tri = (r[:, None] >= r[None, :]).astype(np.float32)
    ones = np.ones((P, P), np.float32)
    diag = np.where(r[None, :] > r[:, None], 0.0, NEG)
    iota = np.broadcast_to(r, (P, P))
    square = np.concatenate([ident, tri, ones, diag, iota], axis=1).astype(np.float32)

    def log_count(dist):
        count = ((dist >= 0) & (dist <= SPAN)).astype(np.int64)
        for dil in DILS[1:]:
            count = count + ((dist >= 0) & (dist % dil == 0) & (dist <= SPAN * dil))
        return np.where(count > 0, np.log(np.maximum(count, 1)) / SCALE, NEG)

    q = np.arange(SEQ)
    prompt = log_count(q[:, None] - q[None, :]).reshape(NT - 1, P, SEQ).transpose(1, 0, 2)
    near = WIN - NEAR * P + np.arange(NEAR * P)
    g = np.arange(FAR * P)
    far = 16 * (g // 4) + g % 4
    t = np.arange(DT)
    rows = WIN + np.tile(t, H)
    window = log_count(rows[:, None] - np.concatenate([near, far])[None, :])
    s = np.arange(NS)
    fresh = log_count(rows[:, None, None] - (WIN + s % DT)[None, None, :])
    own = (s // DT)[None, None, :] == np.arange(DB)[None, :, None]
    fresh = np.where(own, np.broadcast_to(fresh, (NS, DB, NS)), NEG)
    new = np.where((s[:, None] // DT == np.arange(DB)[None, :])[:, :, None]
                   & ((s % DT)[:, None, None] < np.tile(t, H)[None, None, :]), 0.0, NEG)
    pos = np.zeros((NT, P), np.float32)
    pos[:4] = np.arange(SEQ).reshape(4, P)
    pos[4, :NS] = PAST + s % DT
    inv = np.float32(10000.0) ** (-np.arange(HD // 2, dtype=np.float32) / np.float32(HD // 2))
    ang = (pos[:, :, None] * inv[None, None, :]).astype(np.float32).transpose(1, 0, 2)
    f = lambda a: np.ascontiguousarray(a.astype(np.float32))
    return {
        "square": f(square),
        "count_prompt": f(prompt.reshape(P, -1)),
        "count_window": f(window),
        "count_fresh": f(fresh.reshape(NS, -1)),
        "mask_new": f(new.reshape(NS, -1)),
        "cosine": f(np.cos(ang).reshape(P, -1)),
        "sine": f(np.sin(ang).reshape(P, -1)),
    }


class Steps:

    def __init__(self, eng, sem):
        self.eng, self.sem, self.base, self.n = eng, sem, 0, 0

    def do(self, ins):
        ins.then_inc(self.sem, 1)
        self.n += 1

    def wait(self, back=0):
        self.eng.wait_ge(self.sem, self.base + (self.n - back))

    def link(self, ins):
        self.do(ins)
        self.wait()

    def enter(self, i, per_turn):
        self.start, self.per_turn = self.n, per_turn
        self.base = i * per_turn

    def leave(self, turns):
        assert self.n - self.start == self.per_turn, (self.n - self.start, self.per_turn)
        self.base, self.n = 0, self.start + turns * self.per_turn


def build(nc, x_prompt, x_sample, cache_k_sb, cache_v_sb, page_table, state_k_win, state_v_win,
          w_in, w_out, sb_logit_bias, ln1_g, ln1_b, peer_wq, peer_subkeys, peer_u, peer_v, ln2_g, ln2_b,
          square, count_prompt, count_window, count_fresh, mask_new, cosine, sine,
          y_prompt, y_sample, k_sb_prompt, v_sb_prompt, k_sb_sample, v_sb_sample,
          k_win_prompt, v_win_prompt, k_win_sample, v_win_sample):
    with ExitStack() as ctx:
        kept = ctx.enter_context(nc.sbuf_tensor("kept", [P, KEPT], F32))
        pages_sb = ctx.enter_context(nc.sbuf_tensor("pages_sb", [1, DB * PAGES], I32))
        psum = ctx.enter_context(nc.psum_tensor("psum", [P, 8 * BANK], F32))
        gates_dram = nc.dram_tensor("gates_dram", [NCHUNK, P, NK * CHUNK], F32).ap()

        made = {}

        def sem(name):
            if name not in made:
                made[name] = ctx.enter_context(nc.semaphore(name))
            return made[name]

        place, era, era_tensor = [0], ExitStack(), [None]

        def take_in(stack, name, cols):
            era_tensor[0] = stack.enter_context(nc.sbuf_tensor(name, [P, cols], F32)), cols, place[0]

        def open_era(name, cols):
            era.close()
            place[0] = KEPT
            take_in(era, name, cols)

        def take(cols, at=None):
            if at is not None:
                place[0] = at
            o = place[0]
            place[0] = o + cols
            if place[0] <= KEPT:
                return kept[:, o:o + cols]
            tensor, size, base = era_tensor[0]
            assert o >= base and place[0] <= base + size, (o, place[0], base, size)
            return tensor[:, o - base:o - base + cols]

        def bank(b, n=1):
            return psum[:, b * BANK:(b + n) * BANK]

        x_nat = take(NT * D).rearrange("p (t d) -> p t d", t=NT)
        sq = take(5 * P)
        ident, tri, ones, diag, iota = (sq[:, i * P:(i + 1) * P] for i in range(5))
        small = take(384)
        o_t = take(KD * NP).rearrange("p (c n) -> p c n", c=KD)
        ERA = place[0]
        assert ERA == KEPT
        open_era("attention", ATTENTION)
        attention_tensor = era_tensor[0][0]
        v_n = {k: take(NT * DH).rearrange("p (t d) -> p t d", t=NT) for k in ("sb", "dil")}
        q_s = {k: take(H * NS).rearrange("p (h s) -> p h s", h=H) for k in ("sb", "dil")}
        k_s = {k: take(NPAIR * NS).rearrange("p (c s) -> p c s", c=NPAIR) for k in ("sb", "dil")}
        q_wide = take(NPAIR * DB * NS).rearrange("p (c b n) -> p c b n", c=NPAIR, b=DB)
        SAMPLE = place[0]
        assert SAMPLE == KEPT + ATTENTION
        work_era = ExitStack()
        take_in(work_era, "prompt", ALL_COLUMNS - SAMPLE - PROJ_R)
        q_z = {k: take(H * N).rearrange("p (h n) -> p h n", h=H) for k in ("sb", "dil")}
        k_t = {k: take(NPAIR * N).rearrange("p (c n) -> p c n", c=NPAIR) for k in ("sb", "dil")}
        WORK = place[0]

        over = sem("stage_over")
        stage = {}

        def end_stage(eng):
            name = eng.engine
            stage[name] = stage.get(name, 0) + 1
            eng.drain().then_inc(over, 1)
            eng.wait_ge(over, 5 * stage[name])

        programs = {"sp": [], "pe": [], "act": [], "dve": [], "pool": []}

        def part(engine):
            return programs[engine].append
        steps = {}

        def own_steps(eng, name):
            if name not in steps:
                steps[name] = Steps(eng, sem(f"{name}_step"))
            return steps[name]

        WC = DH // 2
        w_sb = [take(KD // 2 * WC, WORK + e * KD // 2 * WC).rearrange("p (k c) -> p k c", c=WC) for e in range(2)]
        proj_tensor = work_era.enter_context(nc.sbuf_tensor("projection_parts", [P, PROJ_R], F32R))
        x_r = proj_tensor[:, 0:2 * KD * N].rearrange("p (s k n) -> p s k n", s=2, k=KD)
        w_in_r = [proj_tensor[:, 2 * KD * (N + e * WC):2 * KD * (N + (e + 1) * WC)].rearrange("p (s k c) -> p s k c", s=2, k=KD)
               for e in range(2)]
        rope_a = attention_tensor[:, 2 * NT * DH:2 * NT * DH + NT * H * 32]
        rope_b = take(NT * H * 32, ERA - KD * NP)
        cos_sb, sin_sb = take(NT * 32), take(NT * 32)
        staged = [v_n["dil"], take(NT * DH).rearrange("p (t c) -> p t c", t=NT)]
        assert place[0] <= ERA
        GROUPS = ("q_sb", "k_sb", "q_dil", "k_dil", "v_sb", "v_dil")
        COLUMN = {"q_sb": 0, "k_sb": 1, "v_sb": 2, "q_dil": 3, "k_dil": 4, "v_dil": 5}
        x_rows = x_prompt.rearrange("b (t p) d -> p (b t) d", p=P)
        xs_rows = x_sample.rearrange("b t d -> (b t) d")
        w_in_g = w_in.rearrange("(e k p) (g c) -> g e p k c", e=2, p=P, c=WC)
        NG_IN = 2 * len(GROUPS)

        def rows_of(t):
            return P if t < NT - 1 else NS

        def proj_out(c, half, t):
            kind = GROUPS[c].split("_")[1]
            to = v_n[kind] if GROUPS[c][0] == "v" else staged[c % 2]
            return to[0:rows_of(t), t, half * WC:(half + 1) * WC]

        @part("sp")
        def _(sp):
            sp.dma_start(x_nat[:, 0:4, :], x_rows).then_inc(sem("x_prompt_in"), 16)
            sp.wait_ge(sem("tail_cleared"), 1)
            sp.dma_start(x_nat[0:NS, 4, :], xs_rows).then_inc(sem("small_in"), 16)
            sp.dma_start(sq, square).then_inc(sem("square_in"), 16)
            sp.dma_start(cos_sb, cosine).then_inc(sem("angles_in"), 16)
            sp.dma_start(sin_sb, sine).then_inc(sem("angles_in"), 16)
            sp.dma_start(pages_sb[:, :], page_table.rearrange("b j -> (b j)").rearrange("(o n) -> o n", o=1))\
              .then_inc(sem("pages_in"), 16)
            for g in range(NG_IN):
                for e in range(2):
                    if g >= 1:
                        sp.wait_ge(sem("w_low"), 2 * (g - 1) + e + 1)
                    sp.dma_start(w_sb[e], w_in_g[2 * COLUMN[GROUPS[g // 2]] + g % 2, e]).then_inc(sem(f"w_in_{e}"), 16)

        @part("pool")
        def _(pool):
            def rows_out(tile, prompt, sample, name, ready, value):
                pool.wait_ge(sem(ready), value)
                pool.dma_start(prompt, tile[:, 0:4, :]).then_inc(sem(f"{name}_out"), 16)
                if name in ("k_sb", "v_sb"):
                    pool.dma_start(sample, tile[0:NS, 4, :]).then_inc(sem(f"{name}_out"), 16)
                else:
                    for b in range(DB):
                        pool.dma_start(sample[b], tile[b * DT:(b + 1) * DT, 4, :])\
                            .then_inc(sem(f"{name}_out"), 16)

            flat = "b (t p) h d -> p (b t) (h d)"
            pages = "b t p h d -> p (b t) (h d)"
            rows_out(staged[1], k_sb_prompt.rearrange(pages), k_sb_sample.rearrange("b t h d -> (b t) (h d)"),
                     "k_sb", "proj_copied", 10 * 2)
            rows_out(staged[1], k_win_prompt.rearrange(flat, p=P),
                     k_win_sample.rearrange("b w h d -> b w (h d)")[:, WIN - DT:WIN, :], "k_dil", "roped", 2)
            rows_out(v_n["sb"], v_sb_prompt.rearrange(pages), v_sb_sample.rearrange("b t h d -> (b t) (h d)"),
                     "v_sb", "proj_copied", 10 * 5)
            rows_out(v_n["dil"], v_win_prompt.rearrange(flat, p=P),
                     v_win_sample.rearrange("b w h d -> b w (h d)")[:, WIN - DT:WIN, :], "v_dil", "proj_copied", 10 * 6)
            pool.wait_ge(sem("k_sb_out"), 2 * 16)
            pool.wait_ge(sem("k_dil_out"), (1 + DB) * 16)

        @part("pe")
        def _(pe):
            pe.wait_ge(sem("square_in"), 16)
            for t in range(NT):
                pe.wait_ge(sem("x_prompt_in" if t < 4 else "small_in"), 16)
                r = rows_of(t)
                for half in range(2):
                    u = 2 * t + half
                    if u >= 4:
                        pe.wait_ge(sem("x_low"), u - 3)
                    for k in range(4):
                        last = pe.transpose(bank(u % 4)[:, k * P:k * P + r],
                                            x_nat[0:r, t, (4 * half + k) * P:(4 * half + k + 1) * P],
                                            ident[0:r, 0:r])
                    last.then_inc(sem("x_t_ready"), 1)
            pe.wait_ge(sem("x_low"), 10)

            def turn(c, tiles):
                if c < 2:
                    pe.wait_ge(sem("proj_copied"), 10 * c + 10)
                else:
                    pe.wait_ge(sem("roped"), c - 1)
                for t in tiles:
                    v = 5 * c + t
                    if v >= 4:
                        pe.wait_ge(sem("qk_copied_dve"), v - 3)
                        if (v - 4) // 5 % 2 == 0:
                            pe.wait_ge(sem("q_copied_act"), 5 * ((v - 4) // 10) + (v - 4) % 5 + 1)
                    r = rows_of(t)
                    for pair in range(NPAIR):
                        last = pe.transpose(bank(4 + v % 4)[:, pair * P:pair * P + r],
                                            staged[c % 2][0:r, t, pair * P:(pair + 1) * P], ident[0:r, 0:r])
                    last.then_inc(sem("qk_ready"), 1)

            for c in range(len(GROUPS)):
                for g in (2 * c, 2 * c + 1):
                    pe.wait_ge(sem("w_low"), 2 * g + 2)
                    for t in range(NT):
                        u = NT * g + t
                        if u >= 4:
                            pe.wait_ge(sem("proj_copied"), u - 3)
                        r = rows_of(t)
                        n = 0
                        for k in range(KD):
                            for x, y in PARTS:
                                n += 1
                                last = pe.matmul(bank(u % 4)[0:r, 0:WC], lhsT=x_r[:, x, k, t * P:t * P + r],
                                                 rhs=w_in_r[g % 2][:, y, k, :], start=(n == 1), stop=(n == 3 * KD))
                        last.then_inc(sem("proj_ready"), 1)
                        if t == 1 and g % 2 == 0 and 2 <= c <= 5:
                            turn(c - 2, (NT - 1,))
                if 1 <= c <= 4:
                    turn(c - 1, range(NT - 1))

        @part("act")
        def _(act):
            for t in range(NT):
                r = rows_of(t)
                for half in range(2):
                    u = 2 * t + half
                    act.wait_ge(sem("x_t_ready"), u + 1)
                    act.activation(x_r[:, 0, 4 * half:4 * half + 4, t * P:t * P + r],
                                   bank(u % 4).rearrange("p (k n) -> p k n", k=4)[:, :, 0:r], ACT.Copy)\
                        .then_inc(sem("x_high"), 1)
            act.wait_ge(sem("staged_cleared"), 7)

            def w_high(g):
                if g < NG_IN:
                    for e in range(2):
                        act.wait_ge(sem(f"w_in_{e}"), 16 * (g + 1))
                        if g >= 2:
                            act.wait_ge(sem("proj_ready"), NT * (g - 1))
                        act.activation(w_in_r[g % 2][:, 0, 4 * e:4 * e + 4, :], w_sb[e], ACT.Copy).then_inc(sem("w_high"), 1)

            def q_copy(c):
                kind = GROUPS[c].split("_")[1]
                for t in range(NT):
                    v = 5 * c + t
                    act.wait_ge(sem("qk_ready"), v + 1)
                    r = rows_of(t)
                    src = bank(4 + v % 4).rearrange("p (c n) -> p c n", c=NPAIR)[0:64, :, 0:r]
                    act.activation(q_z[kind].rearrange("p (c e) n -> p c e n", e=2)[0:64, :, 0, t * P:t * P + r],
                                   src, ACT.Copy).then_inc(sem("q_copied_act"), 1)

            w_high(0)
            w_high(1)
            for c in range(len(GROUPS)):
                if c in (2, 3):
                    act.wait_ge(sem("qk_ready"), 5 * (c - 1))
                if c == 3:
                    act.wait_ge(sem("k_sb_out"), 2 * 16)
                if c == 5:
                    act.wait_ge(sem("qk_ready"), 5 * 3)
                for g in (2 * c, 2 * c + 1):
                    for t in range(NT):
                        u = NT * g + t
                        act.wait_ge(sem("proj_ready"), u + 1)
                        act.activation(proj_out(c, g % 2, t), bank(u % 4)[0:rows_of(t), 0:WC], ACT.Copy)\
                            .then_inc(sem("proj_copied"), 1)
                    w_high(g + 2)
                if c in (1, 3):
                    q_copy(c - 1)

        @part("dve")
        def _(dve):
            dve.memset(x_nat[:, 4, :], 0.0).then_inc(sem("tail_cleared"), 1)
            dve.memset(staged[1][:, 4, :], 0.0).then_inc(sem("staged_cleared"), 1)
            for kind in ("sb", "dil"):
                dve.memset(v_n[kind][:, 4, :], 0.0).then_inc(sem("staged_cleared"), 1)
            for kind in ("sb", "dil"):
                halves = q_z[kind].rearrange("p (c e) n -> p c e n", e=2)
                dve.memset(halves[64:128, :, 0, :], 0.0).then_inc(sem("staged_cleared"), 1)
                dve.memset(halves[0:64, :, 1, :], 0.0).then_inc(sem("staged_cleared"), 1)

            def qk_copy(c):
                kind = GROUPS[c].split("_")[1]
                for t in range(NT):
                    v = 5 * c + t
                    dve.wait_ge(sem("qk_ready"), v + 1)
                    r = rows_of(t)
                    src = bank(4 + v % 4).rearrange("p (c n) -> p c n", c=NPAIR)[:, :, 0:r]
                    if GROUPS[c][0] == "k":
                        dve.tensor_copy(k_t[kind][:, :, t * P:t * P + r], src).then_inc(sem("qk_copied_dve"), 1)
                    else:
                        to = q_z[kind].rearrange("p (c e) n -> p c e n", e=2)
                        dve.tensor_copy(to[64:128, :, 1, t * P:t * P + r], src[64:128]).then_inc(sem("qk_copied_dve"), 1)

            st = own_steps(dve, "dve")

            def rope(c):
                dve.wait_ge(sem("proj_copied"), 10 * c + 10)
                x = staged[c % 2].rearrange("p t (h e d) -> p t h e d", e=2, d=32)
                x1, x2 = x[:, :, :, 0, :], x[:, :, :, 1, :]
                ta, tb = (a.rearrange("p (t h d) -> p t h d", t=NT, h=H) for a in (rope_a, rope_b))
                cos, sin = (a.rearrange("p (t o d) -> p t o d", t=NT, o=1).to_broadcast([P, NT, H, 32])
                            for a in (cos_sb, sin_sb))
                st.do(dve.tensor_tensor(ta, x1, cos, ALU.mult))
                st.link(dve.tensor_tensor(tb, x2, sin, ALU.mult))
                st.do(dve.tensor_tensor(rope_a, rope_a, rope_b, ALU.subtract))
                st.link(dve.tensor_tensor(x1, x1, sin, ALU.mult))
                st.link(dve.tensor_tensor(tb, x2, cos, ALU.mult))
                st.link(dve.tensor_tensor(x2, x1, tb, ALU.add))
                dve.tensor_copy(x1, ta).then_inc(sem("roped"), 1)

            def w_low(g):
                if g < NG_IN:
                    for e in range(2):
                        dve.wait_ge(sem("w_high"), 2 * g + e + 1)
                        ks = slice(4 * e, 4 * e + 4)
                        dve.tensor_tensor(w_in_r[g % 2][:, 1, ks, :], w_sb[e], w_in_r[g % 2][:, 0, ks, :], ALU.subtract)\
                            .then_inc(sem("w_low"), 1)

            for u in range(2 * NT):
                dve.wait_ge(sem("x_high"), u + 1)
                ks, cols = slice(4 * (u % 2), 4 * (u % 2) + 4), slice(u // 2 * P, u // 2 * P + rows_of(u // 2))
                dve.tensor_tensor(x_r[:, 1, ks, cols], bank(u % 4).rearrange("p (k n) -> p k n", k=4)[:, :, 0:rows_of(u // 2)],
                                  x_r[:, 0, ks, cols], ALU.subtract).then_inc(sem("x_low"), 1)
            w_low(0)
            w_low(1)
            dve.wait_ge(sem("angles_in"), 2 * 16)
            for c in range(5):
                w_low(2 * c + 2)
                w_low(2 * c + 3)
                if c >= 1:
                    qk_copy(c - 1)
                if c in (2, 3):
                    rope(c)
            dve.wait_ge(sem("q_copied_act"), 10)
            dve.wait_ge(sem("qk_copied_dve"), 20)
            dve.wait_ge(sem("roped"), 2)
            for kind in ("sb", "dil"):
                dve.tensor_copy(q_s[kind], q_z[kind][:, :, SEQ:N]).then_inc(sem("sample_apart"), 1)
                dve.tensor_copy(k_s[kind], k_t[kind][:, :, SEQ:N]).then_inc(sem("sample_apart"), 1)
            st.link(dve.memset(q_wide, 0.0))
            dve.wait_ge(sem("sample_apart"), 4)
            for pair in range(NPAIR):
                for e in range(2):
                    h = 2 * pair + e
                    dve.tensor_copy(q_wide[:, pair, :, h * DT:(h + 1) * DT],
                                    q_s["dil"][:, h, :].rearrange("p (b t) -> p b t", t=DT))
        for engine in programs:
            programs[engine].append(end_stage)

        KB = SEQ // P
        AT = (0, 512, 1024, 896)
        WIDE = 1280
        work_era.close()
        place[0] = SAMPLE
        take_in(work_era, "prompt_attention", ALL_COLUMNS - SAMPLE)
        place[0] = WORK
        sb_z = [take(WIDE) for _ in range(3)]
        sb_e = [take(WIDE) for _ in range(2)]
        sb_p = [take(WIDE) for _ in range(2)]
        o_nat = take(4 * D).rearrange("p (t d) -> p t d", t=4)
        counts = take(4 * SEQ).rearrange("p (t k) -> p t k", t=4)
        bias = small[:, 0:8]
        bias_ht = small[:, 8:40].rearrange("p (h t) -> p h t", h=H)

        def region(kb):
            return slice(AT[kb], AT[kb] + SEQ - kb * P)

        @part("sp")
        def _(sp):
            sp.dma_start(bias, sb_logit_bias.rearrange("(o h) -> o h", o=1).to_broadcast([P, H]))\
              .then_inc(sem("counts_in"), 16)
            sp.dma_start(counts, count_prompt.rearrange("p (t k) -> p t k", t=4)).then_inc(sem("counts_in"), 16)

        @part("pool")
        def _(pool):
            pool.wait_ge(sem("v_sb_out"), 2 * 16)
            pool.wait_ge(sem("v_dil_out"), (1 + DB) * 16)

        @part("pe")
        def _(pe):
            def scores(h):
                if h >= 1:
                    pe.wait_ge(sem("sb_logits"), h)
                for kb in range(KB):
                    r = region(kb)
                    pe.matmul(psum[:, r], lhsT=k_t["sb"][:, h // 2, kb * P:(kb + 1) * P],
                              rhs=q_z["sb"][:, h, kb * P:SEQ], start=True, stop=False)
                    last = pe.matmul(psum[:, r.start:r.start + P], lhsT=ident, rhs=diag, start=False, stop=True)
                last.then_inc(sem("sb_scores"), 1)

            def weigh(h):
                pe.wait_ge(sem("sb_weights"), h + 1)
                if h >= 2:
                    pe.wait_ge(sem("sb_out_copied"), h - 1)
                out = bank(6 + h % 2)
                for qb in range(KB):
                    for kb in range(qb + 1):
                        a = AT[kb] + (qb - kb) * P
                        last = pe.matmul(out[:, qb * HD:(qb + 1) * HD], lhsT=sb_z[h % 3][:, a:a + P],
                                         rhs=v_n["sb"][:, kb, h * HD:(h + 1) * HD], start=(kb == 0), stop=(kb == qb))
                last.then_inc(sem("sb_out"), 1)

            scores(0)
            for h in range(H):
                if h + 1 < H:
                    scores(h + 1)
                pe.wait_ge(sem("sb_softplus"), h + 1)
                if h >= 1:
                    pe.wait_ge(sem("sb_exponents"), h)
                sp_h = sb_p[h % 2]
                for kb in range(KB):
                    r = region(kb)
                    last = pe.matmul(bank(3, 3)[:, r], lhsT=tri, rhs=sp_h[:, r], start=True, stop=(kb == KB - 1))
                    for later in range(kb + 1, KB):
                        a = r.start + (later - kb) * P
                        last = pe.matmul(bank(3, 3)[:, a:r.stop], lhsT=ones, rhs=sp_h[:, region(later)],
                                         start=False, stop=(later == KB - 1))
                last.then_inc(sem("sb_sums"), 1)
                if h >= 1:
                    weigh(h - 1)
            weigh(H - 1)

        @part("act")
        def _(act):
            st = own_steps(act, "act")

            def log_part(h):
                e = sb_e[h % 2]
                act.wait_ge(sem("sb_logits"), h + 1)
                if h >= 2:
                    act.wait_ge(sem("sb_softplus"), h - 1)
                st.link(act.activation(e, sb_z[h % 3], ACT.Abs))
                st.link(act.activation(e, e, ACT.Exp, scale=-1.0))
                act.activation(e, e, ACT.Ln, bias=1.0).then_inc(sem("sb_log"), 1)

            def out(h):
                act.wait_ge(sem("sb_out"), h + 1)
                act.activation(o_nat[:, :, h * HD:(h + 1) * HD],
                               bank(6 + h % 2)[:, 0:KB * HD].rearrange("p (t d) -> p t d", t=KB), ACT.Copy)\
                    .then_inc(sem("sb_out_copied"), 1)

            log_part(0)
            for h in range(H):
                if h + 1 < H:
                    log_part(h + 1)
                act.wait_ge(sem("sb_exponents"), h + 1)
                act.activation(sb_z[h % 3], sb_z[h % 3], ACT.Exp).then_inc(sem("sb_weights"), 1)
                if h >= 1:
                    out(h - 1)
            out(H - 1)

        @part("dve")
        def _(dve):
            dve.wait_ge(sem("counts_in"), 2 * 16)

            def logits(h):
                dve.wait_ge(sem("sb_scores"), h + 1)
                if h >= 3:
                    dve.wait_ge(sem("sb_out"), h - 2)
                dve.tensor_scalar(sb_z[h % 3], psum[:, 0:WIDE], SCALE, bias[:, h:h + 1], ALU.mult, ALU.add)\
                    .then_inc(sem("sb_logits"), 1)

            def softplus(h):
                dve.wait_ge(sem("sb_log"), h + 1)
                dve.wait_ge(sem("sb_logits"), h + 1)
                if h >= 2:
                    dve.wait_ge(sem("sb_sums"), h - 1)
                dve.scalar_tensor_tensor(sb_p[h % 2], sb_z[h % 3], 0.0, sb_e[h % 2], ALU.max, ALU.add)\
                    .then_inc(sem("sb_softplus"), 1)

            logits(0)
            softplus(0)
            for h in range(H):
                if h + 1 < H:
                    logits(h + 1)
                dve.wait_ge(sem("sb_sums"), h + 1)
                dve.tensor_tensor(sb_z[h % 3], sb_z[h % 3], bank(3, 3)[:, 0:WIDE], ALU.subtract)\
                    .then_inc(sem("sb_exponents"), 1)
                if h + 1 < H:
                    softplus(h + 1)

        for engine in programs:
            programs[engine].append(end_stage)

        PT_AT = (0, 1, 3, 6)
        dl_p = [take(WIDE, WORK)] + [take(WIDE)]
        dl_t = [take(WIDE) for _ in range(2)]
        dl_max, dl_neg, dl_sum, dl_inv = ([small[:, 64 + 16 * i + 4 * e:68 + 16 * i + 4 * e] for e in range(2)]
                                          for i in range(4))
        assert place[0] <= WORK + 6 * WIDE

        @part("pe")
        def _(pe):
            def scores(h):
                if h >= 1:
                    pe.wait_ge(sem("dl_logits"), 4 * h)
                for qb in range(KB):
                    last = pe.matmul(bank(qb)[:, 0:(qb + 1) * P], lhsT=q_z["dil"][:, h, qb * P:(qb + 1) * P],
                                     rhs=k_t["dil"][:, h // 2, 0:(qb + 1) * P], start=True, stop=True)
                last.then_inc(sem("dl_scores"), 1)

            def weigh(h):
                pe.wait_ge(sem("dl_turned"), h + 1)
                if h >= 1:
                    pe.wait_ge(sem("dl_out_scaled"), h)
                for qb in range(KB):
                    for kb in range(qb + 1):
                        a = (PT_AT[qb] + kb) * P
                        c = qb * HD
                        last = pe.matmul(bank(7)[:, c:c + HD], lhsT=dl_t[h % 2][:, a:a + P],
                                         rhs=v_n["dil"][:, kb, h * HD:(h + 1) * HD], start=(kb == 0), stop=(kb == qb))
                last.then_inc(sem("dl_out"), 1)

            scores(0)
            for h in range(H):
                if h + 1 < H:
                    scores(h + 1)
                pe.wait_ge(sem("dl_exp"), 4 * h + 4)
                if h >= 1:
                    pe.wait_ge(sem("dl_turned"), h)
                for j in range(10):
                    last = pe.transpose(bank(4, 3)[:, j * P:(j + 1) * P], dl_p[h % 2][:, j * P:(j + 1) * P], ident)
                last.then_inc(sem("dl_turn"), 1)
                if h >= 1:
                    weigh(h - 1)
            weigh(H - 1)

        @part("act")
        def _(act):
            def exps(h):
                act.wait_ge(sem("dl_neg"), h + 1)
                for qb in range(KB):
                    a = PT_AT[qb] * P
                    x = dl_p[h % 2][:, a:a + (qb + 1) * P]
                    act.activation(x, x, ACT.Exp, bias=dl_neg[h % 2][:, qb:qb + 1],
                                   accum_out=dl_sum[h % 2][:, qb:qb + 1]).then_inc(sem("dl_exp"), 1)

            exps(0)
            for h in range(H):
                if h + 1 < H:
                    exps(h + 1)
                act.wait_ge(sem("dl_turn"), h + 1)
                if h >= 2:
                    act.wait_ge(sem("dl_out"), h - 1)
                act.activation(dl_t[h % 2], bank(4, 3)[:, 0:WIDE], ACT.Copy).then_inc(sem("dl_turned"), 1)

        @part("dve")
        def _(dve):
            dve.wait_ge(sem("counts_in"), 2 * 16)

            def logits(h):
                dve.wait_ge(sem("dl_scores"), h + 1)
                if h >= 2:
                    dve.wait_ge(sem("dl_turn"), h - 1)
                for qb in range(KB):
                    a, w = PT_AT[qb] * P, (qb + 1) * P
                    dve.tensor_tensor_reduce(out=dl_p[h % 2][:, a:a + w], in0=bank(qb)[:, 0:w], in1=counts[:, qb, 0:w],
                                             scale=SCALE, scalar=LOWEST, op0=ALU.add, op1=ALU.max,
                                             accum_out=dl_max[h % 2][:, qb:qb + 1]).then_inc(sem("dl_logits"), 1)
                dve.wait_ge(sem("dl_logits"), 4 * h + 4)
                dve.tensor_scalar(dl_neg[h % 2], dl_max[h % 2], -1.0, None, ALU.mult).then_inc(sem("dl_neg"), 1)

            def scale(h):
                dve.wait_ge(sem("dl_inverse"), h + 1)
                dve.wait_ge(sem("dl_out"), h + 1)
                dve.tensor_tensor(o_nat[:, :, DH + h * HD:DH + (h + 1) * HD],
                                  bank(7)[:, 0:KB * HD].rearrange("p (t d) -> p t d", t=KB),
                                  dl_inv[h % 2].rearrange("p (t o) -> p t o", o=1).to_broadcast([P, KB, HD]), ALU.mult)\
                    .then_inc(sem("dl_out_scaled"), 1)

            logits(0)
            for h in range(H):
                if h + 1 < H:
                    logits(h + 1)
                dve.wait_ge(sem("dl_exp"), 4 * h + 4)
                if h >= 2:
                    dve.wait_ge(sem("dl_out_scaled"), h - 1)
                dve.reciprocal(dl_inv[h % 2], dl_sum[h % 2]).then_inc(sem("dl_inverse"), 1)
                if h >= 1:
                    scale(h - 1)
            scale(H - 1)

        @part("pe")
        def _(pe):
            pe.wait_ge(sem("dl_out_scaled"), H)
            for t in range(4):
                for half in range(2):
                    u = 2 * t + half
                    if u >= 4:
                        pe.wait_ge(sem("o_t_copied"), u - 3)
                    for c in range(4):
                        last = pe.transpose(bank(u % 4)[:, c * P:(c + 1) * P],
                                            o_nat[:, t, (4 * half + c) * P:(4 * half + c + 1) * P], ident)
                    last.then_inc(sem("o_t_ready"), 1)

        @part("act")
        def _(act):
            for u in range(8):
                t, half = u // 2, u % 2
                act.wait_ge(sem("o_t_ready"), u + 1)
                act.activation(o_t[:, 4 * half:4 * half + 4, t * P:(t + 1) * P],
                               bank(u % 4).rearrange("p (c n) -> p c n", c=4), ACT.Copy).then_inc(sem("o_t_copied"), 1)

        for engine in programs:
            programs[engine].append(end_stage)

        HT = H * DT
        SW = PAGES * HT
        SUMS_AT, EXP_AT, PV_AT = 4, 5, 8
        V_SLOTS, V_PARTS = 4, 4
        work_era.close()
        take_in(work_era, "sample", ALL_COLUMNS - SAMPLE - SAMPLE_R)
        parts_tensor = work_era.enter_context(nc.sbuf_tensor("sample_parts", [P, SAMPLE_R], F32R))
        at_r = [0]

        def take_s(cols):
            at_r[0] += cols
            return parts_tensor[:, at_r[0] - cols:at_r[0]]

        k_page = [take(DH) for _ in range(K_SLOTS)]
        v_page = [take(DH) for _ in range(V_SLOTS)]
        ss_e = take(SW)
        ss_p, ss_c = take(SW + HT), take(SW + HT)
        ss_z = take(SW + HT)
        new_z, new_e, new_p = (take(DB * HT) for _ in range(3))
        mask_sb = take(DB * HT)
        k_turned = [take(DH).rearrange("p (c n) -> p c n", c=NPAIR) for _ in range(2)]
        pv_rows = take(DH)
        PV_N = 2 * HT + 8
        pv_cols = take(NPAIR * PV_N)
        v_parts = [take_s(2 * DH).rearrange("p (x c) -> p x c", x=2) for _ in range(V_PARTS)]
        v_new_r = take_s(2 * DH).rearrange("p (x c) -> p x c", x=2)
        w_r = take_s(2 * (SW + HT)).rearrange("p (j x n) -> p j x n", j=PAGES + 1, x=2)
        z_pages = ss_z.rearrange("p (j n) -> p j n", j=PAGES + 1)
        cache_k = cache_k_sb.rearrange("g p h d -> g p (h d)")
        cache_v = cache_v_sb.rearrange("g p h d -> g p (h d)")

        def by_b(a):
            return a.rearrange("p (b n) -> p b n", b=DB)

        def over_sequences(eng, turn, st=None, per_turn=0):
            turn(0, True, False)
            with eng.Fori(0, DB - 1) as i:
                if st:
                    st.enter(i, per_turn)
                turn(i + 1, True, True)
                if st:
                    st.leave(DB - 1)
            turn(DB, False, True)

        def values_at(step):
            return range(2 * (step - PV_AT), 2 * (step - PV_AT) + 2) if PV_AT <= step < PAGES else ()

        @part("sp")
        def _(sp):
            sp.dma_start(mask_sb[0:NS, :], mask_new).then_inc(sem("masks_in"), 16)

            def load(b, j, cache, to, free, name):
                g = PAGES * b + j
                page = sp.value_load(pages_sb[0:1, bass.ds(g, 1)], min_val=0, max_val=N_POOL - 1)
                sp.wait_ge(sem(free), g + 1)
                sp.dma_start(to[j % len(to)], cache[bass.ds(page, 1)].rearrange("o p c -> (o p) c"))\
                    .then_inc(sem(f"{name}_{j % len(to)}"), 16)

            def keys(b, j):
                load(b, j, cache_k, k_page, "page_turned", "k_page")

            def values(b, j):
                load(b, j, cache_v, v_page, "page_v_low", "v_page")

            def turn(b, pages, before):
                for s in range(PAGES):
                    if s < PAGES - K_SLOTS and pages:
                        keys(b, K_SLOTS + s)
                    if s >= PAGES - K_SLOTS and pages and not (isinstance(b, int) and b == DB - 1):
                        keys(b + 1, s - (PAGES - K_SLOTS))
                    if before:
                        for j in range(V_SLOTS) if s == 0 else values_at(s + 1):
                            v = j if s == 0 else j + V_SLOTS
                            if v < PAGES:
                                values(b - 1, v)

            sp.wait_ge(sem("pages_in"), 16)
            for j in range(K_SLOTS):
                keys(0, j)
            turn(0, True, False)
            with sp.Fori(0, DB - 2) as i:
                turn(i + 1, True, True)
            turn(DB - 1, True, True)
            turn(DB, False, True)

        @part("pe")
        def _(pe):
            pe.drain().then_inc(sem("page_turned"), K_SLOTS)
            pe.drain().then_inc(sem("page_scored"), 2)
            pe.drain().then_inc(sem("values_used"), V_PARTS)
            pe.drain().then_inc(sem("seq_out"), 1)
            out = by_b(bank(6)[0:NS, 0:DB * HT])
            for pair in range(NPAIR):
                last = pe.matmul(out[:, :, pair * 8:(pair + 1) * 8].rearrange("p b (e t) -> p b e t", e=2),
                                 lhsT=k_s["sb"][:, pair, :],
                                 rhs=q_s["sb"][:, 2 * pair:2 * pair + 2, :].rearrange("p e (b t) -> p b e t", t=DT),
                                 start=True, stop=True)
            last.then_inc(sem("new_scores"), 1)
            pe.wait_ge(sem("new_softplus"), 1)
            pe.matmul(bank(7)[:, 0:DB * HT], lhsT=tri, rhs=new_p, start=True, stop=True).then_inc(sem("new_sums"), 1)

            def turn_page(b, j):
                pe.wait_ge(sem(f"k_page_{j % K_SLOTS}"), 32 * b + 16 * (j // K_SLOTS) + 16)
                pe.wait_ge(sem("page_copied"), PAGES * b + j + 1)
                for pair in range(NPAIR):
                    last = pe.transpose(bank(j % 2)[:, pair * P:(pair + 1) * P],
                                        k_page[j % K_SLOTS][:, pair * P:(pair + 1) * P], ident)
                last.then_inc(sem("page_turned"), 1)

            def score(b, j):
                if j == 0:
                    pe.wait_ge(sem("seq_logits"), 2 * b + 1)
                pe.wait_ge(sem("page_copied"), PAGES * b + j + 3)
                for pair in range(NPAIR):
                    c = j * HT + pair * 8
                    last = pe.matmul(bank(2)[:, c:c + 8].rearrange("p (e t) -> p e t", e=2), lhsT=k_turned[j % 2][:, pair, :],
                                     rhs=q_s["sb"][:, 2 * pair:2 * pair + 2, bass.ds(b * DT, DT)], start=True, stop=True)
                last.then_inc(sem("page_scored"), 1)

            def sums(b):
                pe.wait_ge(sem("seq_suffix"), b + 1)
                pe.matmul(bank(4), lhsT=tri, rhs=ss_p[:, 0:SW], start=True, stop=False)
                pe.matmul(bank(4), lhsT=ones, rhs=ss_c[:, HT:SW + HT], start=False, stop=True).then_inc(sem("seq_sums"), 1)

            def weigh(b, j):
                if j == 0:
                    pe.wait_ge(sem("weights_low"), b + 1)
                    pe.wait_ge(sem("seq_rows"), b + 1)
                if j < PAGES:
                    pe.wait_ge(sem("page_v_low"), PAGES * b + j + V_SLOTS + 1)
                else:
                    pe.wait_ge(sem("new_v_low"), 1)
                v = v_parts[j % V_PARTS] if j < PAGES else v_new_r
                for x in range(2):
                    last = pe.matmul(bank(5)[0:2 * HT, :], lhsT=w_r[:, j].rearrange("p x n -> p (x n)"), rhs=v[:, x, :],
                                     start=(j == 0 and x == 0), stop=(j == PAGES and x == 1))
                last.then_inc(sem("values_used" if j < PAGES else "seq_out"), 1)

            def turn_out(b):
                pe.wait_ge(sem("seq_rows"), b + 2)
                pe.wait_ge(sem("seq_stored"), 2 * b + 1)
                for pair in range(NPAIR):
                    last = pe.transpose(bank(6)[:, pair * P:(pair + 1) * P], pv_rows[:, pair * P:(pair + 1) * P], ident)
                last.then_inc(sem("seq_turned"), 1)

            def turn(b, pages, before):
                for s in range(PAGES):
                    if pages:
                        turn_page(b, s)
                        if s >= 1:
                            score(b, s - 1)
                    if before:
                        if s == SUMS_AT:
                            sums(b - 1)
                        for j in values_at(s):
                            weigh(b - 1, j)
                if before:
                    weigh(b - 1, PAGES)
                if pages:
                    score(b, PAGES - 1)
                if before:
                    turn_out(b - 1)

            over_sequences(pe, turn)

        @part("act")
        def _(act):
            st = own_steps(act, "act")
            act.drain().then_inc(sem("page_copied"), 2)
            act.activation(v_new_r[:, 0, :], v_n["sb"][:, 4, :], ACT.Copy).then_inc(sem("new_v_high"), 1)
            act.wait_ge(sem("new_logits"), 1)
            st.link(act.activation(new_e[0:NS], new_z[0:NS], ACT.Abs))
            st.link(act.activation(new_e[0:NS], new_e[0:NS], ACT.Exp, scale=-1.0))
            act.activation(new_e[0:NS], new_e[0:NS], ACT.Ln, bias=1.0).then_inc(sem("new_log"), 1)
            act.wait_ge(sem("new_exponents"), 1)
            act.activation(new_z[0:NS], new_z[0:NS], ACT.Exp).then_inc(sem("new_weights"), 1)

            def turn(b, pages, before):
                for s in range(PAGES):
                    if pages:
                        act.wait_ge(sem("page_scored"), PAGES * b + s + 1)
                        act.wait_ge(sem("page_turned"), PAGES * b + s + 1 + K_SLOTS)
                        act.activation(k_turned[s % 2], bank(s % 2).rearrange("p (c n) -> p c n", c=NPAIR), ACT.Copy)\
                            .then_inc(sem("page_copied"), 1)
                    if not before:
                        continue
                    if s == 0:
                        act.wait_ge(sem("seq_logits"), 2 * b + 1)
                        st.do(act.activation(ss_e, ss_z[:, 0:SW], ACT.Abs))
                    if s == 1:
                        st.wait()
                        st.do(act.activation(ss_e, ss_e, ACT.Exp, scale=-1.0))
                    if s == 2:
                        st.wait()
                        act.activation(ss_e, ss_e, ACT.Ln, bias=1.0).then_inc(sem("seq_log"), 1)
                    if s == EXP_AT:
                        act.wait_ge(sem("seq_exponents"), b)
                        st.do(act.activation(ss_z[:, 0:SW], ss_z[:, 0:SW], ACT.Exp))
                        act.wait_ge(sem("seq_out"), b)
                        st.wait()
                        act.activation(w_r[:, :, 0, :], z_pages, ACT.Copy)\
                            .then_inc(sem("weights_high"), 1)
                    for j in values_at(s + 1):
                        act.wait_ge(sem("values_used"), PAGES * (b - 1) + j + 1)
                        act.wait_ge(sem(f"v_page_{j % V_SLOTS}"), 16 * PAGES // V_SLOTS * (b - 1) + 16 * (j // V_SLOTS) + 16)
                        act.activation(v_parts[j % V_PARTS][:, 0], v_page[j % V_SLOTS], ACT.Copy).then_inc(sem("page_v_high"), 1)

            over_sequences(act, turn, st, 3)

        @part("dve")
        def _(dve):
            st = own_steps(dve, "dve")
            st.link(dve.tensor_copy(bias_ht, bias.rearrange("p (h o) -> p h o", o=1).to_broadcast([P, H, DT])))
            st.do(dve.memset(new_z, 0.0))
            st.do(dve.memset(new_p, 0.0))
            flat_bias = small[:, 8:40]
            dve.wait_ge(sem("masks_in"), 16)
            st.wait()
            st.link(dve.tensor_tensor(by_b(mask_sb)[0:NS], by_b(mask_sb)[0:NS],
                                      flat_bias[0:NS].rearrange("p (o n) -> p o n", o=1).to_broadcast([NS, DB, HT]), ALU.add))
            st.do(dve.memset(pv_rows, 0.0))
            dve.wait_ge(sem("new_v_high"), 1)
            dve.tensor_tensor(v_new_r[:, 1, :], v_n["sb"][:, 4, :], v_new_r[:, 0, :], ALU.subtract).then_inc(sem("new_v_low"), 1)
            dve.wait_ge(sem("new_scores"), 1)
            dve.scalar_tensor_tensor(new_z[0:NS], bank(6)[0:NS, 0:DB * HT], SCALE, mask_sb[0:NS], ALU.mult, ALU.add)\
                .then_inc(sem("new_logits"), 1)
            dve.wait_ge(sem("new_log"), 1)
            dve.scalar_tensor_tensor(new_p[0:NS], new_z[0:NS], 0.0, new_e[0:NS], ALU.max, ALU.add)\
                .then_inc(sem("new_softplus"), 1)
            dve.wait_ge(sem("new_sums"), 1)
            dve.tensor_tensor(new_z[0:NS], new_z[0:NS], bank(7)[0:NS, 0:DB * HT], ALU.subtract)\
                .then_inc(sem("new_exponents"), 1)
            dve.wait_ge(sem("new_weights"), 1)
            dve.drain().then_inc(sem("page_v_low"), V_SLOTS)
            dve.drain().then_inc(sem("seq_logits"), 1)
            dve.drain().then_inc(sem("seq_rows"), 1)
            dve.drain().then_inc(sem("seq_stored"), 1)

            def logits(b):
                dve.wait_ge(sem("page_scored"), PAGES * b + PAGES + 2)
                dve.scalar_tensor_tensor(ss_z[:, 0:SW].rearrange("p (j n) -> p j n", j=PAGES),
                                         bank(2).rearrange("p (j n) -> p j n", j=PAGES), SCALE,
                                         flat_bias.rearrange("p (o n) -> p o n", o=1).to_broadcast([P, PAGES, HT]),
                                         ALU.mult, ALU.add).then_inc(sem("seq_logits"), 1)
                dve.tensor_scalar(ss_z[:, SW:SW + HT], by_b(new_z)[:, bass.ds(b, 1), :].rearrange("p o n -> p (o n)"),
                                  1.0, None, ALU.mult).then_inc(sem("seq_logits"), 1)

            def turn(b, pages, before):
                for s in range(PAGES):
                    if not before:
                        continue
                    if s == 3:
                        dve.wait_ge(sem("seq_log"), b)
                        dve.wait_ge(sem("seq_logits"), 2 * b + 1)
                        st.do(dve.scalar_tensor_tensor(ss_p[:, 0:SW], ss_z[:, 0:SW], 0.0, ss_e, ALU.max, ALU.add))
                        st.link(dve.tensor_scalar(ss_p[:, SW:SW + HT], by_b(new_p)[:, bass.ds(b - 1, 1), :]
                                                  .rearrange("p o n -> p (o n)"), 1.0, None, ALU.mult))
                        st.do(dve.tensor_copy(ss_c[:, SW:SW + HT], ss_p[:, SW:SW + HT]))
                        st.link(dve.tensor_tensor(ss_c[:, 0:SW], ss_p[:, 0:SW], ss_p[:, HT:SW + HT], ALU.add))
                        for step in (2, 4, 8, 16):
                            w = SW + HT - step * HT
                            ins = dve.tensor_tensor(ss_c[:, 0:w], ss_c[:, 0:w], ss_c[:, step * HT:SW + HT], ALU.add)
                            if step < 16:
                                st.link(ins)
                            else:
                                ins.then_inc(sem("seq_suffix"), 1)
                    if s == SUMS_AT:
                        dve.wait_ge(sem("seq_sums"), b)
                        dve.tensor_tensor(ss_z[:, 0:SW], ss_z[:, 0:SW], bank(4), ALU.subtract).then_inc(sem("seq_exponents"), 1)
                    if s == EXP_AT:
                        dve.wait_ge(sem("weights_high"), b)
                        dve.tensor_tensor(w_r[:, :, 1, :], z_pages, w_r[:, :, 0, :], ALU.subtract)\
                            .then_inc(sem("weights_low"), 1)
                    for j in values_at(s + 1):
                        dve.wait_ge(sem("page_v_high"), PAGES * (b - 1) + j + 1)
                        dve.tensor_tensor(v_parts[j % V_PARTS][:, 1], v_page[j % V_SLOTS], v_parts[j % V_PARTS][:, 0], ALU.subtract)\
                            .then_inc(sem("page_v_low"), 1)
                if before:
                    dve.wait_ge(sem("seq_out"), b + 1)
                    dve.tensor_copy(pv_rows[0:2 * HT], bank(5)[0:2 * HT, :]).then_inc(sem("seq_rows"), 1)
                if pages:
                    logits(b)
                if before:
                    dve.wait_ge(sem("seq_turned"), b)
                    cols = pv_cols.rearrange("p (c n) -> p c n", c=NPAIR)
                    st.link(dve.tensor_copy(pv_cols[:, 0:NPAIR * 2 * HT].rearrange("p (c n) -> p c n", c=NPAIR),
                                            bank(6).rearrange("p (c n) -> p c n", c=NPAIR)[:, :, 0:2 * HT]))
                    for e in range(2):
                        r = slice(64 * e, 64 * e + 64)
                        dve.tensor_tensor(o_t[r, 0:4, bass.ds((b - 1) * DT + SEQ, DT)], cols[r, :, e * DT:(e + 1) * DT],
                                          cols[r, :, HT + e * DT:HT + (e + 1) * DT], ALU.add).then_inc(sem("seq_stored"), 1)

            over_sequences(dve, turn, st, 8)

        for engine in programs:
            programs[engine].append(end_stage)

        KEYS_IN, VALUES_IN = 16 * DB * PAGES // K_SLOTS, 16 * DB * PAGES // V_SLOTS
        WK = NW * P
        work_era.close()
        take_in(work_era, "windows", ALL_COLUMNS - SAMPLE - KD * D)
        wo_tensor = work_era.enter_context(nc.sbuf_tensor("w_out_sb", [P, KD * D], F32))
        wo_sb = wo_tensor[:, :].rearrange("p (k n) -> p k n", k=KD)
        kw = [take(NW * DH).rearrange("p (m c) -> p m c", m=NW) for _ in range(2)]
        vw = [take(NW * DH).rearrange("p (m c) -> p m c", m=NW) for _ in range(2)]
        kw_t = take(NPAIR * WK).rearrange("p (c n) -> p c n", c=NPAIR)
        q_b = take(NPAIR * HT).rearrange("p (c n) -> p c n", c=NPAIR)
        dw_p = take(WK + NS)
        dw_t = take((NW + 1) * HT).rearrange("p (m n) -> p m n", m=NW + 1)
        window_sb = take(WK)
        fresh_sb = take(DB * NS)
        dw_max, dw_top, dw_sum, dw_inv = (small[0:HT, 128 + 4 * i:129 + 4 * i] for i in range(4))
        dw_max2 = small[0:HT, 129:130]

        def over_windows(eng, turn, st=None, per_turn=0):
            turn(0, 0, 0, False)
            with eng.Fori(0, DB // 2 - 1) as i:
                if st:
                    st.enter(i, per_turn)
                turn(2 * i + 1, 1, i, True)
                turn(2 * i + 2, 0, i + 1, True)
                if st:
                    st.leave(DB // 2 - 1)
            turn(DB - 1, 1, DB // 2 - 1, True)

        near_rows = [a.rearrange("b (m p) h d -> b p m (h d)", p=P) for a in (state_k_win, state_v_win)]
        far_rows = [a.rearrange("b (m g s) h d -> b m g s (h d)", g=32, s=16) for a in (state_k_win, state_v_win)]

        @part("sp")
        def _(sp):
            sp.dma_start(window_sb[0:HT, :], count_window).then_inc(sem("masks_in"), 16)
            sp.dma_start(fresh_sb[0:HT, :], count_fresh).then_inc(sem("masks_in"), 16)
            with sp.Fori(0, DB // 2) as i:
                for s in range(2):
                    b = 2 * i + s
                    for x, to, name in ((0, kw, "k"), (1, vw, "v")):
                        sp.wait_ge(sem("kw_turned" if name == "k" else "dw_out"), b + 1)
                        sp.dma_start(to[s][:, 0:NEAR, :],
                                     near_rows[x][bass.ds(b, 1), :, WIN // P - NEAR:WIN // P, :]
                                     .rearrange("o p m c -> (o p) m c")).then_inc(sem(f"{name}_page_{s}"), 16)
                        for m in range(FAR):
                            sp.dma_start(to[s][:, NEAR + m, :],
                                         far_rows[x][bass.ds(b, 1), m, :, 0:DT, :].rearrange("o g s c -> (o g) s c"))\
                                .then_inc(sem(f"{name}_page_{s}"), 16)
            sp.dma_start(wo_sb, w_out.rearrange("(k p) n -> p k n", p=P)).then_inc(sem("w_out_in"), 16)

        @part("pe")
        def _(pe):
            pe.drain().then_inc(sem("kw_turned"), 2)
            pe.drain().then_inc(sem("dw_out"), 2)
            pe.drain().then_inc(sem("dw_scores"), 1)

            def turn_keys(b, s, i):
                pe.wait_ge(sem(f"k_page_{s}"), KEYS_IN + 64 * i + 64)
                for m in range(NW):
                    pe.wait_ge(sem(f"kw_copied_{m % 2}"), (4 - m % 2) * b + m // 2 + 1)
                    for pair in range(NPAIR):
                        last = pe.transpose(bank(m % 2)[:, pair * P:(pair + 1) * P],
                                            kw[s][:, m, pair * P:(pair + 1) * P], ident)
                    last.then_inc(sem("kw_turned" if m == NW - 1 else "kw_turn"), 1)

            def scores(b):
                pe.wait_ge(sem("kw_copied_0"), 4 * b + 5)
                pe.wait_ge(sem("kw_copied_1"), 3 * b + 4)
                pe.wait_ge(sem("q_b_ready"), b + 1)
                pe.wait_ge(sem("dw_logits"), 2 * b + 2)
                for a, w in ((0, BANK), (BANK, WK - BANK), (WK, NS)):
                    for pair in range(NPAIR):
                        rhs = kw_t[:, pair, a:a + w] if a < WK else k_s["dil"][:, pair, :]
                        last = pe.matmul(bank(2, 2)[0:HT, a:a + w], lhsT=q_b[:, pair, :], rhs=rhs,
                                         start=(pair == 0), stop=(pair == NPAIR - 1))
                last.then_inc(sem("dw_scores"), 1)

            def weigh(b, s, i):
                pe.wait_ge(sem("dw_scaled"), b + 1)
                for m in range(NW + 1):
                    w = P if m < NW else NS
                    last = pe.transpose(bank(6, 2)[0:w, m * P:(m + 1) * P], dw_p[:, m * P:m * P + w], ident)
                last.then_inc(sem("dw_turn"), 1)
                pe.wait_ge(sem("dw_turned"), b + 1)
                pe.wait_ge(sem(f"v_page_{s}"), VALUES_IN + 64 * i + 64)
                pe.wait_ge(sem("dw_stored"), 2 * b + 1)
                for m in range(NW + 1):
                    v = vw[s][:, m, :] if m < NW else v_n["dil"][:, 4, :]
                    for pair in range(NPAIR):
                        last = pe.matmul(bank(5)[:, pair * 8:pair * 8 + 8], lhsT=v[:, pair * P:(pair + 1) * P],
                                         rhs=dw_t[:, m, pair * 8:pair * 8 + 8],
                                         start=(m == 0 and pair == 0), stop=(m == NW), skip_group_check=True)
                last.then_inc(sem("dw_out"), 1)

            def turn(b, s, i, before):
                turn_keys(b, s, i)
                scores(b)
                if before:
                    weigh(b - 1, 1 - s, i if s == 1 else i - 1)

            over_windows(pe, turn)
            weigh(DB - 1, 1, DB // 2 - 1)

        @part("pool")
        def _(pool):
            with pool.Fori(0, DB) as b:
                pool.wait_ge(sem("dw_scores"), b + 1)
                pool.tensor_copy(q_b, q_wide[:, :, bass.ds(b, 1), :].rearrange("p c o n -> p (c o) n"))\
                    .then_inc(sem("q_b_ready"), 1)

        @part("act")
        def _(act):
            act.drain().then_inc(sem("kw_copied_0"), 1)

            def turn(b, s, i, before):
                act.wait_ge(sem("dw_scores"), b + 1)
                for m in range(0, NW, 2):
                    if m < NW - 1:
                        act.wait_ge(sem("kw_turn"), (NW - 1) * b + m + 1)
                    else:
                        act.wait_ge(sem("kw_turned"), b + 3)
                    act.activation(kw_t[:, :, m * P:(m + 1) * P], bank(0).rearrange("p (c n) -> p c n", c=NPAIR),
                                   ACT.Copy).then_inc(sem("kw_copied_0"), 1)
                act.wait_ge(sem("dw_top"), b + 1)
                act.activation(dw_p[0:HT], dw_p[0:HT], ACT.Exp, bias=dw_top, accum_out=dw_sum)\
                    .then_inc(sem("dw_exp"), 1)

            over_windows(act, turn)

        @part("dve")
        def _(dve):
            st = own_steps(dve, "dve")
            st.do(dve.memset(dw_p, 0.0))
            st.link(dve.memset(dw_t, 0.0))
            turned = bank(6, 2).rearrange("p (m n) -> p m n", m=NW + 1)
            dve.drain().then_inc(sem("kw_copied_1"), 1)
            dve.drain().then_inc(sem("dw_logits"), 2)
            dve.drain().then_inc(sem("dw_stored"), 1)
            dve.wait_ge(sem("masks_in"), 3 * 16)

            def normalise(b):
                dve.wait_ge(sem("dw_exp"), b + 1)
                dve.reciprocal(dw_inv, dw_sum).then_inc(sem("dw_inverse"), 1)
                dve.wait_ge(sem("dw_inverse"), b + 1)
                dve.tensor_scalar(dw_p[0:HT], dw_p[0:HT], dw_inv, None, ALU.mult).then_inc(sem("dw_scaled"), 1)

            def copy_turned(b):
                dve.wait_ge(sem("dw_turn"), b + 1)
                dve.tensor_copy(dw_t[:, 0:NW, :], turned[:, 0:NW, 0:HT])
                dve.tensor_copy(dw_t[0:NS, NW, :], turned[0:NS, NW, 0:HT]).then_inc(sem("dw_turned"), 1)

            def logits(b):
                dve.wait_ge(sem("dw_scores"), b + 2)
                st.do(dve.tensor_tensor(dw_p[0:HT, WK:WK + NS], bank(2, 2)[0:HT, WK:WK + NS],
                                        fresh_sb[0:HT, bass.ds(b * NS, NS)], ALU.add))
                dve.tensor_tensor_reduce(out=dw_p[0:HT, 0:WK], in0=bank(2, 2)[0:HT, 0:WK], in1=window_sb[0:HT],
                                         scale=SCALE, scalar=LOWEST, op0=ALU.add, op1=ALU.max, accum_out=dw_max)\
                    .then_inc(sem("dw_logits"), 1)
                st.wait()
                dve.tensor_scalar(dw_p[0:HT, WK:WK + NS], dw_p[0:HT, WK:WK + NS], SCALE, None, ALU.mult)\
                    .then_inc(sem("dw_logits"), 1)
                dve.wait_ge(sem("dw_logits"), 2 * b + 4)
                st.link(dve.tensor_reduce(dw_max2, dw_p[0:HT, WK:WK + NS], AX_X, ALU.max))
                st.link(dve.tensor_tensor(dw_top, dw_max, dw_max2, ALU.max))
                dve.tensor_scalar(dw_top, dw_top, -1.0, None, ALU.mult).then_inc(sem("dw_top"), 1)

            def store(b):
                dve.wait_ge(sem("dw_out"), b + 3)
                out = bank(5)[:, 0:HT].rearrange("p (c n) -> p c n", c=NPAIR)
                for e in range(2):
                    r = slice(64 * e, 64 * e + 64)
                    dve.tensor_scalar(o_t[r, 4:8, bass.ds(b * DT + SEQ, DT)], out[r, :, e * DT:(e + 1) * DT],
                                      1.0, None, ALU.mult).then_inc(sem("dw_stored"), 1)

            def turn(b, s, i, before):
                for m in range(1, NW, 2):
                    dve.wait_ge(sem("kw_turn"), (NW - 1) * b + m + 1)
                    dve.tensor_copy(kw_t[:, :, m * P:(m + 1) * P], bank(1).rearrange("p (c n) -> p c n", c=NPAIR))\
                        .then_inc(sem("kw_copied_1"), 1)
                if before:
                    normalise(b - 1)
                    copy_turned(b - 1)
                logits(b)
                if before:
                    store(b - 1)

            over_windows(dve, turn, st, 6)
            normalise(DB - 1)
            copy_turned(DB - 1)
            store(DB - 1)
            dve.memset(o_t[:, :, N:NP], 0.0).then_inc(sem("pad_cleared"), 1)

        for engine in programs:
            programs[engine].append(end_stage)

        work_era.close()
        era.close()
        h1_r = ctx.enter_context(nc.sbuf_tensor("h1_parts", [P, H1_R], F32R))[:, :]\
            .rearrange("p (s k n) -> p s k n", s=2, k=KD)
        open_era("peer", PEER)
        S_COPY = KEPT + 3 * PH * TK * TK
        row_g, row_b = take(D, S_COPY), take(D)
        stats = small[:, 64:76].rearrange("p (g s) -> p g s", g=2)
        mean_var, deviation, inverse = small[:, 80:82], small[:, 84:85], small[:, 88:89]
        eps = small[:, 92:93]

        def to_rows(a):
            return a.rearrange("(o d) -> o d", o=1).to_broadcast([P, D])

        def layer_norm(dve, st, x, g, b, count, r=P):
            for half in range(2):
                st.do(dve.bn_stats(stats[0:r, half, :], x[:, half * 512:(half + 1) * 512]))
            st.wait()
            dve.bn_aggr(mean_var[0:r], stats[0:r]).then_inc(sem("variance"), 1)
            dve.wait_ge(sem("variance"), count)
            st.do(dve.scalar_tensor_tensor(x, x, mean_var[0:r, 0:1], g[0:r], ALU.subtract, ALU.mult))
            dve.wait_ge(sem("deviation"), count)
            st.link(dve.reciprocal(inverse[0:r], deviation[0:r]))
            dve.scalar_tensor_tensor(x, x, inverse[0:r], b[0:r], ALU.mult, ALU.add).then_inc(sem("normed"), 1)

        @part("sp")
        def _(sp):
            for to, frm in ((row_g, ln1_g), (row_b, ln1_b)):
                sp.dma_start(to, to_rows(frm)).then_inc(sem("norms_in"), 16)
            sp.dma_start(keys_n, peer_subkeys.rearrange("c k d -> k c d")).then_inc(sem("small_in"), 16)
            for g in range(2):
                sp.dma_start(wq_sb[g], wq_g[g]).then_inc(sem(f"w_in_{g}"), 16)

        @part("pe")
        def _(pe):
            pe.wait_ge(sem("w_out_in"), 16)

            def turn(t):
                pe.wait_ge(sem("normed"), t + 1)
                for half in range(2):
                    u = 2 * t + half
                    if u >= 4:
                        pe.wait_ge(sem("h1_low"), u - 3)
                    for k in range(4):
                        last = pe.transpose(bank(4 + u % 4)[:, k * P:(k + 1) * P],
                                            x_nat[:, t, (4 * half + k) * P:(4 * half + k + 1) * P], ident)
                    last.then_inc(sem("h1_t_ready"), 1)

            for t in range(NT):
                if t >= 2:
                    pe.wait_ge(sem("residual"), t - 1)
                for half in range(2):
                    for k in range(KD):
                        last = pe.matmul(bank(2 * (t % 2) + half), lhsT=o_t[:, k, t * P:(t + 1) * P],
                                         rhs=wo_sb[:, k, half * 512:(half + 1) * 512], start=(k == 0), stop=(k == KD - 1))
                last.then_inc(sem("mixed"), 1)
                if t >= 1:
                    turn(t - 1)
            turn(NT - 1)

        @part("act")
        def _(act):
            act.wait_ge(sem("eps_set"), 1)
            for t in range(NT):
                act.wait_ge(sem("variance"), t + 1)
                act.activation(deviation, mean_var[:, 1:2], ACT.Sqrt, bias=eps).then_inc(sem("deviation"), 1)
                for half in range(2):
                    u = 2 * t + half
                    act.wait_ge(sem("h1_t_ready"), u + 1)
                    act.activation(h1_r[:, 0, 4 * half:4 * half + 4, t * P:(t + 1) * P],
                                   bank(4 + u % 4).rearrange("p (k n) -> p k n", k=4), ACT.Copy).then_inc(sem("h1_high"), 1)

        @part("dve")
        def _(dve):
            st = own_steps(dve, "dve")
            dve.memset(eps, EPS).then_inc(sem("eps_set"), 1)
            dve.wait_ge(sem("norms_in"), 2 * 16)

            def low(t):
                for half in range(2):
                    u = 2 * t + half
                    dve.wait_ge(sem("h1_high"), u + 1)
                    ks = slice(4 * half, 4 * half + 4)
                    dve.tensor_tensor(h1_r[:, 1, ks, t * P:(t + 1) * P], bank(4 + u % 4).rearrange("p (k n) -> p k n", k=4),
                                      h1_r[:, 0, ks, t * P:(t + 1) * P], ALU.subtract).then_inc(sem("h1_low"), 1)

            for t in range(NT):
                dve.wait_ge(sem("mixed"), t + 1)
                dve.scalar_tensor_tensor(x_nat[:, t, :], x_nat[:, t, :], ALPHA, bank(2 * (t % 2), 2), ALU.mult, ALU.add)\
                    .then_inc(sem("residual"), 1)
                dve.wait_ge(sem("residual"), t + 1)
                layer_norm(dve, st, x_nat[:, t, :], row_g, row_b, t + 1)
                if t >= 1:
                    low(t - 1)
            low(NT - 1)

        for engine in programs:
            programs[engine].append(end_stage)

        NC = 2 * PH
        NWQ = NC // 2
        place[0] = KEPT
        wq_sb = [take(KD * 2 * P).rearrange("p (k c) -> p k c", k=KD) for _ in range(2)]
        keys_n, keys_t = take(2 * P).rearrange("p (c d) -> p c d", c=2), take(2 * P).rearrange("p (c n) -> p c n", c=2)
        assert place[0] <= KEPT + 3 * PH * TK * TK
        s_copy = [take(NT * NK, S_COPY + e * NT * NK).rearrange("p (t n) -> p t n", t=NT) for e in range(2)]
        s_rest = take(NT * NK).rearrange("p (t n) -> p t n", t=NT)
        top = take(NT * NC * TK).rearrange("p (t c k) -> p t c k", t=NT, c=NC)
        top_i = take(NT * NC * TK).bitcast(U32).rearrange("p (t c k) -> p t c k", t=NT, c=NC)
        top_f = take(NT * NC * TK).rearrange("p (t h e k) -> p t h e k", t=NT, h=PH, e=2)
        assert place[0] == KEPT + PEER
        wq_era = ExitStack()
        wq_tensor = wq_era.enter_context(nc.sbuf_tensor("wq_parts", [P, WQ_R], F32R))
        wq_r = [wq_tensor[:, e * (WQ_R // 2):(e + 1) * (WQ_R // 2)].rearrange("p (s k c) -> p s k c", s=2, k=KD)
                for e in range(2)]
        pq = [o_t.rearrange("p c n -> p (c n)")[:, e * NP:(e + 1) * NP] for e in range(2)]
        wq_g = peer_wq.rearrange("(k p) (g c) -> g p k c", p=P, c=2 * P)

        def top16(dve, st, values, rest, out, index, n, chunk=None):
            for c in range(n):
                st.do(dve.max(out[:, c, 0:8], values[:, c, :]))
            for c in range(n):
                st.wait(n - 1)
                st.do(dve.max_index(index[:, c, 0:8], out[:, c, 0:8], values[:, c, :]))
            for c in range(n):
                st.wait(n - 1)
                st.do(dve.match_replace(rest[:, c, :], out[:, c, 0:8], values[:, c, :], LOWEST))
            for c in range(n):
                st.wait(n - 1)
                st.do(dve.max(out[:, c, 8:16], rest[:, c, :]))
            for c in range(n):
                st.wait(n - 1)
                ins = dve.max_index(index[:, c, 8:16], out[:, c, 8:16], rest[:, c, :])
                if c == n - 1 and chunk is not None:
                    ins.then_inc(sem("top_found"), 1)
                else:
                    st.do(ins)
            if chunk is not None:
                dve.wait_ge(sem("top_found"), chunk + 1)
            else:
                st.wait()

        @part("sp")
        def _(sp):
            for g in range(2, NWQ):
                sp.wait_ge(sem("w_low"), 2 * NG_IN + g - 1)
                sp.dma_start(wq_sb[g % 2], wq_g[g]).then_inc(sem(f"w_in_{g % 2}"), 16)

        @part("pe")
        def _(pe):
            pe.wait_ge(sem("small_in"), 2 * 16)
            for c in range(2):
                last = pe.transpose(bank(4)[:, c * P:(c + 1) * P], keys_n[:, c, :], ident)
            last.then_inc(sem("subkeys_turn"), 1)
            pe.wait_ge(sem("subkeys_turned"), 1)

            def score(c):
                pe.wait_ge(sem("pq_copied"), 2 * c + 2)
                if c >= 2:
                    pe.wait_ge(sem("s_copied"), c - 1)
                for t in range(NT):
                    last = pe.matmul(bank(4 + 2 * (c % 2), 2)[:, t * P:(t + 1) * P], lhsT=pq[c % 2][:, t * P:(t + 1) * P],
                                     rhs=keys_t[:, c % 2, :], start=True, stop=True)
                last.then_inc(sem("s_ready"), 1)

            for c in range(NC):
                pe.wait_ge(sem("w_low"), 2 * NG_IN + c // 2 + 1)
                w = wq_r[c // 2 % 2]
                for half in range(2):
                    u = 2 * c + half
                    if u >= 4:
                        pe.wait_ge(sem("pq_copied"), u - 3)
                    n = 0
                    for x, y in PARTS[::-1]:
                        for k in range(KD):
                            n += 1
                            last = pe.matmul(bank(u % 4)[:, 0:320], lhsT=w[:, x, k, c % 2 * P:(c % 2 + 1) * P],
                                             rhs=h1_r[:, y, k, half * 320:(half + 1) * 320],
                                             start=(n == 1), stop=(n == 3 * KD))
                    last.then_inc(sem("pq_ready"), 1)
                if c >= 1:
                    score(c - 1)
            score(NC - 1)

        @part("act")
        def _(act):
            def high(g):
                act.wait_ge(sem(f"w_in_{g % 2}"), 16 * (NG_IN + g // 2 + 1))
                if g >= 2:
                    act.wait_ge(sem("pq_ready"), 4 * (g - 1))
                act.activation(wq_r[g % 2][:, 0], wq_sb[g % 2], ACT.Copy).then_inc(sem("w_high"), 1)

            def scores_out(c):
                act.wait_ge(sem("s_ready"), c + 1)
                if c >= 2:
                    act.wait_ge(sem("top_found"), c - 1)
                act.activation(s_copy[c % 2], bank(4 + 2 * (c % 2), 2)[:, 0:NT * P].rearrange("p (t n) -> p t n", t=NT), ACT.Copy)\
                    .then_inc(sem("s_copied"), 1)

            high(0)
            high(1)
            for c in range(NC):
                for half in range(2):
                    u = 2 * c + half
                    act.wait_ge(sem("pq_ready"), u + 1)
                    if c >= 2:
                        act.wait_ge(sem("s_ready"), c - 1)
                    act.activation(pq[c % 2][:, half * 320:(half + 1) * 320], bank(u % 4)[:, 0:320], ACT.Copy)\
                        .then_inc(sem("pq_copied"), 1)
                if c % 2 == 1 and c // 2 + 2 < NWQ:
                    high(c // 2 + 2)
                if c >= 1:
                    scores_out(c - 1)
            scores_out(NC - 1)

        @part("dve")
        def _(dve):
            dve.wait_ge(sem("subkeys_turn"), 1)
            dve.tensor_copy(keys_t, bank(4)[:, 0:2 * P].rearrange("p (c n) -> p c n", c=2)).then_inc(sem("subkeys_turned"), 1)

            def low(g):
                dve.wait_ge(sem("w_high"), 2 * NG_IN + g + 1)
                dve.tensor_tensor(wq_r[g % 2][:, 1], wq_sb[g % 2], wq_r[g % 2][:, 0], ALU.subtract).then_inc(sem("w_low"), 1)

            st = own_steps(dve, "dve")
            low(0)
            low(1)
            for c in range(NC):
                if c % 2 == 1 and c // 2 + 2 < NWQ:
                    low(c // 2 + 2)
                dve.wait_ge(sem("s_copied"), c + 1)
                top16(dve, st, s_copy[c % 2], s_rest, top[:, :, c, :], top_i[:, :, c, :], NT, c)
            dve.tensor_copy(top_f.rearrange("p t h e k -> p (t h e k)"), top_i.rearrange("p t c k -> p (t c k)"))

        for engine in programs:
            programs[engine].append(end_stage)

        place[0] = KEPT - KD * NP
        best = take(PH * TK).rearrange("p (h k) -> p h k", h=PH)
        best_i = take(PH * TK).bitcast(U32).rearrange("p (h k) -> p h k", h=PH)
        digit_u = [take(PH * TK).bitcast(U32) for _ in range(2)]
        digit_f = [take(PH * TK) for _ in range(2)]
        ijg = take(3 * P).rearrange("p (x n) -> p x n", x=3)
        best_sum, best_inv = take(PH), take(PH)
        gate_e = take(PH * TK)
        assert place[0] <= KEPT
        cand = take(PH * TK * TK, KEPT).rearrange("p (h n) -> p h n", h=PH)
        equal = [take(PH * TK * TK) for _ in range(2)]
        assert place[0] == S_COPY
        ijg_t = take(3 * NP).rearrange("p (x n) -> p x n", x=3)

        def times_index(eng, t, e):
            x = equal[e].rearrange("p (h k a) -> p h k a", h=PH, k=TK)
            index = top_f[:, t, :, e, :].rearrange("p h (o a) -> p h o a", o=1).to_broadcast([P, PH, TK, TK])
            return eng.tensor_tensor(x, x, index, ALU.mult)

        def top_k(dve, st, t):
            grid = [PH, TK, TK]
            halves = top[:, t].rearrange("p (h e) k -> p h e k", e=2)
            st.link(dve.tensor_tensor(cand.rearrange("p h (a b) -> p h a b", a=TK),
                                      halves[:, :, 0, :].rearrange("p h (a o) -> p h a o", o=1).to_broadcast([P] + grid),
                                      halves[:, :, 1, :].rearrange("p h (o b) -> p h o b", o=1).to_broadcast([P] + grid),
                                      ALU.add))
            top16(dve, st, cand, cand, best, best_i, PH)
            dve.tensor_tensor(gate_e.rearrange("p (h k) -> p h k", h=PH), best,
                              best[:, :, 0:1].to_broadcast([P, PH, TK]), ALU.subtract).then_inc(sem("best_less"), 1)
            flat_i = best_i.rearrange("p h k -> p (h k)")
            st.do(dve.tensor_scalar(digit_u[0], flat_i, 4, None, ALU.logical_shift_right))
            st.link(dve.tensor_scalar(digit_u[1], flat_i, 15, None, ALU.bitwise_and))
            for e in range(2):
                st.do(dve.tensor_copy(digit_f[e], digit_u[e]))
            st.wait()
            if t >= 1:
                dve.wait_ge(sem("ijg_turned"), t)
            for e in range(2):
                ins = dve.tensor_tensor(equal[e].rearrange("p (n a) -> p n a", a=TK),
                                        digit_f[e].rearrange("p (n o) -> p n o", o=1).to_broadcast([P, PH * TK, TK]),
                                        iota[:, 0:TK].rearrange("p (o a) -> p o a", o=1).to_broadcast([P, PH * TK, TK]),
                                        ALU.is_equal)
                if e == 0:
                    ins.then_inc(sem("equal_ready"), 1)
                else:
                    st.link(ins)
            st.link(times_index(dve, t, 1))
            for e in (1, 0):
                if e == 0:
                    dve.wait_ge(sem("equal_times"), t + 1)
                st.do(dve.tensor_reduce(ijg[:, e, :], equal[e].rearrange("p (n a) -> p n a", a=TK), AX_X, ALU.add))
            dve.wait_ge(sem("gate_exp"), t + 1)
            st.link(dve.tensor_reduce(best_sum, gate_e.rearrange("p (h k) -> p h k", h=PH), AX_X, ALU.add))
            st.link(dve.reciprocal(best_inv, best_sum))
            dve.tensor_tensor(ijg[:, 2, :].rearrange("p (h k) -> p h k", h=PH), gate_e.rearrange("p (h k) -> p h k", h=PH),
                              best_inv.rearrange("p (h o) -> p h o", o=1).to_broadcast([P, PH, TK]), ALU.mult)\
                .then_inc(sem("ijg_ready"), 1)

        HALF_C = CHUNK // 2
        TILE_CHUNKS = P // CHUNK
        POOL_N = 13
        wq_era.close()
        place[0] = KEPT + PEER
        take_in(wq_era, "gate_table", 4 * NK * CHUNK)
        table = [take(NK * CHUNK).rearrange("p (i n) -> p i n", i=NK) for _ in range(2)]
        hot_j = [take(HALF_C * NK).rearrange("p (n j) -> p n j", n=HALF_C) for _ in range(2)]
        hot_i = [take(HALF_C * NK).rearrange("p (n i) -> p n i", n=HALF_C) for _ in range(2)]

        def over_chunks(eng, t, body):
            if t < NT - 1:
                with eng.Fori(0, TILE_CHUNKS // 2) as i:
                    for s in range(2):
                        body(TILE_CHUNKS * t + 2 * i + s, s, TILE_CHUNKS // 2 * t + i)
            else:
                body(NCHUNK - 1, 0, NCHUNK // 2)

        def columns(x, c, half, first=0, n=HALF_C):
            cols = ijg_t[:, x, bass.ds(c * CHUNK + half * HALF_C + first, n)]
            return cols.rearrange("p (n o) -> p n o", o=1).to_broadcast([P, n, NK])

        @part("sp")
        def _(sp):
            def store(c, s, i):
                sp.wait_ge(sem("table_copied"), 4 * c + 8)
                sp.dma_start(gates_dram[bass.ds(c, 1)].rearrange("o p n -> (o p) n"),
                             table[s].rearrange("p i n -> p (i n)")).then_inc(sem(f"table_out_{s}"), 16)

            for t in range(NT):
                over_chunks(sp, t, store)
            sp.wait_ge(sem("table_out_0"), 16 * (NCHUNK // 2 + 2))
            sp.wait_ge(sem("table_out_1"), 16 * (NCHUNK // 2 + 1))

        @part("pool")
        def _(pool):
            for t in range(NT + 1):
                if t < NT:
                    pool.wait_ge(sem("equal_ready"), t + 1)
                    times_index(pool, t, 0).then_inc(sem("equal_times"), 1)

                def scale(c, s, i, t=t):
                    for half in range(2):
                        pool.wait_ge(sem("hot_i_ready"), 2 * c + half + 1)
                        pool.wait_ge(sem("ijg_turned"), t)
                        x = hot_i[half][:, 0:POOL_N, :]
                        pool.tensor_tensor(x, x, columns(2, c, half, 0, POOL_N), ALU.mult)\
                            .then_inc(sem("hot_scaled"), 1)

                if t >= 1:
                    over_chunks(pool, t - 1, scale)

        @part("dve")
        def _(dve):
            st = own_steps(dve, "dve")
            iota_b = iota.rearrange("p (o j) -> p o j", o=1).to_broadcast([P, HALF_C, NK])

            def hot(c, s, i):
                for half in range(2):
                    dve.wait_ge(sem("table_ready"), 4 * c + 2 * half + 2)
                    dve.tensor_tensor(hot_i[half], iota_b, columns(0, c, half), ALU.is_equal).then_inc(sem("hot_i_ready"), 1)
                    dve.tensor_tensor(hot_j[half], iota_b, columns(1, c, half), ALU.is_equal).then_inc(sem("hot_ready"), 1)
                    dve.wait_ge(sem("hot_i_ready"), 2 * c + half + 1)
                    x = hot_i[half][:, POOL_N:HALF_C, :]
                    dve.tensor_tensor(x, x, columns(2, c, half, POOL_N, HALF_C - POOL_N), ALU.mult)\
                        .then_inc(sem("hot_ready"), 1)

            for t in range(NT + 1):
                if t < NT:
                    top_k(dve, st, t)
                if t >= 1:
                    dve.wait_ge(sem("ijg_turned"), t)
                    over_chunks(dve, t - 1, hot)

        @part("pe")
        def _(pe):
            pe.drain().then_inc(sem("table_ready"), 4)

            def turn(t):
                pe.wait_ge(sem("ijg_ready"), t + 1)
                if t >= 2:
                    pe.wait_ge(sem("table_copied"), 4 * (TILE_CHUNKS * (t - 1) + 1))
                for x in range(3):
                    last = pe.transpose(bank(0)[:, x * P:(x + 1) * P], ijg[:, x, :], ident)
                last.then_inc(sem("ijg_turn"), 1)

            def spread(c, s, i):
                for half in range(2):
                    pe.wait_ge(sem("hot_ready"), 4 * c + 2 * half + 2)
                    pe.wait_ge(sem("hot_scaled"), 2 * c + half + 1)
                    for n in range(HALF_C):
                        if n % 8 == 0:
                            pe.wait_ge(sem("table_copied"), 4 * c + 2 * half + n // 8 + 1)
                        last = pe.matmul(bank(4 * half + n // 4)[:, n % 4 * NK:(n % 4 + 1) * NK],
                                         lhsT=hot_j[half][:, n, :], rhs=hot_i[half][:, n, :], start=True, stop=True)
                        if n % 8 == 7:
                            last.then_inc(sem("table_ready"), 1)

            for t in range(NT + 1):
                if t < NT:
                    turn(t)
                if t >= 1:
                    pe.wait_ge(sem("ijg_turned"), min(t + 1, NT))
                    over_chunks(pe, t - 1, spread)

        @part("act")
        def _(act):
            act.drain().then_inc(sem("table_copied"), 4)
            act.drain().then_inc(sem("table_out_0"), 16)
            act.drain().then_inc(sem("table_out_1"), 16)

            def copy(c, s, i):
                act.wait_ge(sem(f"table_out_{s}"), 16 * i + 16)
                for q in range(4):
                    act.wait_ge(sem("table_ready"), 4 * c + q + 5)
                    act.activation(table[s][:, :, 8 * q:8 * q + 8].rearrange("p i n -> p n i"),
                                   bank(2 * q, 2).rearrange("p (n i) -> p n i", n=8), ACT.Copy).then_inc(sem("table_copied"), 1)

            for t in range(NT + 1):
                if t < NT:
                    act.wait_ge(sem("best_less"), t + 1)
                    act.activation(gate_e, gate_e, ACT.Exp).then_inc(sem("gate_exp"), 1)
                    act.wait_ge(sem("ijg_turn"), t + 1)
                    act.activation(ijg_t[:, :, t * P:(t + 1) * P], bank(0)[:, 0:3 * P].rearrange("p (x n) -> p x n", x=3), ACT.Copy)\
                        .then_inc(sem("ijg_turned"), 1)
                if t >= 1:
                    over_chunks(act, t - 1, copy)

        for engine in programs:
            programs[engine].append(end_stage)

        wq_era.close()
        era.close()
        f_t = kept[:, KEPT - KD * NP:KEPT - KD * NP + KD * N].rearrange("p (c n) -> p c n", c=KD)
        open_era("experts", ALL_COLUMNS - KEPT - H1_R - EXPERT_R)
        expert_r = era.enter_context(nc.sbuf_tensor("expert_parts", [P, EXPERT_R], F32R))
        ctx.callback(era.close)
        place_r = [0]

        def take_r(cols):
            place_r[0] += cols
            return expert_r[:, place_r[0] - cols:place_r[0]]

        u_sb = [take(D) for _ in range(GI)]
        v_sb = [take(D) for _ in range(GI)]
        gelu = [take(N) for _ in range(GI)]
        gates = take(NCHUNK * 2 * GI * CHUNK).rearrange("p (c i n) -> p c i n", c=NCHUNK, i=2 * GI)
        row_g2, row_b2 = take(D), take(D)
        u_t = [take_r(2 * D).rearrange("p (s k j) -> p s k j", s=2, k=KD) for _ in range(GI)]
        v_r = [[take_r(2 * D).rearrange("p (s d) -> p s d", s=2) for _ in range(GI)] for _ in range(2)]
        weight = [[take_r(2 * N).rearrange("p (s n) -> p s n", s=2) for _ in range(GI)] for _ in range(2)]
        gates_g = gates_dram.rearrange("c p (g n) -> p c g n", g=NG // 2)

        def over_groups(eng, body):
            body(0, 0, 0)
            with eng.Fori(0, NG // 2 - 1) as i:
                body(2 * i + 1, 1, i)
                body(2 * i + 2, 0, i + 1)
            body(NG - 1, 1, NG // 2 - 1)

        @part("sp")
        def _(sp):
            for to, frm in ((row_g2, ln2_g), (row_b2, ln2_b)):
                sp.dma_start(to, to_rows(frm)).then_inc(sem("norms_in"), 16)

            def load(g):
                for blk in range(GI):
                    x = GI * g + blk
                    sp.wait_ge(sem("u_turned"), x + 1)
                    sp.dma_start(u_sb[blk], peer_u[bass.ds(x * P, P), :]).then_inc(sem(f"u_in_{blk}"), 16)
                    sp.wait_ge(sem("v_low"), x + 1)
                    sp.dma_start(v_sb[blk], peer_v[bass.ds(x * P, P), :]).then_inc(sem(f"v_in_{blk}"), 16)

            with sp.Fori(0, NG // 2) as pair:
                load(2 * pair)
                sp.wait_ge(sem("gated"), 2 * GI * pair + 1)
                sp.dma_start(gates.rearrange("p c i n -> p c (i n)"),
                             gates_g[:, :, bass.ds(pair, 1), :].rearrange("p c o n -> p (c o) n")).then_inc(sem("gates_in"), 16)
                load(2 * pair + 1)

        @part("pool")
        def _(pool):
            for b in range(DB):
                pool.wait_ge(sem("y_ready"), 16 * (7 * b + 3))
                for to, frm in ((k_win_sample, state_k_win), (v_win_sample, state_v_win)):
                    pool.dma_start(to[b].rearrange("w h d -> (w h d)")[0:(WIN - DT) * DH],
                                   frm[b].rearrange("w h d -> (w h d)")[DT * DH:WIN * DH]).then_inc(sem("window_moved"), 16)

        @part("pe")
        def _(pe):
            pe.drain().then_inc(sem("u_turned"), 2)
            pe.drain().then_inc(sem("h_ready"), 4)
            pe.drain().then_inc(sem("y_ready"), 32)

            def turn(g, s, blk):
                x = GI * g + blk
                pe.wait_ge(sem(f"u_in_{blk}"), 16 * g + 16)
                pe.wait_ge(sem("u_low"), 2 * x + 4)
                for k in range(KD):
                    last = pe.transpose(bank(0, 2)[:, k * P:(k + 1) * P], u_sb[blk][:, k * P:(k + 1) * P], ident)
                last.then_inc(sem("u_turned"), 1)

            def hidden(g, s, blk):
                x = GI * g + blk
                pe.wait_ge(sem("u_low"), 2 * x + 6)
                for half in range(2):
                    pe.wait_ge(sem("gelu_done"), 2 * x + half + 1)
                    n = 0
                    for k in range(KD):
                        for a, b in PARTS:
                            n += 1
                            last = pe.matmul(bank(2 + half)[:, 0:HALF], lhsT=u_t[blk][:, a, k, :],
                                             rhs=h1_r[:, b, k, half * HALF:(half + 1) * HALF],
                                             start=(n == 1), stop=(n == 3 * KD))
                    last.then_inc(sem("h_ready"), 1)

            def add_up(g, s, dcs):
                pe.wait_ge(sem("v_low"), GI * g + GI + 2)
                pe.wait_ge(sem("weight_low"), GI * g + GI + 2)
                for dc in dcs:
                    for half in range(2):
                        pe.wait_ge(sem("y_added"), 16 * g + 2 * dc + half + 1)
                        n = 0
                        for blk in range(GI):
                            for a, b in PARTS:
                                n += 1
                                last = pe.matmul(bank(4 + (2 * dc + half) % 4)[:, 0:HALF], lhsT=v_r[s][blk][:, a, dc * P:(dc + 1) * P],
                                                 rhs=weight[s][blk][:, b, half * HALF:(half + 1) * HALF],
                                                 start=(n == 1), stop=(n == 3 * GI))
                        last.then_inc(sem("y_ready"), 1)

            turn(0, 0, 0)

            def group(g, s, pair):
                first, final = s == 0 and isinstance(g, int), s == 1 and isinstance(g, int)
                turn(g, s, 1)
                hidden(g, s, 0)
                if not first:
                    add_up(g - 1, 1 - s, range(0, KD // 2))
                if not final:
                    turn(g + 1, 1 - s, 0)
                hidden(g, s, 1)
                if not first:
                    add_up(g - 1, 1 - s, range(KD // 2, KD))

            over_groups(pe, group)
            add_up(NG - 1, 1, range(KD))

        @part("act")
        def _(act):
            act.drain().then_inc(sem("gelu_done"), 2)

            def u_high(g, s, blk):
                x = GI * g + blk
                act.wait_ge(sem("h_ready"), 2 * x + 2)
                for half in range(2):
                    act.wait_ge(sem("u_turned"), x + 3)
                    act.activation(u_t[blk][:, 0, 4 * half:4 * half + 4, :],
                                   bank(half).rearrange("p (k j) -> p k j", k=4), ACT.Copy)\
                        .then_inc(sem("u_high"), 1)

            def v_high(g, s, blk):
                act.wait_ge(sem("y_ready"), 16 * g + 16)
                act.wait_ge(sem(f"v_in_{blk}"), 16 * g + 16)
                act.activation(v_r[s][blk][:, 0, :], v_sb[blk], ACT.Copy).then_inc(sem("v_high"), 1)

            def activate(g, s, blk):
                x = GI * g + blk
                act.wait_ge(sem("weight_low"), x + 1)
                for half in range(2):
                    act.wait_ge(sem("h_ready"), 2 * x + half + 5)
                    act.activation(gelu[blk][:, half * HALF:(half + 1) * HALF], bank(2 + half)[:, 0:HALF], ACT.Gelu)\
                        .then_inc(sem("gelu_done"), 1)

            def weight_high(g, s, blk):
                act.wait_ge(sem("gated"), GI * g + blk + 2)
                act.activation(weight[s][blk][:, 0, :], gelu[blk], ACT.Copy).then_inc(sem("weight_high"), 1)

            u_high(0, 0, 0)

            def group(g, s, pair):
                final = s == 1 and isinstance(g, int)
                for blk in range(GI):
                    if blk == 0:
                        u_high(g, s, 1)
                    elif not final:
                        u_high(g + 1, 1 - s, 0)
                    v_high(g, s, blk)
                    activate(g, s, blk)
                    weight_high(g, s, blk)

            over_groups(act, group)

        @part("dve")
        def _(dve):
            dve.memset(f_t, 0.0).then_inc(sem("f_cleared"), 1)
            dve.wait_ge(sem("f_cleared"), 1)
            dve.drain().then_inc(sem("u_low"), 4)
            dve.drain().then_inc(sem("v_low"), 2)
            dve.drain().then_inc(sem("weight_low"), 2)
            dve.drain().then_inc(sem("gated"), 1)
            dve.drain().then_inc(sem("y_added"), 4)

            def u_low(g, s, blk):
                x = GI * g + blk
                for half in range(2):
                    dve.wait_ge(sem("u_high"), 2 * x + half + 1)
                    ks = slice(4 * half, 4 * half + 4)
                    dve.tensor_tensor(u_t[blk][:, 1, ks, :], bank(half).rearrange("p (k j) -> p k j", k=4),
                                      u_t[blk][:, 0, ks, :], ALU.subtract).then_inc(sem("u_low"), 1)

            def v_low(g, s, blk):
                dve.wait_ge(sem("v_high"), GI * g + blk + 1)
                dve.tensor_tensor(v_r[s][blk][:, 1, :], v_sb[blk], v_r[s][blk][:, 0, :], ALU.subtract).then_inc(sem("v_low"), 1)

            def gate(g, s, pair, blk):
                if blk == 0:
                    dve.wait_ge(sem("gates_in"), 16 * pair + 16)
                dve.wait_ge(sem("gelu_done"), 2 * (GI * g + blk) + 4)
                out = gelu[blk].rearrange("p (c n) -> p c n", c=NCHUNK)
                dve.tensor_tensor(out, out, gates[:, :, GI * s + blk, :], ALU.mult).then_inc(sem("gated"), 1)

            def weight_low(g, s, blk):
                dve.wait_ge(sem("weight_high"), GI * g + blk + 1)
                dve.tensor_tensor(weight[s][blk][:, 1, :], gelu[blk], weight[s][blk][:, 0, :], ALU.subtract)\
                    .then_inc(sem("weight_low"), 1)

            def add(g, ks):
                for k in ks:
                    to = f_t[:, k // 2, k % 2 * HALF:(k % 2 + 1) * HALF]
                    dve.wait_ge(sem("y_ready"), 16 * g + k + 33)
                    if k < 4:
                        dve.wait_ge(sem("y_added"), 16 * g + k + 2)
                    dve.tensor_tensor(to, to, bank(4 + k % 4)[:, 0:HALF], ALU.add).then_inc(sem("y_added"), 1)

            u_low(0, 0, 0)

            def group(g, s, pair):
                first, final = s == 0 and isinstance(g, int), s == 1 and isinstance(g, int)
                for blk in range(GI):
                    if blk == 0:
                        u_low(g, s, 1)
                    elif not final:
                        u_low(g + 1, 1 - s, 0)
                    v_low(g, s, blk)
                    gate(g, s, pair, blk)
                    if not first:
                        add(g - 1, range(KD * blk, KD * (blk + 1)))
                    weight_low(g, s, blk)

            over_groups(dve, group)
            add(NG - 1, range(2 * KD))

        for engine in programs:
            programs[engine].append(end_stage)

        y_rows = y_prompt.rearrange("b (t p) d -> t (b p) d", p=P)

        @part("pe")
        def _(pe):
            for t in range(NT):
                r = rows_of(t)
                if t >= 2:
                    pe.wait_ge(sem("residual"), NT + t - 1)
                for k in range(KD):
                    last = pe.transpose(bank(2 * (t % 2), 2)[0:r, k * P:(k + 1) * P], f_t[:, k, t * P:t * P + r], ident)
                last.then_inc(sem("f_turned"), 1)

        @part("act")
        def _(act):
            for t in range(NT):
                r = rows_of(t)
                act.wait_ge(sem("variance"), NT + t + 1)
                act.activation(deviation[0:r], mean_var[0:r, 1:2], ACT.Sqrt, bias=eps[0:r]).then_inc(sem("deviation"), 1)

        @part("dve")
        def _(dve):
            st = own_steps(dve, "dve")
            dve.wait_ge(sem("norms_in"), 4 * 16)
            for t in range(NT):
                r = rows_of(t)
                dve.wait_ge(sem("f_turned"), t + 1)
                dve.scalar_tensor_tensor(x_nat[0:r, t, :], x_nat[0:r, t, :], ALPHA, bank(2 * (t % 2), 2)[0:r],
                                         ALU.mult, ALU.add).then_inc(sem("residual"), 1)
                dve.wait_ge(sem("residual"), NT + t + 1)
                layer_norm(dve, st, x_nat[0:r, t, :], row_g2, row_b2, NT + t + 1, r)

        @part("sp")
        def _(sp):
            for t in range(NT):
                sp.wait_ge(sem("normed"), NT + t + 1)
                to = y_rows[t] if t < 4 else y_sample.rearrange("b t d -> (b t) d")
                sp.dma_start(to, x_nat[0:rows_of(t), t, :]).then_inc(sem("y_out"), 16)


        @part("sp")
        def _(sp):
            sp.wait_ge(sem("y_out"), NT * 16)
            sp.wait_ge(sem("window_moved"), 2 * DB * 16)
        block = ctx.enter_context(nc.Block())

        def run(parts, eng):
            for p in parts:
                p(eng)

        @block.sync
        def _(eng):
            run(programs["sp"], eng)

        @block.tensor
        def _(eng):
            run(programs["pe"], eng)

        @block.scalar
        def _(eng):
            run(programs["act"], eng)

        @block.vector
        def _(eng):
            run(programs["dve"], eng)

        @block.gpsimd
        def _(eng):
            run(programs["pool"], eng)


_INS = ["x_prompt", "x_sample", "cache_k_sb", "cache_v_sb", "page_table", "state_k_win", "state_v_win",
        "w_in", "w_out", "sb_logit_bias", "ln1_g", "ln1_b", "peer_wq", "peer_subkeys", "peer_u", "peer_v",
        "ln2_g", "ln2_b"]
_OUTS = [(1, SEQ, D), (DB, DT, D), (1, SEQ // P, P, H, HD), (1, SEQ // P, P, H, HD), (DB, DT, H, HD),
         (DB, DT, H, HD), (1, SEQ, H, HD), (1, SEQ, H, HD), (DB, WIN, H, HD), (DB, WIN, H, HD)]


def kernel(**inputs):
    import numpy as _np
    import concourse.bacc as _bacc
    from concourse.bass_utils import run_bass_kernel_spmd as _run

    nc = _bacc.Bacc("TRN2", target_bir_lowering=False, num_devices=1)
    given = {name: _np.ascontiguousarray(inputs[name]) for name in _INS}
    given.update(constants())
    arrays, args = {}, []
    for name, a in given.items():
        arrays[f"in_{name}_dram"] = a
        args.append(nc.dram_tensor(f"in_{name}_dram", a.shape, mybir.dt.from_np(a.dtype), kind="ExternalInput").ap())
    for i, shape in enumerate(_OUTS):
        args.append(nc.dram_tensor(f"out_{i}_dram", shape, F32, kind="ExternalOutput").ap())
    build(nc, *args)
    r = _run(nc, [arrays], core_ids=[0])
    return tuple(r.results[0][f"out_{i}_dram"] for i in range(len(_OUTS)))
```
